# Optimizing a Trainium2 kernel written in Bass

```python
import jax, jax.numpy as jnp
from jax import lax
import numpy as np
import math

D_MODEL = 1024
BATCH = 1
SEQ = 256
DEPTH = 1

CHUNK = 64
EPS = 1e-6
GLA_HEADS = 4
GLA_DK = 128
GLA_DV = 128
GLA_LOWRANK = 16
GLA_TAU = 16.0
GLA_QK = GLA_HEADS * GLA_DK
GLA_V = GLA_HEADS * GLA_DV
SGU_GROUPS = 4
SGU_GROUP_DIM = 128
SGU_BLOCK = 128
SGU_W = SGU_GROUPS * SGU_GROUP_DIM
PEER_HEADS = 8
PEER_DKEY = 256
PEER_NKEYS = 128
PEER_TOPK = 16
PEER_EXPERTS = PEER_NKEYS * PEER_NKEYS
PEER_TOKEN_BLOCK = 128
IN_COLS = (GLA_QK, GLA_QK, GLA_V, GLA_V, GLA_LOWRANK, SGU_W, SGU_W, D_MODEL, D_MODEL)
IN_WIDTH = sum(IN_COLS)


def rmsnorm(x, g):
    xf = x.astype(jnp.float32)
    y = xf * lax.rsqrt(jnp.mean(xf * xf, axis=-1, keepdims=True) + EPS)
    return (y * g.astype(jnp.float32)).astype(x.dtype)

def gla_branch(q, k, v, r, a_lr, w_a2, b_a, g_out):
    B, S, _ = q.shape
    NC = S // CHUNK
    f32 = jnp.float32
    qc = q.astype(f32).reshape(B, NC, CHUNK, GLA_HEADS, GLA_DK) * (GLA_DK ** -0.5)
    kc = k.astype(f32).reshape(B, NC, CHUNK, GLA_HEADS, GLA_DK)
    vc = v.astype(f32).reshape(B, NC, CHUNK, GLA_HEADS, GLA_DV)
    log_a = jax.nn.log_sigmoid((a_lr @ w_a2 + b_a).astype(f32)) / GLA_TAU
    log_a = log_a.reshape(B, NC, CHUNK, GLA_HEADS, GLA_DK)
    cum = jnp.cumsum(log_a, axis=2)
    total = cum[:, :, -1]
    k_dec = kc * jnp.exp(total[:, :, None] - cum)
    chunk_kv = jnp.einsum('bnchk,bnchv->bnhkv', k_dec, vc)
    decay = jnp.exp(total)

    def step(state, inp):
        dec, kv, qq = inp
        state = dec[..., None] * state + kv
        out = jnp.einsum('bchk,bhkv->bchv', qq, state)
        return state, out

    init = jnp.zeros((B, GLA_HEADS, GLA_DK, GLA_DV), f32)
    _, o = lax.scan(step, init, (jnp.moveaxis(decay, 1, 0), jnp.moveaxis(chunk_kv, 1, 0),
                                 jnp.moveaxis(qc, 1, 0)))
    o = jnp.moveaxis(o, 0, 1).reshape(B, S, GLA_HEADS, GLA_DV)
    o = o * lax.rsqrt(jnp.mean(o * o, axis=-1, keepdims=True) + EPS)
    o = o.reshape(B, S, GLA_V) * g_out.astype(f32)
    return (o * jax.nn.silu(r.astype(f32))).astype(q.dtype)

def sgu_branch(u, v, ln_g, ln_b, w_s, b_s):
    B, S, _ = v.shape
    f32 = jnp.float32
    vf = v.astype(f32)
    mu = jnp.mean(vf, axis=-1, keepdims=True)
    var = jnp.mean(jnp.square(vf - mu), axis=-1, keepdims=True)
    vn = (vf - mu) * lax.rsqrt(var + EPS) * ln_g.astype(f32) + ln_b.astype(f32)
    NB = S // SGU_BLOCK
    vn = vn.reshape(B, NB, SGU_BLOCK, SGU_GROUPS, SGU_GROUP_DIM)
    pos = jnp.arange(SGU_BLOCK) // CHUNK
    mask = pos[:, None] >= pos[None, :]
    w = jnp.where(mask[None], w_s.astype(f32), 0.0)
    mixed = jnp.einsum('gij,bnjgc->bnigc', w, vn) + b_s.astype(f32).T[None, None, :, :, None]
    return (u.astype(f32) * mixed.reshape(B, S, SGU_W)).astype(u.dtype)

def peer(x, w_q, sub_k1, sub_k2, expert_u, expert_v):
    B, S, D = x.shape
    T = B * S
    f32 = jnp.float32
    xt = x.reshape(T, D)
    q = (xt @ w_q).astype(f32).reshape(T, PEER_HEADS, 2, PEER_DKEY // 2)
    s1 = jnp.einsum('thd,kd->thk', q[:, :, 0], sub_k1.astype(f32))
    s2 = jnp.einsum('thd,kd->thk', q[:, :, 1], sub_k2.astype(f32))
    v1, i1 = lax.top_k(s1, PEER_TOPK)
    v2, i2 = lax.top_k(s2, PEER_TOPK)
    cand = (v1[..., :, None] + v2[..., None, :]).reshape(T, PEER_HEADS, PEER_TOPK * PEER_TOPK)
    vals, ci = lax.top_k(cand, PEER_TOPK)
    ia = ci // PEER_TOPK
    ib = ci % PEER_TOPK
    idx = jnp.take_along_axis(i1, ia, axis=-1) * PEER_NKEYS + jnp.take_along_axis(i2, ib, axis=-1)
    gates = jax.nn.softmax(vals, axis=-1)
    NBLK = T // PEER_TOKEN_BLOCK
    HK = PEER_HEADS * PEER_TOPK
    idx = idx.reshape(NBLK, PEER_TOKEN_BLOCK, HK)
    gates = gates.reshape(NBLK, PEER_TOKEN_BLOCK, HK)
    xb = xt.reshape(NBLK, PEER_TOKEN_BLOCK, D)

    def block(args):
        xx, ii, gg = args
        u = expert_u[ii]
        h = jnp.einsum('tkd,td->tk', u, xx).astype(f32)
        a = (jax.nn.gelu(h) * gg).astype(x.dtype)
        return jnp.einsum('tk,tkd->td', a, expert_v[ii])

    out = lax.map(block, (xb, idx, gates))
    return out.reshape(B, S, D)

def first_inputs(seed: int = 0) -> dict:
    key = jax.random.key(seed)
    ks = jax.random.split(key, 24)
    f32 = jnp.float32
    L, D = DEPTH, D_MODEL
    nrm = lambda k, shape, scale: jax.random.normal(k, shape, f32) * scale
    return {
        "x": jax.random.normal(ks[0], (BATCH, SEQ, D), f32),
        "norm1_g": 1.0 + nrm(ks[1], (L, D), 0.02),
        "w_in": nrm(ks[2], (L, D, IN_WIDTH), D ** -0.5),
        "w_gate_up": nrm(ks[3], (L, GLA_LOWRANK, GLA_QK), GLA_LOWRANK ** -0.5),
        "b_gate": 1.0 + nrm(ks[4], (L, GLA_QK), 0.1),
        "gla_norm_g": 1.0 + nrm(ks[5], (L, GLA_V), 0.02),
        "sgu_ln_g": 1.0 + nrm(ks[6], (L, SGU_W), 0.02),
        "sgu_ln_b": nrm(ks[7], (L, SGU_W), 0.02),
        "sgu_w": nrm(ks[8], (L, SGU_GROUPS, SGU_BLOCK, SGU_BLOCK), 0.5 * SGU_BLOCK ** -0.5),
        "sgu_b": 1.0 + nrm(ks[9], (L, SGU_GROUPS, SGU_BLOCK), 0.02),
        "w_branch_a": nrm(ks[10], (L, GLA_V, D), GLA_V ** -0.5),
        "w_branch_b": nrm(ks[11], (L, SGU_W, D), SGU_W ** -0.5),
        "w_out": nrm(ks[12], (L, D, D), D ** -0.5),
        "norm2_g": 1.0 + nrm(ks[13], (L, D), 0.02),
        "peer_wq": nrm(ks[14], (L, D, PEER_HEADS * PEER_DKEY), D ** -0.5),
        "peer_k1": nrm(ks[15], (L, PEER_NKEYS, PEER_DKEY // 2), (PEER_DKEY // 2) ** -0.5),
        "peer_k2": nrm(ks[16], (L, PEER_NKEYS, PEER_DKEY // 2), (PEER_DKEY // 2) ** -0.5),
        "peer_u": nrm(ks[17], (L, PEER_EXPERTS, D), D ** -0.5),
        "peer_v": nrm(ks[18], (L, PEER_EXPERTS, D), PEER_HEADS ** -0.5),
        "final_g": 1.0 + nrm(ks[19], (D,), 0.02),
    }

def first_block(x, norm1_g, w_in, w_gate_up, b_gate, gla_norm_g, sgu_ln_g, sgu_ln_b, sgu_w, sgu_b,
              w_branch_a, w_branch_b, w_out, norm2_g, peer_wq, peer_k1, peer_k2, peer_u, peer_v,
              final_g):
    offs = np.cumsum(IN_COLS)[:-1].tolist()
    h = x
    for l in range(DEPTH):
        n1 = rmsnorm(h, norm1_g[l])
        proj = n1 @ w_in[l]
        q, k, v, r, a_lr, su, sv, ga, gb = jnp.split(proj, offs, axis=-1)
        y_a = gla_branch(q, k, v, r, a_lr, w_gate_up[l], b_gate[l], gla_norm_g[l])
        su = jax.nn.gelu(su)
        sv = jax.nn.gelu(sv)
        y_b = sgu_branch(su, sv, sgu_ln_g[l], sgu_ln_b[l], sgu_w[l], sgu_b[l])
        merged = (jax.nn.sigmoid(ga) * (y_a @ w_branch_a[l])
                  + jax.nn.sigmoid(gb) * (y_b @ w_branch_b[l]))
        h = h + merged @ w_out[l]
        n2 = rmsnorm(h, norm2_g[l])
        h = h + peer(n2, peer_wq[l], peer_k1[l], peer_k2[l], peer_u[l], peer_v[l])
    return rmsnorm(h, final_g)


ATTN_HEADS = 8
ATTN_QK_DIM = 32
ATTN_V_DIM = 2 * ATTN_QK_DIM
ATTN_WIDTH = ATTN_HEADS * ATTN_V_DIM
Q_BLOCK = 128
SSM_HEADS = 16
SSM_HEAD_DIM = 64
SSM_WIDTH = SSM_HEADS * SSM_HEAD_DIM
SSM_GROUPS = 2
SSM_HEADS_PER_GROUP = SSM_HEADS // SSM_GROUPS
SSM_STATE = 128
CONV_WIDTH = 4
CHUNK_2 = 128
MIX_WIDTH = ATTN_WIDTH + SSM_WIDTH
D_FF = 2816
Q_COLS = ATTN_HEADS * 2 * ATTN_QK_DIM
K_COLS = ATTN_HEADS * 2 * ATTN_QK_DIM
V_COLS = ATTN_WIDTH
Z_COLS = SSM_WIDTH
XBC_COLS = SSM_WIDTH + 2 * SSM_GROUPS * SSM_STATE
DT_COLS = SSM_HEADS
IN_COLS_2 = Q_COLS + K_COLS + V_COLS + Z_COLS + XBC_COLS + DT_COLS
IN_SPLITS = (Q_COLS, Q_COLS + K_COLS, Q_COLS + K_COLS + V_COLS,
             Q_COLS + K_COLS + V_COLS + Z_COLS,
             Q_COLS + K_COLS + V_COLS + Z_COLS + XBC_COLS)


def rms_norm(x, g):
    xf = x.astype(jnp.float32)
    y = xf * lax.rsqrt(jnp.mean(xf * xf, axis=-1, keepdims=True) + EPS)
    return (y * g.astype(jnp.float32)).astype(x.dtype)

def swiglu(h, w_gate, w_up, w_down):
    return (jax.nn.silu(h @ w_gate) * (h @ w_up)) @ w_down

def alibi_slopes(n):
    return jnp.asarray(2.0 ** (-8.0 * np.arange(1, n + 1) / n), dtype=jnp.float32)

def diff_attention(q, k, v, lam, subln_g, lambda_init):
    b, s, _ = q.shape
    f32 = jnp.float32
    q = q.astype(f32).reshape(b, s, ATTN_HEADS, 2, ATTN_QK_DIM) * (ATTN_QK_DIM ** -0.5)
    k = k.astype(f32).reshape(b, s, ATTN_HEADS, 2, ATTN_QK_DIM)
    v = v.astype(f32).reshape(b, s, ATTN_HEADS, ATTN_V_DIM).transpose(0, 2, 1, 3)
    q1, q2 = q[..., 0, :].transpose(0, 2, 1, 3), q[..., 1, :].transpose(0, 2, 1, 3)
    k1, k2 = k[..., 0, :].transpose(0, 2, 1, 3), k[..., 1, :].transpose(0, 2, 1, 3)
    slopes = alibi_slopes(ATTN_HEADS)
    kpos = jnp.arange(s)
    nb = s // Q_BLOCK

    def to_blocks(t):
        return t.reshape(b, ATTN_HEADS, nb, Q_BLOCK, ATTN_QK_DIM).transpose(2, 0, 1, 3, 4)

    def block(args):
        q1b, q2b, start = args
        qpos = start + jnp.arange(Q_BLOCK)
        dist = qpos[:, None] - kpos[None, :]
        causal = dist >= 0
        bias = -slopes[:, None, None] * dist.astype(f32)

        def probs(qb, kk):
            sc = jnp.einsum('bhqd,bhkd->bhqk', qb, kk) + bias
            return jax.nn.softmax(jnp.where(causal, sc, -jnp.inf), axis=-1)

        a = probs(q1b, k1) - lam * probs(q2b, k2)
        return jnp.einsum('bhqk,bhkv->bhqv', a, v)

    starts = jnp.arange(nb) * Q_BLOCK
    o = lax.map(block, (to_blocks(q1), to_blocks(q2), starts))
    o = o.transpose(1, 0, 3, 2, 4).reshape(b, s, ATTN_HEADS, ATTN_V_DIM)
    o = rms_norm(o, subln_g) * (1.0 - lambda_init)
    return o.reshape(b, s, ATTN_WIDTH)

def causal_depthwise_conv(u, w, bias):
    c = u.shape[-1]
    out = lax.conv_general_dilated(u, w[:, None, :], window_strides=(1,),
                                   padding=[(CONV_WIDTH - 1, 0)],
                                   dimension_numbers=('NWC', 'WIO', 'NWC'),
                                   feature_group_count=c)
    return out + bias

def segsum(a):
    t = a.shape[-1]
    rep = jnp.broadcast_to(a[..., :, None], a.shape + (t,))
    rep = jnp.where(jnp.tril(jnp.ones((t, t), dtype=bool), -1), rep, 0.0)
    ss = jnp.cumsum(rep, axis=-2)
    return jnp.where(jnp.tril(jnp.ones((t, t), dtype=bool)), ss, -jnp.inf)

def ssd_chunked(x, a, bm, cm):
    b, s = x.shape[:2]
    c = s // CHUNK_2
    x = x.reshape(b, c, CHUNK_2, SSM_GROUPS, SSM_HEADS_PER_GROUP, SSM_HEAD_DIM)
    a = a.reshape(b, c, CHUNK_2, SSM_GROUPS, SSM_HEADS_PER_GROUP).transpose(0, 3, 4, 1, 2)
    bm = bm.reshape(b, c, CHUNK_2, SSM_GROUPS, SSM_STATE)
    cm = cm.reshape(b, c, CHUNK_2, SSM_GROUPS, SSM_STATE)
    a_cs = jnp.cumsum(a, axis=-1)
    decay = jnp.exp(segsum(a))
    cb = jnp.einsum('bclgn,bcsgn->bgcls', cm, bm)
    y_diag = jnp.einsum('bgjcls,bcsgjp->bclgjp', cb[:, :, None] * decay, x)
    decay_states = jnp.exp(a_cs[..., -1:] - a_cs)
    states = jnp.einsum('bclgn,bgjcl,bclgjp->bcgjpn', bm, decay_states, x)
    states = jnp.concatenate([jnp.zeros_like(states[:, :1]), states], axis=1)
    decay_chunk = jnp.exp(segsum(jnp.pad(a_cs[..., -1], ((0, 0), (0, 0), (0, 0), (1, 0)))))
    states = jnp.einsum('bgjzc,bcgjpn->bzgjpn', decay_chunk, states)[:, :-1]
    y_off = jnp.einsum('bclgn,bcgjpn,bgjcl->bclgjp', cm, states, jnp.exp(a_cs))
    return (y_diag + y_off).reshape(b, s, SSM_GROUPS, SSM_HEADS_PER_GROUP, SSM_HEAD_DIM)

def ssd_mixer(z, xbc, dt, conv_w, conv_b, dt_bias, a_log, d_skip, norm_g):
    b, s, _ = z.shape
    f32 = jnp.float32
    xbc = jax.nn.silu(causal_depthwise_conv(xbc, conv_w, conv_b))
    xs, bm, cm = jnp.split(xbc, [SSM_WIDTH, SSM_WIDTH + SSM_GROUPS * SSM_STATE], axis=-1)
    xs = xs.astype(f32).reshape(b, s, SSM_GROUPS, SSM_HEADS_PER_GROUP, SSM_HEAD_DIM)
    bm = bm.astype(f32).reshape(b, s, SSM_GROUPS, SSM_STATE)
    cm = cm.astype(f32).reshape(b, s, SSM_GROUPS, SSM_STATE)
    dt = jax.nn.softplus(dt.astype(f32) + dt_bias.astype(f32)).reshape(b, s, SSM_GROUPS, SSM_HEADS_PER_GROUP)
    a = -jnp.exp(a_log.astype(f32)).reshape(SSM_GROUPS, SSM_HEADS_PER_GROUP)
    y = ssd_chunked(xs * dt[..., None], a * dt, bm, cm)
    y = y + xs * d_skip.astype(f32).reshape(SSM_GROUPS, SSM_HEADS_PER_GROUP, 1)
    y = y.reshape(b, s, SSM_WIDTH) * jax.nn.silu(z.astype(f32))
    y = rms_norm(y.reshape(b, s, SSM_GROUPS, SSM_WIDTH // SSM_GROUPS),
                 norm_g.reshape(SSM_GROUPS, SSM_WIDTH // SSM_GROUPS))
    return y.reshape(b, s, SSM_WIDTH).astype(z.dtype)

def hybrid_layer(x, ffn1_pre_g, ffn1_w_gate, ffn1_w_up, ffn1_w_down, ffn1_post_g,
                 mix_pre_g, w_in, lambda_q1, lambda_k1, lambda_q2, lambda_k2, attn_subln_g,
                 conv_w, conv_b, dt_bias, a_log, d_skip, ssm_norm_g, w_out, mix_post_g,
                 ffn2_pre_g, ffn2_w_gate, ffn2_w_up, ffn2_w_down, ffn2_post_g, lambda_init):
    h = rms_norm(x, ffn1_pre_g)
    x = x + 0.5 * rms_norm(swiglu(h, ffn1_w_gate, ffn1_w_up, ffn1_w_down), ffn1_post_g)
    h = rms_norm(x, mix_pre_g)
    proj = h @ w_in
    q, k, v, z, xbc, dt = jnp.split(proj, IN_SPLITS, axis=-1)
    f32 = jnp.float32
    lam = (jnp.exp(jnp.sum(lambda_q1.astype(f32) * lambda_k1.astype(f32)))
           - jnp.exp(jnp.sum(lambda_q2.astype(f32) * lambda_k2.astype(f32))) + lambda_init)
    attn = diff_attention(q, k, v, lam, attn_subln_g, lambda_init).astype(x.dtype)
    ssm = ssd_mixer(z, xbc, dt, conv_w, conv_b, dt_bias, a_log, d_skip, ssm_norm_g)
    mixed = jnp.concatenate([attn, ssm], axis=-1) @ w_out
    x = x + rms_norm(mixed, mix_post_g)
    h = rms_norm(x, ffn2_pre_g)
    x = x + 0.5 * rms_norm(swiglu(h, ffn2_w_gate, ffn2_w_up, ffn2_w_down), ffn2_post_g)
    return x

def second_inputs(seed: int = 0) -> dict:
    key = jax.random.key(seed)
    ks = jax.random.split(key, 28)
    f32 = jnp.float32

    def normal(k, shape, scale):
        return jax.random.normal(k, shape, f32) * scale

    def gain(k, shape):
        return 1.0 + 0.05 * jax.random.normal(k, shape, f32)

    L = DEPTH
    u = jax.random.uniform(ks[15], (L, SSM_HEADS), f32)
    dt0 = jnp.exp(u * (math.log(0.1) - math.log(0.001)) + math.log(0.001))
    dt_bias = dt0 + jnp.log(-jnp.expm1(-dt0))
    return {
        'x': normal(ks[0], (BATCH, SEQ, D_MODEL), 1.0),
        'ffn1_pre_g': gain(ks[1], (L, D_MODEL)),
        'ffn1_w_gate': normal(ks[2], (L, D_MODEL, D_FF), D_MODEL ** -0.5),
        'ffn1_w_up': normal(ks[3], (L, D_MODEL, D_FF), D_MODEL ** -0.5),
        'ffn1_w_down': normal(ks[4], (L, D_FF, D_MODEL), D_FF ** -0.5),
        'ffn1_post_g': gain(ks[5], (L, D_MODEL)),
        'mix_pre_g': gain(ks[6], (L, D_MODEL)),
        'w_in': normal(ks[7], (L, D_MODEL, IN_COLS_2), D_MODEL ** -0.5),
        'lambda_q1': normal(ks[8], (L, ATTN_QK_DIM), 0.1),
        'lambda_k1': normal(ks[9], (L, ATTN_QK_DIM), 0.1),
        'lambda_q2': normal(ks[10], (L, ATTN_QK_DIM), 0.1),
        'lambda_k2': normal(ks[11], (L, ATTN_QK_DIM), 0.1),
        'attn_subln_g': gain(ks[12], (L, ATTN_V_DIM)),
        'conv_w': normal(ks[13], (L, CONV_WIDTH, XBC_COLS), CONV_WIDTH ** -0.5),
        'conv_b': normal(ks[14], (L, XBC_COLS), 0.02),
        'dt_bias': dt_bias,
        'a_log': jnp.log(jax.random.uniform(ks[16], (L, SSM_HEADS), f32, 1.0, 16.0)),
        'd_skip': 1.0 + 0.1 * jax.random.normal(ks[17], (L, SSM_HEADS), f32),
        'ssm_norm_g': gain(ks[18], (L, SSM_WIDTH)),
        'w_out': normal(ks[19], (L, MIX_WIDTH, D_MODEL), MIX_WIDTH ** -0.5),
        'mix_post_g': gain(ks[20], (L, D_MODEL)),
        'ffn2_pre_g': gain(ks[21], (L, D_MODEL)),
        'ffn2_w_gate': normal(ks[22], (L, D_MODEL, D_FF), D_MODEL ** -0.5),
        'ffn2_w_up': normal(ks[23], (L, D_MODEL, D_FF), D_MODEL ** -0.5),
        'ffn2_w_down': normal(ks[24], (L, D_FF, D_MODEL), D_FF ** -0.5),
        'ffn2_post_g': gain(ks[25], (L, D_MODEL)),
    }

def second_block(x, ffn1_pre_g, ffn1_w_gate, ffn1_w_up, ffn1_w_down, ffn1_post_g,
              mix_pre_g, w_in, lambda_q1, lambda_k1, lambda_q2, lambda_k2, attn_subln_g,
              conv_w, conv_b, dt_bias, a_log, d_skip, ssm_norm_g, w_out, mix_post_g,
              ffn2_pre_g, ffn2_w_gate, ffn2_w_up, ffn2_w_down, ffn2_post_g):
    for i in range(DEPTH):
        lambda_init = 0.8 - 0.6 * math.exp(-0.3 * i)
        x = hybrid_layer(x, ffn1_pre_g[i], ffn1_w_gate[i], ffn1_w_up[i], ffn1_w_down[i], ffn1_post_g[i],
                         mix_pre_g[i], w_in[i], lambda_q1[i], lambda_k1[i], lambda_q2[i], lambda_k2[i],
                         attn_subln_g[i], conv_w[i], conv_b[i], dt_bias[i], a_log[i], d_skip[i],
                         ssm_norm_g[i], w_out[i], mix_post_g[i],
                         ffn2_pre_g[i], ffn2_w_gate[i], ffn2_w_up[i], ffn2_w_down[i], ffn2_post_g[i],
                         lambda_init)
    return x


def setup_inputs(seed=0):
    out = dict(first_inputs(seed))
    for name, value in second_inputs(seed + 1).items():
        if name != "x":
            out[name + "_2"] = value
    return out


def reference(
    x, norm1_g, w_in, w_gate_up, b_gate, gla_norm_g, sgu_ln_g, sgu_ln_b, sgu_w, sgu_b,
    w_branch_a, w_branch_b, w_out, norm2_g, peer_wq, peer_k1, peer_k2, peer_u, peer_v, final_g,
    ffn1_pre_g_2, ffn1_w_gate_2, ffn1_w_up_2, ffn1_w_down_2, ffn1_post_g_2, mix_pre_g_2, w_in_2,
    lambda_q1_2, lambda_k1_2, lambda_q2_2, lambda_k2_2, attn_subln_g_2, conv_w_2, conv_b_2,
    dt_bias_2, a_log_2, d_skip_2, ssm_norm_g_2, w_out_2, mix_post_g_2, ffn2_pre_g_2,
    ffn2_w_gate_2, ffn2_w_up_2, ffn2_w_down_2, ffn2_post_g_2,
):
    x = first_block(
        x, norm1_g, w_in, w_gate_up, b_gate, gla_norm_g, sgu_ln_g, sgu_ln_b, sgu_w, sgu_b,
        w_branch_a, w_branch_b, w_out, norm2_g, peer_wq, peer_k1, peer_k2, peer_u, peer_v,
        final_g,
    )
    return second_block(
        x, ffn1_pre_g_2, ffn1_w_gate_2, ffn1_w_up_2, ffn1_w_down_2, ffn1_post_g_2, mix_pre_g_2,
        w_in_2, lambda_q1_2, lambda_k1_2, lambda_q2_2, lambda_k2_2, attn_subln_g_2, conv_w_2,
        conv_b_2, dt_bias_2, a_log_2, d_skip_2, ssm_norm_g_2, w_out_2, mix_post_g_2,
        ffn2_pre_g_2, ffn2_w_gate_2, ffn2_w_up_2, ffn2_w_down_2, ffn2_post_g_2,
    )


_drawn_inputs = setup_inputs


def setup_inputs(seed=0):
    import zlib

    import numpy as np

    out = dict(_drawn_inputs(seed))
    spreads = {}
    factors = {'gla_norm_g': 7.925,
     'sgu_ln_g': 11.824,
     'sgu_ln_b': 11.82,
     'sgu_b': 8.311,
     'lambda_q1_2': 8.0,
     'lambda_k1_2': 6.248,
     'lambda_k2_2': 45.925,
     'attn_subln_g_2': 3.068,
     'conv_b_2': 3.429,
     'ffn2_post_g_2': 3.571,
     'norm2_g': 2.829}
    for name, (base, spread) in spreads.items():
        noise = np.random.default_rng([zlib.crc32(name.encode()), seed]).standard_normal(out[name].shape)
        drawn = base * np.exp(spread * noise) if base else spread * noise
        out[name] = __import__('jax').numpy.asarray(drawn.astype(out[name].dtype))
    for name, factor in factors.items():
        out[name] = (out[name] * factor).astype(out[name].dtype)
    return out
```

```python
import math
from contextlib import ExitStack

import concourse.bass as bass
from concourse import mybir

P = 128
T, D = 256, 1024
NT, NK = T // P, D // P
RING = 3
SLOT = 4096
EPS = 1e-6
GLA_H, GLA_TAU, CH = 4, 16.0, 64
LOWR = 16
PEER_H, TOPK, NKEYS = 8, 16, 128
NEG = -3.0e38
FF = 2816
NF = FF // P
AT_H, AT_D, AT_V = 8, 32, 64
LAMBDA_INIT = 0.8 - 0.6 * math.exp(0.0)
SSM_H, SSM_G, SSM_P = 16, 2, 64
XC = 12
CONVW = 4

PANELS1 = ["q", "k", "v", "r", "su", "sv", "ga0", "ga1", "gb0", "gb1", "wa", "wb", "wo0", "wo1",
           "wq0", "wq1", "wq2", "wq3"]
PANELS2 = ["xbc0", "xbc1", "xbc2", "z0", "z1", "aq", "ak", "av", "wm0", "wm1", "wm2"]
N1, NE, N2 = len(PANELS1), P // 2, len(PANELS2)
EXP0 = N1
FFA0 = EXP0 + NE
MIX0 = FFA0 + NF
FFB0 = MIX0 + N2
ITEMS = FFB0 + NF

COLS = {}
_at = 0
for _name, _n in (("norm1", 8), ("norm2", 8), ("gla", 4), ("ffa", 8), ("mix", 8), ("ffb", 8), ("subln", 1),
                  ("ssm", 8), ("convw", XC * CONVW), ("convb", XC), ("sgub", 4)):
    COLS[_name] = (_at, _n)
    _at += _n
NCOLS = _at

MAIN = ([("alr", "dve"), ("q0", "dve"), ("q1", "dve"), ("z0", "dve"), ("z1", "dve"),
         ("k0", "dve"), ("k1", "dve"), ("v0", "dve"), ("v1", "dve"),
         ("d0", "act"), ("d1", "act"), ("tot", "act"),
         ("r0", "act"), ("r1", "act"), ("su0", "act"), ("su1", "act")]
        + [(f"kv{n}", "dve") for n in range(4)]
        + [("sv0", "act"), ("sv1", "act"), ("oe0", "dve"), ("oo0", "dve"), ("oe1", "dve"), ("oo1", "dve")]
        + [("ga00", "act"), ("ga01", "act"), ("ga10", "act"), ("ga11", "act"), ("mx0", "dve"), ("mx1", "dve")]
        + [("gb00", "act"), ("gb01", "act"), ("gb10", "act"), ("gb11", "act")]
        + [(f"pa{i}", "dve") for i in range(4)] + [(f"pb{i}", "dve") for i in range(4)]
        + [(f"ho{i}", "dve") for i in range(4)]
        + [(f"wq{i}", ("act", "dve")[i % 2]) for i in range(8)]
        + [(f"sc{i}", ("act", "dve")[i % 2]) for i in range(8)]
        + [(f"ex{i}", "dve") for i in range(4)]
        + [(f"fa{i}", "dve") for i in range(4)]
        + [("dt", "dve")] + [(f"xb{i}", ("act", "dve")[i % 2]) for i in range(6)]
        + [(f"zz{i}", "act") for i in range(4)]
        + [("aq0", "dve"), ("aq1", "dve"), ("ak0", "dve"), ("ak1", "dve"), ("av0", "act"), ("av1", "act")]
        + [(f"at{i}", "dve") for i in range(16)]
        + [("cum", "act"), ("cb", "dve")]
        + [(f"ss{i}", "act") for i in range(8)]
        + [(f"yd{i}", "dve") for i in range(4)]
        + [("st0", "act"), ("st1", "act"), ("yo0", "dve"), ("yo1", "dve")]
        + [("ao0", "dve"), ("ao1", "dve")]
        + [(f"wm{i}", "dve") for i in range(4)]
        + [(f"fb{i}", "dve") for i in range(4)])
MAIN_AT = {name: i for i, (name, _) in enumerate(MAIN)}
PANEL_END = ["q1", "k1", "v1", "r1", "su1", "sv1", "ga01", "ga11", "gb01", "gb11", "pa3", "pb3", "ho1", "ho3",
             "wq1", "wq3", "wq5", "wq7"]
MIX_END = ["xb1", "xb3", "xb5", "zz1", "zz3", "aq1", "ak1", "av1", None, None, "wm3"]
PANEL_END = ["q1", "k1", "v1", "r1", "su1", "sv1", "ga01", "ga11", "gb01", "gb11", "pa3", "pb3", "ho1", "ho3",
             "wq1", "wq3", "wq5", "wq7"]
MIX_END = ["xb1", "xb3", "xb5", "zz1", "zz3", "aq1", "ak1", "av1", None, None, "wm3"]
PANEL_END = ["q1", "k1", "v1", "r1", "su1", "sv1", "ga01", "ga11", "gb01", "gb11", "pa3", "pb3", "ho1", "ho3",
             "wq1", "wq3", "wq5", "wq7"]
MIX_END = ["xb1", "xb3", "xb5", "zz1", "zz3", "aq1", "ak1", "av1", None, None, "wm3"]
PANEL_END = ["q1", "k1", "v1", "r1", "su1", "sv1", "ga01", "ga11", "gb01", "gb11", "pa3", "pb3", "ho1", "ho3",
             "wq1", "wq3", "wq5", "wq7"]
MIX_END = ["xb1", "xb3", "xb5", "zz1", "zz3", "aq1", "ak1", "av1", None, None, "wm3"]
TSTAGES = [("n1", 4), ("ya", 2), ("yb", 2), ("mg", 4), ("n2", 4), ("idx", 2), ("ffa", 4), ("mix", 4),
           ("xs", 4), ("bm", 1), ("pt", 6), ("att", 2), ("ssm", 4), ("ffb", 4)]
T_AT, _n = {}, 0
for _name, _k in TSTAGES:
    T_AT[_name] = _n
    _n += _k


def reads_upto(i, who):
    return sum(1 for _, e in MAIN[:i + 1] if e == who)


def program(nc, x, panels1, experts, ffa, panels2, ffb, cols, w_low, w_gate_up, w_sgu, k12, w_dt,
            row_ln, row_post, row_small, row_lam, out):
    f32 = mybir.dt.float32
    u32 = mybir.dt.uint32
    ALU = mybir.AluOpType
    ACT = mybir.ActivationFunctionType
    AX = mybir.AxisListType.X
    ctx = ExitStack()
    with ctx:
        def sb(name, shape, dt=f32):
            return ctx.enter_context(nc.sbuf_tensor(name, shape, dt))

        def sem(name):
            return ctx.enter_context(nc.semaphore(name))

        ring = sb("ring", [P, RING, SLOT])
        arena = sb("arena", [P, P * T])
        X = sb("X", [P, NT, D])
        XT = sb("XT", [P, NK, T])
        work = sb("work", [P, 2048])
        i1T = sb("i1T", [P, T])
        i2T = sb("i2T", [P, T])
        gT = sb("gT", [P, T])
        ident = sb("ident", [P, P])
        iota = sb("iota", [P, P])
        C = sb("C", [P, NCOLS])
        nst = sb("nst", [P, 9, 10])
        hst = sb("hst", [P, 4, 2, 16])
        ps = ctx.enter_context(nc.psum_tensor("ps", [P, 8, 512], f32))

        def col(name, k=0):
            a, n = COLS[name]
            assert k < n
            return C[:, a + k:a + k + 1]

        class Cut:
            def __init__(self, at=0):
                self.at = at

            def __call__(self, *dims):
                n = math.prod(dims)
                v = arena[:, self.at:self.at + n]
                self.at += n
                assert self.at <= P * T, self.at
                if len(dims) == 2:
                    v = v.rearrange("p (a b) -> p a b", a=dims[0])
                if len(dims) == 3:
                    v = v.rearrange("p (a b c) -> p a b c", a=dims[0], b=dims[1])
                return v

        cut = Cut()
        XN = cut(NT, D)
        Kk, V, R, SU, SV = (cut(NT, 512) for _ in range(5))
        GA, GB = cut(NT, D), cut(NT, D)
        L, ZA, O, OSQ = (cut(NT, 512) for _ in range(4))
        ST = cut(4, GLA_H, P)
        QT = cut(4, T)
        LNG, LNB = cut(512), cut(512)
        WS = cut(4, P)
        YAT, YBT = cut(4, T), cut(4, T)
        MT = cut(NK, T)
        QP = cut(16, T)
        MDEC, WG, ALR = cut(P), cut(512), cut(T)
        C2 = cut(2)
        KS = cut(2, P)
        WL = cut(NK, LOWR)
        DEC = cut(16)
        BNS, MV = cut(NT, 6), cut(NT, 2)
        cut = Cut()
        SC = cut(NT, 16, P)
        CAND = cut(NT, PEER_H, 256)
        OH = cut(P, TOPK)
        VAL = cut(NT, 16, TOPK)
        IDF = cut(NT, 16, TOPK)
        BEST = cut(NT, P)
        GS = cut(NT, P)
        IA, IB = cut(NT, P), cut(NT, P)
        I1S, I2S = cut(NT, P), cut(NT, P)
        IDX = cut(NT, 16, TOPK).bitcast(u32)
        CI = cut(NT, P).bitcast(u32)
        CIA = cut(NT, P).bitcast(u32)
        PST = cut(NT, PEER_H)
        G = arena[:, :].rearrange("p (c t) -> p c t", c=P)
        cut = Cut()
        XN2 = cut(NT, D)
        XRAW = cut(XC, T + CONVW - 1)
        XBC = cut(XC, T)
        Z = cut(NT, D)
        AQ, AK = cut(4, T), cut(4, T)
        AV = cut(NT, 512)
        XS, XD = cut(NT, D), cut(NT, D)
        PR = cut(4, 4, 384)
        AOUT = cut(NT, 512)
        BM = cut(2, P)
        CB = cut(4, P)
        MLE, MGT = cut(P), cut(P)
        DB = cut(384)
        WD = cut(NK, SSM_H)
        DT, DU, AD = cut(NT, SSM_H), cut(NT, SSM_H), cut(NT, SSM_H)
        ECUM = cut(3, SSM_H)
        SMALL = cut(3, SSM_H)
        LAM = cut(4, AT_D)
        LS = cut(8)
        AMAX, ASUM = cut(16, 2), cut(16, 2)
        PG = cut(D)
        SSTATE = cut(2, 512)
        TA0 = cut(SSM_H, P)
        YOFF = cut(D)
        prf = PR.rearrange("p a b c -> p (a b c)")
        AT = Cut(2048)(24, P)
        TA = [TA0, work[:, :].rearrange("p (h s) -> p h s", h=SSM_H)]
        W = [XN2.rearrange("p a b -> p (a b)").rearrange("p (h s) -> p h s", h=SSM_H),
             prf[:, 0:2048].rearrange("p (h s) -> p h s", h=SSM_H)]
        XDS = prf[:, 2048:3072]
        ASQ = prf[:, 3072:4096].rearrange("p (t n) -> p t n", t=NT)
        SSQ = prf[:, 4096:6144].rearrange("p (t n) -> p t n", t=NT)
        MIXA = AQ
        MIXS = XBC[:, 0:8, :]
        HID = work[:, 0:512].rearrange("p (b t) -> p b t", b=2)
        HA = work[:, 512:1024].rearrange("p (b t) -> p b t", b=2)
        FG = work[:, 1024:2048]
        ONE1 = work[:, 0:1024].rearrange("p (b j c) -> p b j c", b=2, j=4)
        ONE2 = work[:, 1024:2048].rearrange("p (b j c) -> p b j c", b=2, j=4)

        slot_ready = [sem(f"slot_ready{s}") for s in range(RING)]
        x_in, consts_in, rows_in = sem("x_in"), sem("consts_in"), sem("rows_in")
        final_in, post_in, mix_in, out_done = sem("final_in"), sem("post_in"), sem("mix_in"), sem("out_done")
        pool_const, pool_const2 = sem("pool_const"), sem("pool_const2")
        dve_step, act_step = sem("dve_step"), sem("act_step")
        main_done = sem("main_done")
        main_read = {"act": sem("main_read_act"), "dve": sem("main_read_dve")}
        t_done = sem("t_done")
        t_read = [sem("t_read_dve"), sem("t_read_act")]
        norm_sq, norm_ms, norm_sd, norm_out = sem("norm_sq"), sem("norm_ms"), sem("norm_sd"), sem("norm_out")
        x_new = sem("x_new")
        gla_abs, gla_ln, gla_l, gla_e = sem("gla_abs"), sem("gla_ln"), sem("gla_l"), sem("gla_e")
        gla_kd, gla_state = sem("gla_kd"), sem("gla_state")
        head_ms, head_sd = sem("head_ms"), sem("head_sd")
        ya_ready, vn_ready, yb_ready, merged, masked = (sem("ya_ready"), sem("vn_ready"), sem("yb_ready"),
                                                        sem("merged"), sem("masked"))
        top_shift, top_exp, sel_ready = sem("top_shift"), sem("top_exp"), sem("sel_ready")
        one_ready, gate_mm, gate_out = sem("one_ready"), sem("gate_mm"), sem("gate_out")
        h_done, gelu_done, a_ready, a_used = sem("h_done"), sem("gelu_done"), sem("a_ready"), sem("a_used")
        gu_done, silu_done, fa_ready, fa_used = sem("gu_done"), sem("silu_done"), sem("fa_ready"), sem("fa_used")
        dt_abs, dt_ln, ad_ready = sem("dt_abs"), sem("dt_ln"), sem("ad_ready")
        conv_out, conv_silu = sem("conv_out"), sem("conv_silu")
        lam_sum, lam_exp = sem("lam_sum"), sem("lam_exp")
        att_max, att_exp, att_a, att_y = sem("att_max"), sem("att_exp"), sem("att_a"), sem("att_y")
        ta_ready, xd_ready, xskip_ready, xds_ready = (sem("ta_ready"), sem("xd_ready"), sem("xskip_ready"),
                                                      sem("xds_ready"))
        w_ready, ssm_y, wm_used = sem("w_ready"), sem("ssm_y"), sem("wm_used")

        def bank(name):
            return ps[:, MAIN_AT[name] % 4]

        def claim(pe, name):
            i = MAIN_AT[name] - 4
            if i >= 0:
                who = MAIN[i][1]
                pe.wait_ge(main_read[who], reads_upto(i, who))

        def read_out(eng, name):
            i = MAIN_AT[name]
            who = MAIN[i][1]
            eng.wait_ge(main_read[who], reads_upto(i, who))

        def arrived(eng, name):
            eng.wait_ge(main_done, MAIN_AT[name] + 1)
            return bank(name)

        def t_bank(stage, j):
            return ps[:, 6 + (T_AT[stage] + j) % 2]

        def t_claim(pe, stage, j):
            i = T_AT[stage] + j - 2
            if i >= 0:
                pe.wait_ge(t_read[i % 2], i // 2 + 1)

        def t_read_all(eng, stage, pairs):
            last = T_AT[stage] + pairs - 1
            for i in (last, last - 1):
                if i >= 0:
                    eng.wait_ge(t_read[i % 2], i // 2 + 1)

        def t_mine(who, stage, pairs):
            return [j for j in range(pairs) if (T_AT[stage] + j) % 2 == who]

        def slot(item):
            return ring[:, item % RING]

        def got(pe, item):
            pe.wait_ge(slot_ready[item % RING], 16 * (item // RING + 1))

        block = ctx.enter_context(nc.Block())

        @block.sync
        def _(sp):
            sp.dma_start(X[:, :, :], x.rearrange("a (n p) d -> p (a n) d", p=P)).then_inc(x_in, 16)

            def wait_used(item):
                if item < EXP0:
                    sp.wait_ge(main_done, MAIN_AT[PANEL_END[item]] + 1)
                elif item < FFA0:
                    m = item - EXP0
                    sp.wait_ge(main_done, MAIN_AT["ex3"] + 1) if m == NE - 1 else sp.wait_ge(a_used, 2 * m + 2)
                elif item < MIX0:
                    f = item - FFA0
                    sp.wait_ge(main_done, MAIN_AT["fa3"] + 1) if f == NF - 1 else sp.wait_ge(fa_used, f + 1)
                elif item < FFB0:
                    j = item - MIX0
                    if MIX_END[j]:
                        sp.wait_ge(main_done, MAIN_AT[MIX_END[j]] + 1)
                    else:
                        sp.wait_ge(wm_used, j - 7)
                else:
                    sp.wait_ge(fa_used, NF - 1 + item - FFB0 + 1)

            def load(item, src, n):
                if item >= RING:
                    wait_used(item - RING)
                sp.dma_start(slot(item)[:, 0:n], src).then_inc(slot_ready[item % RING], 16)

            for j in range(N1):
                load(j, panels1[j], SLOT)

            def stream(item0, count, src, n, used, used0, per_item):
                for j in range(RING):
                    load(item0 + j, src[j], n)
                turns = (count - RING) // RING
                with sp.Fori(0, turns, 1) as i:
                    for s in range(RING):
                        sp.wait_ge(used, i * (RING * per_item) + (used0 + (s + 1) * per_item))
                        sp.dma_start(slot(item0 + s)[:, 0:n], src[i * RING + (RING + s)])\
                          .then_inc(slot_ready[(item0 + s) % RING], 16)
                for j in range(RING * (turns + 1), count):
                    load(item0 + j, src[j], n)

            stream(EXP0, NE, experts, SLOT, a_used, 0, 2)
            stream(FFA0, NF, ffa, 3 * D, fa_used, 0, 1)
            for j in range(N2):
                load(MIX0 + j, panels2[j], SLOT)
            stream(FFB0, NF, ffb, 3 * D, fa_used, NF - 1, 1)
            sp.wait_ge(x_new, 6)
            sp.dma_start(out.rearrange("a (n p) d -> p (a n) d", p=P), X[:, :, :]).then_inc(out_done, 16)
            sp.wait_ge(out_done, 16)

        @block.gpsimd
        def _(pool):
            pool.iota(iota[:, :], pattern=[[1, P]], base=0, channel_multiplier=0,
                      allow_small_or_imprecise_dtypes=True).then_inc(pool_const, 1)
            pool.memset(ident[:, :], 0.0).then_inc(pool_const, 1)
            pool.memset(MDEC, 1.0).then_inc(pool_const, 1)
            pool.memset(C2, 1.0).then_inc(pool_const, 1)
            pool.memset(ALR[0:32, :], 1.0).then_inc(pool_const, 1)
            pool.wait_ge(pool_const, 5)
            pool.affine_select(out=ident[:, :], in_=ident[:, :], compare_op=ALU.not_equal, fill=1.0, base=0,
                               pattern=[[-1, P]], channel_multiplier=1).then_inc(pool_const, 1)
            pool.affine_select(out=MDEC, in_=MDEC, compare_op=ALU.is_gt, fill=0.0, base=0,
                               pattern=[[-1, P]], channel_multiplier=1).then_inc(pool_const, 1)
            pool.wait_ge(pool_const, 7)
            pool.affine_select(out=MDEC[:, 0:CH], in_=MDEC[:, 0:CH], compare_op=ALU.is_ge, fill=0.0, base=CH - 1,
                               pattern=[[0, CH]], channel_multiplier=-1).then_inc(pool_const, 1)
            pool.affine_select(out=C2[:, 0:1], in_=C2[:, 0:1], compare_op=ALU.is_ge, fill=0.0, base=CH - 1,
                               pattern=[[0, 1]], channel_multiplier=-1).then_inc(pool_const, 1)
            pool.affine_select(out=C2[:, 1:2], in_=C2[:, 1:2], compare_op=ALU.is_ge, fill=0.0, base=-CH,
                               pattern=[[0, 1]], channel_multiplier=1).then_inc(pool_const, 1)
            pool.wait_ge(rows_in, 16 * 3)
            for g in range(4):
                pool.affine_select(out=WS[:, g, 0:CH], in_=WS[:, g, 0:CH], compare_op=ALU.is_ge, fill=0.0,
                                   base=CH - 1, pattern=[[0, CH]], channel_multiplier=-1).then_inc(masked, 1)
            pool.wait_ge(x_new, 2)
            pool.memset(MLE, 1.0).then_inc(pool_const2, 1)
            pool.memset(MGT, 1.0).then_inc(pool_const2, 1)
            pool.memset(XRAW[:, :, 0:CONVW - 1], 0.0).then_inc(pool_const2, 1)
            pool.iota(DB[:, 0:P], pattern=[[1, P]], base=0, channel_multiplier=-1,
                      allow_small_or_imprecise_dtypes=True).then_inc(pool_const2, 1)
            pool.iota(DB[:, P:384], pattern=[[1, T]], base=-P, channel_multiplier=-1,
                      allow_small_or_imprecise_dtypes=True).then_inc(pool_const2, 1)
            pool.wait_ge(pool_const2, 5)
            pool.affine_select(out=MLE, in_=MLE, compare_op=ALU.is_ge, fill=0.0, base=0,
                               pattern=[[1, P]], channel_multiplier=-1).then_inc(pool_const2, 1)
            pool.affine_select(out=MGT, in_=MGT, compare_op=ALU.is_gt, fill=0.0, base=0,
                               pattern=[[-1, P]], channel_multiplier=1).then_inc(pool_const2, 1)
            pool.affine_select(out=DB[:, 0:P], in_=DB[:, 0:P], compare_op=ALU.is_ge, fill=-1e32, base=0,
                               pattern=[[-1, P]], channel_multiplier=1).then_inc(pool_const2, 1)
            pool.affine_select(out=DB[:, P:384], in_=DB[:, P:384], compare_op=ALU.is_ge, fill=-1e32, base=P,
                               pattern=[[-1, T]], channel_multiplier=1).then_inc(pool_const2, 1)
            pool.wait_ge(pool_const2, 9)
            pool.wait_ge(ad_ready, 1)
            for c in range(2):
                pool.tensor_tensor(TA[c], MGT.unsqueeze(1).broadcast_to([P, SSM_H, P]),
                                   AD[:, c, :].unsqueeze(2).broadcast_to([P, SSM_H, P]), ALU.mult)\
                    .then_inc(ta_ready, 1)
            t_read_all(pool, "xs", 4)
            for c in range(2):
                xs = XS[:, c, :].rearrange("p (h n) -> p h n", h=SSM_H)
                pool.tensor_tensor(XD[:, c, :].rearrange("p (h n) -> p h n", h=SSM_H), xs,
                                   DT[:, c, :].unsqueeze(2).broadcast_to([P, SSM_H, SSM_P]), ALU.mult)\
                    .then_inc(xd_ready, 1)
            pool.wait_ge(xd_ready, 2)
            for c in range(2):
                xs = XS[:, c, :].rearrange("p (h n) -> p h n", h=SSM_H)
                pool.tensor_tensor(xs, xs, SMALL[:, 2, :].unsqueeze(2).broadcast_to([P, SSM_H, SSM_P]), ALU.mult)\
                    .then_inc(xskip_ready, 1)
            read_out(pool, "cum")
            pool.wait_ge(t_done, T_AT["pt"] + 6)
            pool.tensor_tensor(XDS.rearrange("p (h n) -> p h n", h=SSM_H),
                               XD[:, 0, :].rearrange("p (h n) -> p h n", h=SSM_H),
                               ECUM[:, 2, :].unsqueeze(2).broadcast_to([P, SSM_H, SSM_P]), ALU.mult)\
                .then_inc(xds_ready, 1)

        @block.tensor
        def _(pe):
            def transposes(stage, srcs):
                for j in range((len(srcs) + 3) // 4):
                    t_claim(pe, stage, j)
                    for q, s in enumerate(srcs[4 * j:4 * j + 4]):
                        last = pe.transpose(t_bank(stage, j)[:, P * q:P * q + P], s, ident[:, :])
                    last.then_inc(t_done, 1)

            def tiles(src, n):
                return [src[:, tt, P * k:P * k + P] for k in range(n) for tt in range(NT)]

            def by_token(names, item, act_t, chunks=NK, halves=1):
                got(pe, item)
                w = slot(item).rearrange("p (k n) -> p k n", k=chunks)
                for n, name in enumerate(names):
                    tt, hf = n // halves, n % halves
                    claim(pe, name)
                    for k in range(chunks):
                        last = pe.matmul(bank(name), act_t[:, k, P * tt:P * tt + P],
                                         w[:, k, 512 * hf:512 * hf + 512], start=(k == 0), stop=(k == chunks - 1))
                    last.then_inc(main_done, 1)

            def by_feature(names, item, act_t):
                got(pe, item)
                w = slot(item).rearrange("p (k n) -> p k n", k=NK)
                for c in range(4):
                    if c % 2 == 0:
                        claim(pe, names[c // 2])
                    for k in range(NK):
                        last = pe.matmul(bank(names[c // 2])[:, T * (c % 2):T * (c % 2) + T],
                                         w[:, k, P * c:P * c + P], act_t[:, k, :], start=(k == 0),
                                         stop=(k == NK - 1))
                    if c % 2:
                        last.then_inc(main_done, 1)

            pe.wait_ge(pool_const, 6)
            pe.wait_ge(norm_out, 1)
            transposes("n1", tiles(XN, NK))
            t_read_all(pe, "n1", 4)
            pe.wait_ge(consts_in, 16 * 4)
            claim(pe, "alr")
            for k in range(NK):
                last = pe.matmul(bank("alr")[0:LOWR, 0:T], WL[:, k, :], XT[:, k, :], start=(k == 0),
                                 stop=(k == NK - 1))
            last.then_inc(main_done, 1)
            by_feature(["q0", "q1"], 0, XT)
            read_out(pe, "alr")
            for tt in range(NT):
                claim(pe, f"z{tt}")
                pe.matmul(bank(f"z{tt}"), ALR[0:LOWR + 1, P * tt:P * tt + P], WG[0:LOWR + 1, :], start=True,
                          stop=True).then_inc(main_done, 1)
            by_token(["k0", "k1"], 1, XT)
            by_token(["v0", "v1"], 2, XT)
            pe.wait_ge(gla_l, 1)
            pe.wait_ge(pool_const, 10)
            for tt in range(NT):
                claim(pe, f"d{tt}")
                pe.matmul(bank(f"d{tt}"), MDEC, L[:, tt, :], start=True, stop=True).then_inc(main_done, 1)
            claim(pe, "tot")
            for tt in range(NT):
                for h in range(GLA_H):
                    c = 2 * (GLA_H * tt + h)
                    last = pe.matmul(bank("tot")[:, c:c + 2], L[:, tt, P * h:P * h + P], C2, start=True, stop=True)
            last.then_inc(main_done, 1)
            by_token(["r0", "r1"], 3, XT)
            by_token(["su0", "su1"], 4, XT)
            pe.wait_ge(gla_kd, 1)
            for n in range(4):
                claim(pe, f"kv{n}")
                rows = slice(CH * (n % 2), CH * (n % 2) + CH)
                for h in range(GLA_H):
                    last = pe.matmul(bank(f"kv{n}")[:, P * h:P * h + P], Kk[rows, n // 2, P * h:P * h + P],
                                     V[rows, n // 2, P * h:P * h + P], start=True, stop=True)
                last.then_inc(main_done, 1)
            by_token(["sv0", "sv1"], 5, XT)
            pe.wait_ge(gla_state, 1)
            for tt in range(NT):
                for j, name in enumerate((f"oe{tt}", f"oo{tt}")):
                    claim(pe, name)
                    for h in range(GLA_H):
                        last = pe.matmul(bank(name)[:, P * h:P * h + P], QT[:, h, P * tt:P * tt + P],
                                         ST[:, 2 * tt + j, h, :],
                                         start=True, stop=True)
                    last.then_inc(main_done, 1)
            by_token(["ga00", "ga01"], 6, XT)
            by_token(["ga10", "ga11"], 7, XT)
            pe.wait_ge(vn_ready, 1)
            pe.wait_ge(masked, 4)
            for tt in range(NT):
                claim(pe, f"mx{tt}")
                for g in range(4):
                    last = pe.matmul(bank(f"mx{tt}")[:, P * g:P * g + P], WS[:, g, :], SV[:, tt, P * g:P * g + P],
                                     start=True, stop=True)
                last.then_inc(main_done, 1)
            by_token(["gb00", "gb01"], 8, XT)
            by_token(["gb10", "gb11"], 9, XT)
            pe.wait_ge(ya_ready, 1)
            transposes("ya", tiles(O, 4))
            pe.wait_ge(yb_ready, 1)
            transposes("yb", tiles(SU, 4))
            t_read_all(pe, "ya", 2)
            by_token([f"pa{i}" for i in range(4)], 10, YAT, chunks=4, halves=2)
            t_read_all(pe, "yb", 2)
            by_token([f"pb{i}" for i in range(4)], 11, YBT, chunks=4, halves=2)
            pe.wait_ge(merged, 1)
            transposes("mg", tiles(XN, NK))
            t_read_all(pe, "mg", 4)
            by_token(["ho0", "ho1"], 12, MT)
            by_token(["ho2", "ho3"], 13, MT)
            pe.wait_ge(norm_out, 2)
            transposes("n2", tiles(XN, NK))
            t_read_all(pe, "n2", 4)
            for j in range(4):
                by_feature([f"wq{2 * j}", f"wq{2 * j + 1}"], 14 + j, XT)
            read_out(pe, "wq6")
            read_out(pe, "wq7")
            for i in range(8):
                tt, q = i // 4, i % 4
                claim(pe, f"sc{i}")
                for j in range(4):
                    hp = 4 * q + j
                    last = pe.matmul(bank(f"sc{i}")[:, P * j:P * j + P], QP[:, hp, P * tt:P * tt + P],
                                     KS[:, hp % 2, :], start=True, stop=True)
                last.then_inc(main_done, 1)
            pe.wait_ge(sel_ready, 1)
            transposes("idx", [s[:, tt, :] for s in (I1S, I2S, GS) for tt in range(NT)])

            def gate_products(b):
                for j in range(4):
                    last = pe.matmul(ps[:, 4 + b, P * j:P * j + P], ONE1[:, b, j, :], ONE2[:, b, j, :], start=True,
                                     stop=True)
                last.then_inc(gate_mm, 1)

            for g in range(2):
                pe.wait_ge(one_ready, g + 1)
                gate_products(g)
            with pe.Fori(1, T // 8, 1) as pair:
                g = pair * 2
                for b in range(2):
                    pe.wait_ge(one_ready, g + (b + 1))
                    pe.wait_ge(gate_out, g + (b - 1))
                    gate_products(b)
            pe.wait_ge(gate_out, T // 4)

            def expert_h(b, item, half):
                w = slot(item)[:, 2048 * half:2048 * half + D].rearrange("p (k e) -> p k e", k=NK)
                for k in range(NK):
                    last = pe.matmul(ps[:, 4 + b, 0:T], w[:, k, :], XT[:, k, :], start=(k == 0), stop=(k == NK - 1))
                last.then_inc(h_done, 1)

            def expert_out(b, item, half, start=False, stop=False):
                w = slot(item)[:, 2048 * half + D:2048 * half + 2 * D]
                for tt in range(NT):
                    for hf in range(2):
                        last = pe.matmul(bank(f"ex{2 * tt + hf}"), HA[:, b, P * tt:P * tt + P],
                                         w[:, 512 * hf:512 * hf + 512], start=start, stop=stop)
                        if stop:
                            last.then_inc(main_done, 1)
                if not stop:
                    last.then_inc(a_used, 1)

            def expert_item(m, item, turn, start=False, end=False):
                if not start:
                    pe.wait_ge(gelu_done, m * 2)
                expert_h(1, item, 1)
                pe.wait_ge(a_ready, m * 2 + 1)
                expert_out(0, item, 0, start=start)
                if not end:
                    pe.wait_ge(slot_ready[(item + 1) % RING], turn)
                    pe.wait_ge(gelu_done, m * 2 + 1)
                    expert_h(0, item + 1, 0)
                pe.wait_ge(a_ready, m * 2 + 2)
                expert_out(1, item, 1, stop=end)

            for i in range(4):
                claim(pe, f"ex{i}")
            got(pe, EXP0)
            expert_h(0, EXP0, 0)
            expert_item(0, EXP0, 16 * ((EXP0 + 1) // RING + 1), start=True)
            turns = (NE - 2) // RING
            with pe.Fori(0, turns, 1) as i:
                for s in range(RING):
                    item = EXP0 + 1 + s
                    expert_item(i * RING + (1 + s), item, i * 16 + 16 * ((item + 1) // RING + 1))
            for m in range(1 + turns * RING, NE):
                expert_item(m, EXP0 + m, 16 * ((EXP0 + m + 1) // RING + 1), end=(m == NE - 1))

            def feed_forward(item0, base, outs):
                def gate_up(b, item):
                    w = slot(item)[:, 0:2 * D].rearrange("p (u k f) -> p u k f", u=2, k=NK)
                    for u in range(2):
                        for k in range(NK):
                            last = pe.matmul(ps[:, 4 + b, T * u:T * u + T], w[:, u, k, :], XT[:, k, :],
                                             start=(k == 0), stop=(k == NK - 1))
                    last.then_inc(gu_done, 1)

                def down(b, item, start=False, stop=False):
                    w = slot(item)[:, 2 * D:3 * D]
                    for tt in range(NT):
                        for hf in range(2):
                            last = pe.matmul(bank(outs[2 * tt + hf]), HA[:, b, P * tt:P * tt + P],
                                             w[:, 512 * hf:512 * hf + 512], start=start, stop=stop)
                            if stop:
                                last.then_inc(main_done, 1)
                    if not stop:
                        last.then_inc(fa_used, 1)

                def chunk(f, b, item, turn, start=False, end=False):
                    if not end:
                        pe.wait_ge(slot_ready[(item + 1) % RING], turn)
                        if not start:
                            pe.wait_ge(fa_ready, f + base)
                        gate_up(1 - b, item + 1)
                    pe.wait_ge(fa_ready, f + (base + 1))
                    down(b, item, start=start, stop=end)

                for name in outs:
                    claim(pe, name)
                got(pe, item0)
                if base:
                    pe.wait_ge(fa_ready, base)
                gate_up(0, item0)
                chunk(0, 0, item0, 16 * ((item0 + 1) // RING + 1), start=True)
                steps = 2 * RING
                turns = (NF - 2) // steps
                with pe.Fori(0, turns, 1) as i:
                    for s in range(steps):
                        item = item0 + 1 + s
                        chunk(i * steps + (1 + s), (1 + s) % 2, item, i * 32 + 16 * ((item + 1) // RING + 1))
                for f in range(1 + turns * steps, NF):
                    chunk(f, f % 2, item0 + f, 16 * ((item0 + f + 1) // RING + 1), end=(f == NF - 1))

            pe.wait_ge(norm_out, 3)
            transposes("ffa", tiles(XN2, NK))
            t_read_all(pe, "ffa", 4)
            feed_forward(FFA0, 0, [f"fa{i}" for i in range(4)])

            pe.wait_ge(norm_out, 4)
            transposes("mix", tiles(XN2, NK))
            t_read_all(pe, "mix", 4)
            pe.wait_ge(mix_in, 16 * 3)
            claim(pe, "dt")
            for tt in range(NT):
                for k in range(NK):
                    last = pe.matmul(bank("dt")[:, SSM_H * tt:SSM_H * tt + SSM_H], XT[:, k, P * tt:P * tt + P],
                                     WD[:, k, :], start=(k == 0), stop=(k == NK - 1))
            last.then_inc(main_done, 1)
            for j in range(3):
                by_feature([f"xb{2 * j}", f"xb{2 * j + 1}"], MIX0 + j, XT)
            for j in range(2):
                by_token([f"zz{2 * j}", f"zz{2 * j + 1}"], MIX0 + 3 + j, XT)
            by_feature(["aq0", "aq1"], MIX0 + 5, XT)
            by_feature(["ak0", "ak1"], MIX0 + 6, XT)
            by_token(["av0", "av1"], MIX0 + 7, XT)
            pe.wait_ge(conv_silu, 2)
            transposes("xs", [XBC[:, k, P * tt:P * tt + P] for k in range(8) for tt in range(NT)])
            transposes("bm", [XBC[:, 8 + g, 0:P] for g in range(2)])
            read_out(pe, "ak1")
            for i in range(16):
                r, g = i // 4, i % 4
                claim(pe, f"at{i}")
                rows = slice(AT_D * g, AT_D * g + AT_D)
                pe.matmul(bank(f"at{i}")[:, 0:P], AQ[rows, r, 0:P], AK[rows, r, 0:P], start=True, stop=True)
                pe.matmul(bank(f"at{i}")[:, P:384], AQ[rows, r, P:T], AK[rows, r, :], start=True,
                          stop=True).then_inc(main_done, 1)
            pe.wait_ge(ad_ready, 1)
            pe.wait_ge(pool_const2, 9)
            claim(pe, "cum")
            for n, (m, c) in enumerate(((MLE, 0), (MLE, 1), (MGT, 0))):
                last = pe.matmul(bank("cum")[:, SSM_H * n:SSM_H * n + SSM_H], m, AD[:, c, :], start=True, stop=True)
            last.then_inc(main_done, 1)
            claim(pe, "cb")
            for c in range(2):
                for g in range(2):
                    last = pe.matmul(bank("cb")[:, P * (2 * c + g):P * (2 * c + g) + P],
                                     XBC[:, 8 + g, P * c:P * c + P], XBC[:, 10 + g, P * c:P * c + P], start=True,
                                     stop=True)
            last.then_inc(main_done, 1)

            def between_tokens(c):
                pe.wait_ge(ta_ready, c + 1)
                for q in range(4):
                    claim(pe, f"ss{4 * c + q}")
                    for j in range(4):
                        last = pe.matmul(bank(f"ss{4 * c + q}")[:, P * j:P * j + P], TA[c][:, 4 * q + j, :], MLE,
                                         start=True, stop=True)
                    last.then_inc(main_done, 1)

            between_tokens(0)
            pe.wait_ge(att_a, 1)
            transposes("pt", [PR[:, h // 2, 2 * (h % 2), P * j:P * j + P] for h in range(AT_H) for j in range(3)])
            between_tokens(1)
            pe.wait_ge(xd_ready, 2)
            for c in range(2):
                pe.wait_ge(w_ready, 2 * c + 2)
                for g in range(2):
                    name = f"yd{2 * c + g}"
                    claim(pe, name)
                    for j in range(8):
                        h = 8 * g + j
                        last = pe.matmul(bank(name)[:, SSM_P * j:SSM_P * j + SSM_P], W[c][:, h, :],
                                         XD[:, c, SSM_P * h:SSM_P * h + SSM_P], start=True, stop=True)
                    last.then_inc(main_done, 1)
            pe.wait_ge(xds_ready, 1)
            t_read_all(pe, "bm", 1)
            for g in range(2):
                claim(pe, f"st{g}")
                pe.matmul(bank(f"st{g}"), BM[:, g, :], XDS[:, 512 * g:512 * g + 512], start=True,
                          stop=True).then_inc(main_done, 1)
            read_out(pe, "st1")
            for g in range(2):
                claim(pe, f"yo{g}")
                pe.matmul(bank(f"yo{g}"), XBC[:, 10 + g, P:T], SSTATE[:, g, :], start=True,
                          stop=True).then_inc(main_done, 1)
            t_read_all(pe, "pt", 6)
            read_out(pe, "av1")
            for tt in range(NT):
                claim(pe, f"ao{tt}")
                for h in range(AT_H):
                    for j in range(tt + 1):
                        last = pe.matmul(bank(f"ao{tt}")[:, AT_V * h:AT_V * h + AT_V], AT[:, 3 * h + tt + j, :],
                                         AV[:, j, AT_V * h:AT_V * h + AT_V], start=(j == 0), stop=(j == tt))
                last.then_inc(main_done, 1)
            pe.wait_ge(att_y, 1)
            transposes("att", tiles(AOUT, 4))
            pe.wait_ge(ssm_y, 1)
            transposes("ssm", tiles(XS, NK))
            t_read_all(pe, "att", 2)
            for p in range(3):
                item = MIX0 + 8 + p
                got(pe, item)
                if p == 1:
                    t_read_all(pe, "ssm", 4)
                w = slot(item).rearrange("p (k n) -> p k n", k=4)
                for tt in range(NT):
                    for hf in range(2):
                        name = f"wm{2 * tt + hf}"
                        if p == 0:
                            claim(pe, name)
                        for k in range(4):
                            a = MIXA[:, k] if p == 0 else MIXS[:, 4 * (p - 1) + k]
                            last = pe.matmul(bank(name), a[:, P * tt:P * tt + P], w[:, k, 512 * hf:512 * hf + 512],
                                             start=(p == 0 and k == 0), stop=(p == 2 and k == 3))
                        if p == 2:
                            last.then_inc(main_done, 1)
                if p < 2:
                    last.then_inc(wm_used, 1)
            pe.wait_ge(norm_out, 5)
            transposes("ffb", tiles(XN2, NK))
            t_read_all(pe, "ffb", 4)
            feed_forward(FFB0, NF, [f"fb{i}" for i in range(4)])

        @block.scalar
        def _(act):
            steps = [0]

            def link(ins):
                steps[0] += 1
                ins.then_inc(act_step, 1)
                act.wait_ge(act_step, steps[0])

            def read_done(ins):
                ins.then_inc(main_read["act"], 1)

            def norm_stats(i, parts):
                for n, part in enumerate(parts):
                    w = part.shape[-1]
                    last = act.activation(XN.rearrange("p t d -> p (t d)")[:, w * n:w * n + w], part, ACT.Square,
                                          accum_out=nst[:, i, n:n + 1])
                last.then_inc(norm_sq, 1)
                act.wait_ge(norm_ms, i + 1)
                act.activation(nst[:, i, 6:8], nst[:, i, 4:6], ACT.Sqrt).then_inc(norm_sd, 1)

            def head_root(i, n):
                act.wait_ge(head_ms, i + 1)
                act.activation(hst[:, i, 1, 0:n], hst[:, i, 0, 0:n], ACT.Sqrt).then_inc(head_sd, 1)

            def turned(stage, pairs, dst, gain=None):
                for j in t_mine(1, stage, pairs):
                    act.wait_ge(t_done, T_AT[stage] + j + 1)
                    for q in range(2):
                        k = 2 * j + q
                        last = act.activation(dst[:, k, :], t_bank(stage, j)[:, T * q:T * q + T], ACT.Copy,
                                              scale=1.0 if gain is None else gain(k))
                    last.then_inc(t_read[1], 1)

            act.dma_start(C[:, :], cols).then_inc(consts_in, 16)
            act.dma_start(WL, w_low).then_inc(consts_in, 16)
            act.dma_start(WG[0:LOWR + 1, :], w_gate_up).then_inc(consts_in, 16)
            act.dma_start(KS, k12).then_inc(consts_in, 16)
            act.dma_start(LNG, row_ln[0:1, :].broadcast_to([P, 512])).then_inc(rows_in, 16)
            act.dma_start(LNB, row_ln[1:2, :].broadcast_to([P, 512])).then_inc(rows_in, 16)
            act.dma_start(WS, w_sgu).then_inc(rows_in, 16)

            act.wait_ge(x_in, 16)
            norm_stats(0, [X[:, tt, :] for tt in range(NT)])
            act.wait_ge(consts_in, 16 * 4)
            turned("n1", 4, XT, lambda k: col("norm1", k))
            act.wait_ge(gla_abs, 1)
            link(act.activation(ZA, ZA, ACT.Exp, scale=-1.0))
            act.activation(ZA, ZA, ACT.Ln, bias=1.0).then_inc(gla_ln, 1)
            act.wait_ge(gla_l, 1)
            for tt in range(NT):
                b = arrived(act, f"d{tt}")
                read_done(act.activation(ZA[:, tt, :], b, ACT.Exp, scale=1.0 / GLA_TAU))
            b = arrived(act, "tot")
            read_done(act.activation(DEC, b[:, 0:16], ACT.Exp, scale=1.0 / GLA_TAU))
            for tt in range(NT):
                b = arrived(act, f"r{tt}")
                read_done(act.activation(R[:, tt, :], b, ACT.Silu))
            for name, dst in (("su", SU), ("sv", SV)):
                for tt in range(NT):
                    b = arrived(act, f"{name}{tt}")
                    read_done(act.activation(dst[:, tt, :], b, ACT.Gelu_apprx_tanh))
            head_root(0, NT)
            head_root(1, 8)
            for name, dst in (("ga", GA), ("gb", GB)):
                for hf in range(2):
                    for tt in range(NT):
                        b = arrived(act, f"{name}{hf}{tt}")
                        read_done(act.activation(dst[:, tt, 512 * hf:512 * hf + 512], b, ACT.Sigmoid))
            turned("ya", 2, YAT, lambda k: col("gla", k))
            turned("yb", 2, YBT)
            turned("mg", 4, MT)
            act.wait_ge(x_new, 1)
            norm_stats(1, [X[:, tt, :] for tt in range(NT)])
            turned("n2", 4, XT, lambda k: col("norm2", k))
            for i in range(0, 8, 2):
                b = arrived(act, f"wq{i}")
                read_done(act.activation(QP[:, 2 * i:2 * i + 2, :], b.rearrange("p (c t) -> p c t", c=2), ACT.Copy))
            for i in range(0, 8, 2):
                b = arrived(act, f"sc{i}")
                read_done(act.activation(SC[:, i // 4, 4 * (i % 4):4 * (i % 4) + 4, :],
                                         b.rearrange("p (j k) -> p j k", j=4), ACT.Copy))
            act.wait_ge(top_shift, 1)
            act.activation(GS, GS, ACT.Exp).then_inc(top_exp, 1)
            act.wait_ge(t_done, T_AT["idx"] + 2)
            act.activation(gT[:, :], t_bank("idx", 1)[:, 0:T], ACT.Copy).then_inc(t_read[1], 1)

            def gate_copy(g, b):
                src = ps[:, 4 + b, :].rearrange("p (j c) -> p c j", j=4)
                act.activation(G[:, :, bass.ds(g * 4, 4)], src, ACT.Copy).then_inc(gate_out, 1)

            with act.Fori(0, T // 8, 1) as pair:
                g = pair * 2
                for b in range(2):
                    act.wait_ge(gate_mm, g + (b + 1))
                    gate_copy(g + b, b)
            act.wait_ge(gate_mm, T // 4)
            act.dma_start(FG, row_post[0:1, :].broadcast_to([P, D])).then_inc(final_in, 16)

            def expert_gelu(b):
                act.activation(HID[:, b, :], ps[:, 4 + b, 0:T], ACT.Gelu_apprx_tanh).then_inc(gelu_done, 1)

            for b in range(2):
                act.wait_ge(h_done, b + 1)
                expert_gelu(b)
            with act.Fori(1, P // 2, 1) as pair:
                n = pair * 2
                for b in range(2):
                    act.wait_ge(h_done, n + (b + 1))
                    act.wait_ge(a_ready, n + (b - 1))
                    expert_gelu(b)
            act.wait_ge(x_new, 2)
            norm_stats(2, [X[:, tt, :] for tt in range(NT)])
            act.wait_ge(x_new, 3)
            norm_stats(3, [X[:, tt, :] for tt in range(NT)])
            act.dma_start(PG, row_post[1:2, :].broadcast_to([P, D])).then_inc(post_in, 16)
            act.dma_start(WD, w_dt).then_inc(mix_in, 16)
            act.dma_start(SMALL, row_small.rearrange("(o a) n -> o a n", o=1).broadcast_to([P, 3, SSM_H]))\
               .then_inc(mix_in, 16)
            act.dma_start(LAM, row_lam.rearrange("(o a) n -> o a n", o=1).broadcast_to([P, 4, AT_D]))\
               .then_inc(mix_in, 16)
            turned("ffa", 4, XT, lambda k: col("ffa", k))

            def feed_forward(base):
                def silu(b):
                    act.activation(HID[:, b, :], ps[:, 4 + b, 0:T], ACT.Silu).then_inc(silu_done, 1)

                for b in range(2):
                    act.wait_ge(gu_done, base + b + 1)
                    silu(b)
                with act.Fori(1, NF // 2, 1) as pair:
                    f = pair * 2
                    for b in range(2):
                        act.wait_ge(gu_done, f + (base + b + 1))
                        act.wait_ge(fa_ready, f + (base + b - 1))
                        silu(b)

            feed_forward(0)
            norm_stats(4, [arrived(act, f"fa{i}") for i in range(4)])
            act.wait_ge(x_new, 4)
            act.dma_start(PG, row_post[2:3, :].broadcast_to([P, D])).then_inc(post_in, 16)
            norm_stats(5, [X[:, tt, :] for tt in range(NT)])
            turned("mix", 4, XT, lambda k: col("mix", k))
            act.wait_ge(dt_abs, 1)
            link(act.activation(DU, DU, ACT.Exp, scale=-1.0))
            act.activation(DU, DU, ACT.Ln, bias=1.0)
            act.activation(SMALL[:, 1, :], SMALL[:, 1, :], ACT.Exp).then_inc(dt_ln, 1)
            act.wait_ge(lam_sum, 1)
            act.activation(LS[:, 2:4], LS[:, 0:2], ACT.Exp).then_inc(lam_exp, 1)
            act.wait_ge(pool_const2, 3)
            for i in range(0, 6, 2):
                b = arrived(act, f"xb{i}")
                read_done(act.activation(XRAW[:, 2 * i:2 * i + 2, CONVW - 1:], b.rearrange("p (c t) -> p c t", c=2),
                                         ACT.Copy))
            for j in range(2):
                for tt in range(NT):
                    b = arrived(act, f"zz{2 * j + tt}")
                    read_done(act.activation(Z[:, tt, 512 * j:512 * j + 512], b, ACT.Silu))
            act.wait_ge(conv_out, 1)
            act.activation(XBC[:, 0:8, :], XBC[:, 0:8, :], ACT.Silu).then_inc(conv_silu, 1)
            act.activation(XBC[:, 8:12, :], XBC[:, 8:12, :], ACT.Silu).then_inc(conv_silu, 1)
            for tt in range(NT):
                b = arrived(act, f"av{tt}")
                read_done(act.activation(AV[:, tt, :], b, ACT.Copy))

            def to_tokens(j):
                act.wait_ge(t_done, T_AT["xs"] + j + 1)
                b = t_bank("xs", j).rearrange("p (k t n) -> p t k n", k=2, t=NT)
                dst = XS[:, :, T * j:T * j + T].rearrange("p t (k n) -> p t k n", k=2)
                act.activation(dst, b, ACT.Copy).then_inc(t_read[1], 1)

            for j in t_mine(1, "xs", 4):
                to_tokens(j)
            for j in t_mine(1, "bm", 1):
                act.wait_ge(t_done, T_AT["bm"] + 1)
                act.activation(BM, t_bank("bm", 0)[:, 0:2 * P].rearrange("p (g n) -> p g n", g=2), ACT.Copy)\
                   .then_inc(t_read[1], 1)
            b = arrived(act, "cum")
            read_done(act.activation(ECUM, b[:, 0:3 * SSM_H].rearrange("p (a h) -> p a h", a=3), ACT.Exp))

            def decays(c):
                for q in range(4):
                    b = arrived(act, f"ss{4 * c + q}")
                    read_done(act.activation(W[c][:, 4 * q:4 * q + 4, :], b.rearrange("p (j l) -> p j l", j=4),
                                             ACT.Exp))

            decays(0)
            act.wait_ge(att_max, 1)
            for i in range(16):
                r, g = i // 4, i % 4
                for tt, seg in enumerate((slice(0, P), slice(P, 384))):
                    last = act.activation(PR[:, r, g, seg], PR[:, r, g, seg], ACT.Exp, bias=AMAX[:, i, tt:tt + 1],
                                          accum_out=ASUM[:, i, tt:tt + 1])
            last.then_inc(att_exp, 1)
            for j in t_mine(1, "pt", 6):
                act.wait_ge(t_done, T_AT["pt"] + j + 1)
                act.activation(AT[:, 4 * j:4 * j + 4, :], t_bank("pt", j).rearrange("p (a q) -> p a q", a=4),
                               ACT.Copy).then_inc(t_read[1], 1)
            decays(1)
            for g in range(2):
                b = arrived(act, f"st{g}")
                read_done(act.activation(SSTATE[:, g, :], b, ACT.Copy))
            head_root(2, 16)
            turned("att", 2, MIXA, lambda k: col("subln"))
            head_root(3, 4)
            turned("ssm", 4, MIXS, lambda k: col("ssm", k))
            norm_stats(6, [arrived(act, f"wm{i}") for i in range(4)])
            act.wait_ge(x_new, 5)
            act.dma_start(PG, row_post[3:4, :].broadcast_to([P, D])).then_inc(post_in, 16)
            norm_stats(7, [X[:, tt, :] for tt in range(NT)])
            turned("ffb", 4, XT, lambda k: col("ffb", k))
            feed_forward(NF)
            norm_stats(8, [arrived(act, f"fb{i}") for i in range(4)])

        @block.vector
        def _(dve):
            steps = [0]

            def link(ins):
                steps[0] += 1
                ins.then_inc(dve_step, 1)
                dve.wait_ge(dve_step, steps[0])

            def read_done(ins):
                ins.then_inc(main_read["dve"], 1)

            def norm_scale(i, parts, gain=1.0):
                dve.wait_ge(norm_sq, i + 1)
                if parts == 4:
                    s = nst[:, i, 0:4].rearrange("p (t h) -> p t h", t=2)
                    link(dve.tensor_tensor(nst[:, i, 4:6], s[:, :, 0], s[:, :, 1], ALU.add))
                    src = nst[:, i, 4:6]
                else:
                    src = nst[:, i, 0:2]
                dve.tensor_scalar(nst[:, i, 4:6], src, 1.0 / D, EPS, ALU.mult, ALU.add).then_inc(norm_ms, 1)
                dve.wait_ge(norm_sd, i + 1)
                link(dve.reciprocal(nst[:, i, 8:10], nst[:, i, 6:8]))
                if gain != 1.0:
                    link(dve.tensor_scalar(nst[:, i, 8:10], nst[:, i, 8:10], gain, None, ALU.mult))

            def pre_norm(i, dst):
                norm_scale(i, 2)
                for tt in range(NT):
                    last = dve.tensor_scalar(dst[:, tt, :], X[:, tt, :], nst[:, i, 8 + tt:9 + tt], None, ALU.mult)
                last.then_inc(norm_out, 1)

            def post_norm(i, names, gain, loads):
                norm_scale(i, 4, gain)
                dve.wait_ge(post_in, 16 * loads)
                for n, name in enumerate(names):
                    tt, hf = n // 2, n % 2
                    read_done(dve.scalar_tensor_tensor(XN2[:, tt, 512 * hf:512 * hf + 512], bank(name),
                                                       nst[:, i, 8 + tt:9 + tt], PG[:, 512 * hf:512 * hf + 512],
                                                       ALU.mult, ALU.mult))
                dve.wait_ge(main_read["dve"], reads_upto(MAIN_AT[names[-1]], "dve"))
                dve.tensor_tensor(X[:, :, :], X[:, :, :], XN2, ALU.add).then_inc(x_new, 1)

            def head_scale(i, n, width, gain=1.0):
                dve.tensor_scalar(hst[:, i, 0, 0:n], hst[:, i, 0, 0:n], 1.0 / width, EPS, ALU.mult, ALU.add)\
                   .then_inc(head_ms, 1)
                dve.wait_ge(head_sd, i + 1)
                link(dve.reciprocal(hst[:, i, 1, 0:n], hst[:, i, 1, 0:n]))
                if gain != 1.0:
                    link(dve.tensor_scalar(hst[:, i, 1, 0:n], hst[:, i, 1, 0:n], gain, None, ALU.mult))
                return hst[:, i, 1, 0:n]

            def turned(stage, pairs, dst, gain=None):
                for j in t_mine(0, stage, pairs):
                    dve.wait_ge(t_done, T_AT[stage] + j + 1)
                    for q in range(2):
                        k = 2 * j + q
                        src = t_bank(stage, j)[:, T * q:T * q + T]
                        if gain is None:
                            last = dve.tensor_copy(dst[:, k, :], src)
                        else:
                            last = dve.tensor_scalar(dst[:, k, :], src, gain(k), None, ALU.mult)
                    last.then_inc(t_read[0], 1)

            pre_norm(0, XN)
            dve.wait_ge(consts_in, 16 * 4)
            turned("n1", 4, XT, lambda k: col("norm1", k))
            dve.wait_ge(pool_const, 5)
            b = arrived(dve, "alr")
            read_done(dve.tensor_copy(ALR[0:LOWR, :], b[0:LOWR, 0:T]))
            for j in range(2):
                b = arrived(dve, f"q{j}")
                read_done(dve.tensor_scalar(QT[:, 2 * j:2 * j + 2, :], b.rearrange("p (c t) -> p c t", c=2),
                                            float(P) ** -0.5, None, ALU.mult))
            for tt in range(NT):
                b = arrived(dve, f"z{tt}")
                link(dve.tensor_scalar(L[:, tt, :], b, 0.0, None, ALU.min))
                read_done(dve.scalar_tensor_tensor(ZA[:, tt, :], L[:, tt, :], -2.0, b, ALU.mult, ALU.add))
            read_out(dve, "z1")
            dve.sem_inc(gla_abs, 1)
            for name, dst in (("k", Kk), ("v", V)):
                for tt in range(NT):
                    if name == "k" and tt == 0:
                        dve.wait_ge(gla_ln, 1)
                        dve.tensor_tensor(L, L, ZA, ALU.subtract).then_inc(gla_l, 1)
                    b = arrived(dve, f"{name}{tt}")
                    read_done(dve.tensor_copy(dst[:, tt, :], b))
            read_out(dve, "d1")
            read_out(dve, "k1")
            dve.tensor_tensor(Kk, Kk, ZA, ALU.mult).then_inc(gla_kd, 1)
            read_out(dve, "tot")
            for n in range(4):
                b = arrived(dve, f"kv{n}")
                if n == 0:
                    ins = dve.tensor_copy(ST[:, 0], b.rearrange("p (h v) -> p h v", h=GLA_H))
                else:
                    for h in range(GLA_H):
                        c = 2 * (GLA_H * (n // 2) + h) + n % 2
                        ins = dve.scalar_tensor_tensor(ST[:, n, h, :], ST[:, n - 1, h, :], DEC[:, c:c + 1],
                                                       b[:, P * h:P * h + P], ALU.mult, ALU.add)
                read_done(ins)
                read_out(dve, f"kv{n}")
            dve.sem_inc(gla_state, 1)
            dve.wait_ge(rows_in, 16 * 3)
            read_out(dve, "sv1")
            for tt in range(NT):
                ins = dve.bn_stats(BNS[:, tt, :], SV[:, tt, :])
            link(ins)
            for tt in range(NT):
                ins = dve.bn_aggr(MV[:, tt, :], BNS[:, tt, :])
            link(ins)
            link(dve.tensor_copy(hst[:, 0, 0, 0:NT], MV[:, :, 1]))
            rs = head_scale(0, NT, 1.0)
            for tt in range(NT):
                ins = dve.tensor_scalar(SV[:, tt, :], SV[:, tt, :], MV[:, tt, 0:1], rs[:, tt:tt + 1], ALU.subtract,
                                        ALU.mult)
            link(ins)
            link(dve.tensor_tensor(SV, SV, LNG.unsqueeze(1).broadcast_to([P, NT, 512]), ALU.mult))
            dve.tensor_tensor(SV, SV, LNB.unsqueeze(1).broadcast_to([P, NT, 512]), ALU.add).then_inc(vn_ready, 1)
            for tt in range(NT):
                for j, name in enumerate((f"oe{tt}", f"oo{tt}")):
                    b = arrived(dve, name)
                    rows = slice(CH * j, CH * j + CH)
                    read_done(dve.tensor_copy(O[rows, tt, :], b[rows, :]))
            read_out(dve, "oo1")
            link(dve.tensor_tensor(OSQ, O, O, ALU.mult))
            link(dve.tensor_reduce(hst[:, 1, 0, 0:8], OSQ.rearrange("p t (h v) -> p (t h) v", h=GLA_H), AX, ALU.add))
            rs = head_scale(1, 8, P)
            o8 = O.rearrange("p t (h v) -> p (t h) v", h=GLA_H)
            link(dve.tensor_tensor(o8, o8, rs.unsqueeze(2).broadcast_to([P, 8, P]), ALU.mult))
            dve.tensor_tensor(O, O, R, ALU.mult).then_inc(ya_ready, 1)
            for tt in range(NT):
                b = arrived(dve, f"mx{tt}")
                for g in range(4):
                    ins = dve.scalar_tensor_tensor(SU[:, tt, P * g:P * g + P], b[:, P * g:P * g + P],
                                                   col("sgub", g), SU[:, tt, P * g:P * g + P], ALU.add, ALU.mult)
                read_done(ins)
            read_out(dve, "mx1")
            dve.sem_inc(yb_ready, 1)
            turned("ya", 2, YAT, lambda k: col("gla", k))
            turned("yb", 2, YBT)
            for name, gate in (("pa", GA), ("pb", GB)):
                for i in range(4):
                    tt, hf = i // 2, i % 2
                    b = arrived(dve, f"{name}{i}")
                    g = gate[:, tt, 512 * hf:512 * hf + 512]
                    if i == 0:
                        read_out(dve, "ga11" if name == "pa" else "gb11")
                    read_done(dve.tensor_tensor(g, g, b, ALU.mult))
            read_out(dve, "pb3")
            dve.tensor_tensor(XN, GA, GB, ALU.add).then_inc(merged, 1)
            turned("mg", 4, MT)
            for i in range(4):
                hf, tt = i // 2, i % 2
                b = arrived(dve, f"ho{i}")
                xp = X[:, tt, 512 * hf:512 * hf + 512]
                read_done(dve.tensor_tensor(xp, xp, b, ALU.add))
            read_out(dve, "ho3")
            dve.sem_inc(x_new, 1)
            pre_norm(1, XN)
            turned("n2", 4, XT, lambda k: col("norm2", k))
            for i in range(1, 8, 2):
                b = arrived(dve, f"wq{i}")
                read_done(dve.tensor_copy(QP[:, 2 * i:2 * i + 2, :], b.rearrange("p (c t) -> p c t", c=2)))

            def top16(rows, values, indices):
                n = len(rows)
                for k in range(n):
                    ins = dve.max(values[k][:, 0:8], rows[k])
                link(ins)
                for k in range(n):
                    ins = dve.max_index(indices[k][:, 0:8], values[k][:, 0:8], rows[k])
                link(ins)
                for k in range(n):
                    ins = dve.match_replace(rows[k], values[k][:, 0:8], rows[k], NEG)
                link(ins)
                for k in range(n):
                    ins = dve.max(values[k][:, 8:16], rows[k])
                link(ins)
                for k in range(n):
                    ins = dve.max_index(indices[k][:, 8:16], values[k][:, 8:16], rows[k])
                link(ins)

            for i in range(8):
                tt, hp = i // 4, 4 * (i % 4)
                if i % 2:
                    b = arrived(dve, f"sc{i}")
                    read_done(dve.tensor_copy(SC[:, tt, hp:hp + 4, :], b.rearrange("p (j k) -> p j k", j=4)))
                read_out(dve, f"sc{i}")
                top16([SC[:, tt, hp + j, :] for j in range(4)], [VAL[:, tt, hp + j, :] for j in range(4)],
                      [IDX[:, tt, hp + j, :] for j in range(4)])
            link(dve.tensor_copy(IDF, IDX))
            for tt in range(NT):
                v = VAL[:, tt].rearrange("p (h s) k -> p h s k", s=2)
                four = [P, PEER_H, TOPK, TOPK]
                link(dve.tensor_tensor(CAND[:, tt].rearrange("p h (a b) -> p h a b", a=TOPK),
                                       v[:, :, 0, :].unsqueeze(3).broadcast_to(four),
                                       v[:, :, 1, :].unsqueeze(2).broadcast_to(four), ALU.add))
                for h in range(0, PEER_H, 4):
                    hs = range(h, h + 4)
                    top16([CAND[:, tt, k, :] for k in hs], [BEST[:, tt, TOPK * k:TOPK * k + TOPK] for k in hs],
                          [CI[:, tt, TOPK * k:TOPK * k + TOPK] for k in hs])
            best = BEST.rearrange("p t (h k) -> p (t h) k", h=PEER_H)
            gs = GS.rearrange("p t (h k) -> p (t h) k", h=PEER_H)
            dve.tensor_tensor(gs, best, best[:, :, 0:1].broadcast_to([P, NT * PEER_H, TOPK]), ALU.subtract)\
               .then_inc(top_shift, 1)
            dve.tensor_scalar(CIA, CI, 4, None, ALU.logical_shift_right)
            link(dve.tensor_scalar(CI, CI, 15, None, ALU.bitwise_and))
            dve.tensor_copy(IA, CIA)
            link(dve.tensor_copy(IB, CI))
            for tt in range(NT):
                for half, (rank, dst) in enumerate(((IA, I1S), (IB, I2S))):
                    three = [P, P, TOPK]
                    link(dve.tensor_tensor(OH, rank[:, tt, :].unsqueeze(2).broadcast_to(three),
                                           iota[:, 0:TOPK].unsqueeze(1).broadcast_to(three), ALU.is_equal))
                    oh = OH.rearrange("p (h k) j -> p h k j", h=PEER_H)
                    idf = IDF[:, tt].rearrange("p (h s) k -> p h s k", s=2)[:, :, half, :]
                    link(dve.tensor_tensor(oh, oh, idf.unsqueeze(2).broadcast_to(four), ALU.mult))
                    link(dve.tensor_reduce(dst[:, tt, :], OH, AX, ALU.add))
            dve.wait_ge(top_exp, 1)
            pst = PST.rearrange("p t h -> p (t h)")
            link(dve.tensor_reduce(pst, gs, AX, ALU.add))
            link(dve.reciprocal(pst, pst))
            dve.tensor_tensor(gs, gs, pst.unsqueeze(2).broadcast_to([P, NT * PEER_H, TOPK]), ALU.mult)\
               .then_inc(sel_ready, 1)
            dve.wait_ge(t_done, T_AT["idx"] + 1)
            dve.tensor_copy(i1T[:, :], t_bank("idx", 0)[:, 0:T])
            link(dve.tensor_copy(i2T[:, :], t_bank("idx", 0)[:, T:2 * T]))
            dve.sem_inc(t_read[0], 1)
            dve.wait_ge(t_read[1], (T_AT["idx"] + 1) // 2 + 1)

            def one_hots(g, b):
                for j in range(4):
                    t1 = bass.ds(g * 4 + j, 1)
                    dve.tensor_scalar(ONE1[:, b, j, :], iota[:, :], i1T[:, t1], None, ALU.is_equal)
                    ins = dve.tensor_scalar(ONE2[:, b, j, :], iota[:, :], i2T[:, t1], gT[:, t1], ALU.is_equal,
                                            ALU.mult)
                ins.then_inc(one_ready, 1)

            for g in range(2):
                one_hots(g, g)
            with dve.Fori(1, T // 8, 1) as pair:
                g = pair * 2
                for b in range(2):
                    dve.wait_ge(gate_mm, g + (b - 1))
                    one_hots(g + b, b)

            def expert_gate(n, b):
                dve.tensor_tensor(HA[:, b, :], HID[:, b, :], G[:, n, :], ALU.mult).then_inc(a_ready, 1)

            for b in range(2):
                dve.wait_ge(gelu_done, b + 1)
                expert_gate(b, b)
            with dve.Fori(1, P // 2, 1) as pair:
                n = pair * 2
                for b in range(2):
                    dve.wait_ge(gelu_done, n + (b + 1))
                    dve.wait_ge(a_used, n + (b - 1))
                    expert_gate(n + b, b)
            for i in range(4):
                tt, hf = i // 2, i % 2
                b = arrived(dve, f"ex{i}")
                xp = X[:, tt, 512 * hf:512 * hf + 512]
                read_done(dve.tensor_tensor(xp, xp, b, ALU.add))
            read_out(dve, "ex3")
            dve.sem_inc(x_new, 1)
            norm_scale(2, 2)
            dve.wait_ge(final_in, 16)
            for tt in range(NT):
                ins = dve.scalar_tensor_tensor(X[:, tt, :], X[:, tt, :], nst[:, 2, 8 + tt:9 + tt], FG, ALU.mult,
                                               ALU.mult)
            ins.then_inc(x_new, 1)
            dve.wait_ge(x_new, 3)

            def feed_forward(base):
                def times_up(b):
                    dve.tensor_tensor(HA[:, b, :], HID[:, b, :], ps[:, 4 + b, T:2 * T], ALU.mult)\
                       .then_inc(fa_ready, 1)

                used = NF - 1 if base else 0
                for b in range(2):
                    dve.wait_ge(silu_done, base + b + 1)
                    times_up(b)
                with dve.Fori(1, NF // 2, 1) as pair:
                    f = pair * 2
                    for b in range(2):
                        dve.wait_ge(silu_done, f + (base + b + 1))
                        dve.wait_ge(fa_used, f + (used + b - 1))
                        times_up(b)

            pre_norm(3, XN2)
            turned("ffa", 4, XT, lambda k: col("ffa", k))
            feed_forward(0)
            post_norm(4, [f"fa{i}" for i in range(4)], 0.5, 1)
            dve.wait_ge(x_new, 4)
            pre_norm(5, XN2)
            turned("mix", 4, XT, lambda k: col("mix", k))
            dve.wait_ge(mix_in, 16 * 3)
            b = arrived(dve, "dt")
            read_done(dve.tensor_tensor(DT, b[:, 0:2 * SSM_H].rearrange("p (t h) -> p t h", t=NT),
                                        SMALL[:, 0, :].unsqueeze(1).broadcast_to([P, NT, SSM_H]), ALU.add))
            read_out(dve, "dt")
            dve.scalar_tensor_tensor(DU, DT, -1.0, DT, ALU.mult, ALU.max).then_inc(dt_abs, 1)
            link(dve.tensor_scalar(DT, DT, 0.0, None, ALU.max))
            lam = LAM.rearrange("p (a b) n -> p a b n", a=2)
            link(dve.tensor_tensor(lam[:, :, 0, :], lam[:, :, 0, :], lam[:, :, 1, :], ALU.mult))
            dve.tensor_reduce(LS[:, 0:2], lam[:, :, 0, :], AX, ALU.add).then_inc(lam_sum, 1)
            dve.wait_ge(dt_ln, 1)
            link(dve.tensor_tensor(DT, DT, DU, ALU.add))
            ins = dve.scalar_tensor_tensor(AD, DT, -1.0, SMALL[:, 1, :].unsqueeze(1).broadcast_to([P, NT, SSM_H]),
                                           ALU.mult, ALU.mult)
            ins.then_inc(ad_ready, 1)
            dve.wait_ge(lam_exp, 1)
            link(dve.tensor_tensor(LS[:, 4:5], LS[:, 3:4], LS[:, 2:3], ALU.subtract))
            link(dve.tensor_scalar(LS[:, 5:6], LS[:, 4:5], -LAMBDA_INIT, None, ALU.add))
            dve.wait_ge(pool_const2, 3)
            for i in range(1, 6, 2):
                b = arrived(dve, f"xb{i}")
                read_done(dve.tensor_copy(XRAW[:, 2 * i:2 * i + 2, CONVW - 1:], b.rearrange("p (c t) -> p c t", c=2)))
            read_out(dve, "xb4")
            read_out(dve, "xb5")
            for c in range(XC):
                ins = dve.tensor_scalar(XBC[:, c, :], XRAW[:, c, 0:T], col("convw", CONVW * c), col("convb", c),
                                        ALU.mult, ALU.add)
            link(ins)
            for w in range(1, CONVW):
                for c in range(XC):
                    ins = dve.scalar_tensor_tensor(XBC[:, c, :], XRAW[:, c, w:w + T], col("convw", CONVW * c + w),
                                                   XBC[:, c, :], ALU.mult, ALU.add)
                if w < CONVW - 1:
                    link(ins)
            ins.then_inc(conv_out, 1)
            for name, dst, scale in (("aq", AQ, float(AT_D) ** -0.5), ("ak", AK, 1.0)):
                for j in range(2):
                    b = arrived(dve, f"{name}{j}")
                    read_done(dve.tensor_scalar(dst[:, 2 * j:2 * j + 2, :], b.rearrange("p (c t) -> p c t", c=2),
                                                scale, None, ALU.mult))
            for j in t_mine(0, "xs", 4):
                dve.wait_ge(t_done, T_AT["xs"] + j + 1)
                b = t_bank("xs", j).rearrange("p (k t n) -> p t k n", k=2, t=NT)
                dst = XS[:, :, T * j:T * j + T].rearrange("p t (k n) -> p t k n", k=2)
                dve.tensor_copy(dst, b).then_inc(t_read[0], 1)
            for j in t_mine(0, "bm", 1):
                dve.wait_ge(t_done, T_AT["bm"] + 1)
                dve.tensor_copy(BM, t_bank("bm", 0)[:, 0:2 * P].rearrange("p (g n) -> p g n", g=2))\
                   .then_inc(t_read[0], 1)
            dve.wait_ge(pool_const2, 9)
            for i in range(16):
                r, g = i // 4, i % 4
                h = 2 * r + g // 2
                b = arrived(dve, f"at{i}")
                read_done(dve.scalar_tensor_tensor(PR[:, r, g, :], DB, 2.0 ** (-8.0 * (h + 1) / AT_H), b[:, 0:384],
                                                   ALU.mult, ALU.add))
            b = arrived(dve, "cb")
            read_done(dve.tensor_tensor(CB, b.rearrange("p (a l) -> p a l", a=4),
                                        MLE.unsqueeze(1).broadcast_to([P, 4, P]), ALU.mult))
            read_out(dve, "cb")
            pr = PR.rearrange("p r g n -> p (r g) n")
            dve.tensor_reduce(AMAX[:, :, 0], pr[:, :, 0:P], AX, ALU.max, negate=True)
            dve.tensor_reduce(AMAX[:, :, 1], pr[:, :, P:384], AX, ALU.max, negate=True).then_inc(att_max, 1)

            def weights(c):
                read_out(dve, f"ss{4 * c + 3}")
                for g in range(2):
                    w = W[c][:, 8 * g:8 * g + 8, :]
                    dve.tensor_tensor(w, w, CB[:, 2 * c + g, :].unsqueeze(1).broadcast_to([P, 8, P]), ALU.mult)\
                       .then_inc(w_ready, 1)

            weights(0)
            dve.wait_ge(att_exp, 1)
            link(dve.reciprocal(ASUM, ASUM))
            second = ASUM.rearrange("p (h b) t -> p h b t", b=2)[:, :, 1, :]
            link(dve.tensor_scalar(second, second, LS[:, 5:6], None, ALU.mult))
            segs = (slice(0, P), slice(P, 384))
            for i in range(1, 16, 2):
                for tt, seg in enumerate(segs):
                    p2 = PR[:, i // 4, i % 4, seg]
                    ins = dve.tensor_scalar(p2, p2, ASUM[:, i, tt:tt + 1], None, ALU.mult)
            link(ins)
            for i in range(0, 16, 2):
                for tt, seg in enumerate(segs):
                    p1 = PR[:, i // 4, i % 4, seg]
                    ins = dve.scalar_tensor_tensor(p1, p1, ASUM[:, i, tt:tt + 1], PR[:, i // 4, i % 4 + 1, seg],
                                                   ALU.mult, ALU.add)
            ins.then_inc(att_a, 1)
            for j in t_mine(0, "pt", 6):
                dve.wait_ge(t_done, T_AT["pt"] + j + 1)
                dve.tensor_copy(AT[:, 4 * j:4 * j + 4, :], t_bank("pt", j).rearrange("p (a q) -> p a q", a=4))\
                   .then_inc(t_read[0], 1)
            weights(1)
            dve.wait_ge(xskip_ready, 2)
            for i in range(4):
                c, g = i // 2, i % 2
                b = arrived(dve, f"yd{i}")
                y = XS[:, c, 512 * g:512 * g + 512]
                read_done(dve.tensor_tensor(y, y, b, ALU.add))
            for g in range(2):
                b = arrived(dve, f"yo{g}")
                e = ECUM[:, 1, 8 * g:8 * g + 8].unsqueeze(2).broadcast_to([P, 8, SSM_P])
                read_done(dve.tensor_tensor(YOFF[:, 512 * g:512 * g + 512].rearrange("p (h n) -> p h n", h=8),
                                            b.rearrange("p (h n) -> p h n", h=8), e, ALU.mult))
            for tt in range(NT):
                b = arrived(dve, f"ao{tt}")
                read_done(dve.tensor_copy(AOUT[:, tt, :], b))
            read_out(dve, "ao1")
            link(dve.tensor_tensor(ASQ, AOUT, AOUT, ALU.mult))
            link(dve.tensor_reduce(hst[:, 2, 0, 0:16], ASQ.rearrange("p t (h v) -> p (t h) v", h=AT_H), AX, ALU.add))
            rs = head_scale(2, 16, AT_V, 1.0 - LAMBDA_INIT)
            a16 = AOUT.rearrange("p t (h v) -> p (t h) v", h=AT_H)
            dve.tensor_tensor(a16, a16, rs.unsqueeze(2).broadcast_to([P, 16, AT_V]), ALU.mult).then_inc(att_y, 1)
            turned("att", 2, MIXA, lambda k: col("subln"))
            link(dve.tensor_tensor(XS[:, 1, :], XS[:, 1, :], YOFF, ALU.add))
            link(dve.tensor_tensor(XS, XS, Z, ALU.mult))
            link(dve.tensor_tensor(SSQ, XS, XS, ALU.mult))
            link(dve.tensor_reduce(hst[:, 3, 0, 0:4], SSQ.rearrange("p t (g n) -> p (t g) n", g=2), AX, ALU.add))
            rs = head_scale(3, 4, 512)
            y4 = XS.rearrange("p t (g n) -> p (t g) n", g=2)
            dve.tensor_tensor(y4, y4, rs.unsqueeze(2).broadcast_to([P, 4, 512]), ALU.mult).then_inc(ssm_y, 1)
            turned("ssm", 4, MIXS, lambda k: col("ssm", k))
            post_norm(6, [f"wm{i}" for i in range(4)], 1.0, 2)
            dve.wait_ge(x_new, 5)
            pre_norm(7, XN2)
            turned("ffb", 4, XT, lambda k: col("ffb", k))
            feed_forward(NF)
            post_norm(8, [f"fb{i}" for i in range(4)], 0.5, 3)


def kernel(**inputs):
    import numpy as np
    import concourse.bacc as bacc
    from concourse.bass_utils import run_bass_kernel_spmd as run

    a = {k: np.asarray(v) for k, v in inputs.items()}

    def panel(w):
        return w.reshape(NK, P, -1).transpose(1, 0, 2).reshape(P, -1)

    def wide(w):
        return w.reshape(4, P, D).transpose(1, 0, 2).reshape(P, -1)

    def features(v, n):
        return v.reshape(n, P).T

    w_in = a["w_in"][0]
    at1 = {"q": 0, "k": 512, "v": 1024, "r": 1536, "su": 2064, "sv": 2576, "ga0": 3088, "ga1": 3600, "gb0": 4112,
           "gb1": 4624}
    p1 = [panel(w_in[:, c:c + 512]) for c in at1.values()]
    p1 += [wide(a["w_branch_a"][0]), wide(a["w_branch_b"][0])]
    p1 += [panel(a["w_out"][0][:, 512 * j:512 * j + 512]) for j in range(2)]
    p1 += [panel(a["peer_wq"][0][:, 512 * j:512 * j + 512]) for j in range(4)]
    u = a["peer_u"][0].reshape(P, P, NK, P).transpose(1, 3, 2, 0).reshape(P, P, D)
    v = a["peer_v"][0].reshape(P, P, D).transpose(1, 0, 2)
    experts = np.stack([u, v], axis=2).reshape(NE, 2, P, 2 * D).transpose(0, 2, 1, 3).reshape(NE, P, SLOT)

    def ffn(n):
        up = [a[f"ffn{n}_w_{w}_2"][0].reshape(NK, P, NF, P).transpose(2, 1, 0, 3).reshape(NF, P, D)
              for w in ("gate", "up")]
        return np.concatenate(up + [a[f"ffn{n}_w_down_2"][0].reshape(NF, P, D)], axis=2)

    w2 = a["w_in_2"][0]
    at2 = {"xbc0": 2560, "xbc1": 3072, "xbc2": 3584, "z0": 1536, "z1": 2048, "aq": 0, "ak": 512, "av": 1024}
    p2 = [panel(w2[:, c:c + 512]) for c in at2.values()]
    p2 += [wide(a["w_out_2"][0][512 * j:512 * j + 512]) for j in range(3)]
    cols = np.concatenate([
        features(a["norm1_g"][0], 8), features(a["norm2_g"][0], 8), features(a["gla_norm_g"][0], 4),
        features(a["ffn1_pre_g_2"][0], 8), features(a["mix_pre_g_2"][0], 8), features(a["ffn2_pre_g_2"][0], 8),
        np.tile(a["attn_subln_g_2"][0], 2)[:, None], features(a["ssm_norm_g_2"][0], 8),
        a["conv_w_2"][0].reshape(CONVW, XC, P).transpose(2, 1, 0).reshape(P, -1),
        features(a["conv_b_2"][0], XC), a["sgu_b"][0].T], axis=1)
    arrays = {
        "x": a["x"], "panels1": np.stack(p1), "experts": experts, "ffa": ffn(1), "panels2": np.stack(p2),
        "ffb": ffn(2), "cols": cols,
        "w_low": w_in[:, 2048:2064].reshape(NK, P, LOWR).transpose(1, 0, 2),
        "w_gate_up": np.concatenate([a["w_gate_up"][0], a["b_gate"]]),
        "w_sgu": a["sgu_w"][0].transpose(2, 0, 1),
        "k12": np.stack([a["peer_k1"][0].T, a["peer_k2"][0].T], axis=1),
        "w_dt": w2[:, 4096:4112].reshape(NK, P, SSM_H).transpose(1, 0, 2),
        "row_ln": np.concatenate([a["sgu_ln_g"], a["sgu_ln_b"]]),
        "row_post": np.stack([a["final_g"], a["ffn1_post_g_2"][0], a["mix_post_g_2"][0], a["ffn2_post_g_2"][0]]),
        "row_small": np.concatenate([a["dt_bias_2"], a["a_log_2"], a["d_skip_2"]]),
        "row_lam": np.concatenate([a[f"lambda_{n}_2"] for n in ("q1", "k1", "q2", "k2")]),
    }
    arrays = {f"in_{n}": np.ascontiguousarray(v) for n, v in arrays.items()}
    nc = bacc.Bacc("TRN2", target_bir_lowering=False, num_devices=1)
    args = [nc.dram_tensor(n, v.shape, mybir.dt.from_np(v.dtype), kind="ExternalInput").ap()
            for n, v in arrays.items()]
    out = nc.dram_tensor("out", (1, T, D), mybir.dt.float32, kind="ExternalOutput").ap()
    program(nc, *args, out)
    r = run(nc, [arrays], core_ids=[0])
    return r.results[0]["out"]
```

```python
import math
from contextlib import ExitStack

import concourse.bass as bass
from concourse import mybir

P = 128
T, D = 256, 1024
NT, NK = T // P, D // P
RING = 3
PART = 1024
ITEM = 2 * PART
NBUF = 3
EPS = 1e-6
GLA_H, GLA_TAU, CH = 4, 16.0, 64
LOWR = 16
PEER_H, TOPK, NKEYS = 8, 16, 128
NEG = -3.0e38
FF = 2816
NF = FF // P
AT_H, AT_D, AT_V = 8, 32, 64
LAMBDA_INIT = 0.8 - 0.6 * math.exp(0.0)
SSM_H, SSM_G, SSM_P = 16, 2, 64
XC = 12
CONVW = 4

PANELS1 = ["q", "k", "v", "r", "su", "sv", "ga0", "ga1", "gb0", "gb1", "wa", "wb", "wo0", "wo1",
           "wq0", "wq1", "wq2", "wq3"]
PANELS2 = ["xbc0", "xbc1", "xbc2", "z0", "z1", "aq", "ak", "av", "wm0", "wm1", "wm2"]
RAW1 = 2 * 10
WQ0 = RAW1 + 2 * 4
EXP0 = WQ0 + 2 * 4
FFA0 = EXP0 + P
FFI = 3 * NF // 2
MIX0 = FFA0 + FFI
RAW2 = MIX0 + 2 * 8
FFB0 = RAW2 + 2 * 3
ITEMS = FFB0 + FFI
S_WQ, S_EXP = 40, 56
S_FFA = S_EXP + 2 * P
S_MIX = S_FFA + 3 * NF
S_FFB = S_MIX + 32
S_END = S_FFB + 3 * NF

COLS = {}
_at = 0
for _name, _n in (("norm1", 8), ("norm2", 8), ("gla", 4), ("ffa", 8), ("mix", 8), ("ffb", 8), ("subln", 1),
                  ("ssm", 8), ("convw", XC * CONVW), ("convb", XC), ("sgub", 4)):
    COLS[_name] = (_at, _n)
    _at += _n
NCOLS = _at

PART_END = {}
MAIN, USE_PART = [], {}
_parts, _counted = 0, 0


def _part(main=None, other=None):
    global _parts, _counted
    if main is None and other is None:
        _counted += 1
        PART_END[_parts] = ("part_used", _counted)
    else:
        PART_END[_parts] = other or ("main", main)
    _parts += 1


def _use(*names_who):
    for name, who in names_who:
        USE_PART[name] = _parts - 1
        MAIN.append((name, who))


def _by_feature(a, b, wa, wb):
    _part(), _part(main=a), _use((a, wa)), _part(), _part(main=b), _use((b, wb))


def _by_token(a, b, who):
    _part(), _part(), _part(), _part(main=b), _use((a, who), (b, who))


_use(("alr", "dve"))
_by_feature("q0", "q1", "dve", "dve")
_use(("z0", "dve"), ("z1", "dve"))
_by_token("k0", "k1", "dve")
_by_token("v0", "v1", "dve")
_use(("d0", "act"), ("d1", "act"), ("tot", "act"))
_by_token("r0", "r1", "act")
_by_token("su0", "su1", "act")
_use(*[(f"kv{n}", "dve") for n in range(4)])
_by_token("sv0", "sv1", "act")
_use(*[(n, "dve") for n in ("oe0", "oo0", "oe1", "oo1")])
_by_token("ga00", "ga01", "act")
_by_token("ga10", "ga11", "act")
_use(("mx0", "dve"), ("mx1", "dve"))
_by_token("gb00", "gb01", "act")
_by_token("gb10", "gb11", "act")
_use(*[(f"pa{i}", "dve") for i in range(4)], *[(f"pb{i}", "dve") for i in range(4)],
     *[(f"ho{i}", "dve") for i in range(4)])
assert _parts == S_WQ
for _h in range(8):
    _part(), _part(main=f"wq{_h}"), _use((f"wq{_h}", "act"))
    if _h:
        _use((f"sc{_h - 1}", "act"))
_use(("sc7", "act"))
assert _parts == S_EXP
_part(other=("h_done", 1)), _part(other=("h_done", 2))
for _n in range(P - 2):
    _part(other=("h_done", _n + 3)), _part(other=("a_used", _n + 1))
_part(other=("a_used", P - 1)), _part(main="ex3")
_use(*[(f"ex{i}", "dve") for i in range(4)])


def _feed_forward(base, last):
    _part(), _part(other=("gu_done", base + 1))
    for f in range(NF - 1):
        _part(), _part(other=("gu_done", base + f + 2)), _part(other=("fa_used", (NF - 1) * (base > 0) + f + 1))
    _part(main=last + "3")
    _use(*[(f"{last}{i}", "dve") for i in range(4)])


assert _parts == S_FFA
FFA_COUNT = _counted
_feed_forward(0, "fa")
_use(("dt", "dve"))
for _j in range(3):
    _by_feature(f"xb{2 * _j}", f"xb{2 * _j + 1}", "act", "dve")
_by_token("zz0", "zz1", "act")
_by_token("zz2", "zz3", "act")
_by_feature("aq0", "aq1", "dve", "dve")
_by_feature("ak0", "ak1", "dve", "dve")
_by_token("av0", "av1", "act")
_use(*[(f"at{i}", "dve") for i in range(16)], ("cum", "act"), ("cb", "dve"), *[(f"ss{i}", "act") for i in range(8)],
     *[(f"yd{i}", "dve") for i in range(4)], ("st0", "act"), ("st1", "act"), ("yo0", "dve"), ("yo1", "dve"),
     ("ao0", "dve"), ("ao1", "dve"), *[(f"wm{i}", "dve") for i in range(4)])
assert _parts == S_FFB
FFB_COUNT = _counted
_feed_forward(NF, "fb")
assert _parts == S_END
MAIN_AT = {name: i for i, (name, _) in enumerate(MAIN)}
T_PART = {"n1": -1, "ya": S_WQ - 1, "yb": S_WQ - 1, "mg": S_WQ - 1, "n2": S_WQ, "idx": S_EXP - 1,
          "ffa": S_FFA - 1, "mix": S_MIX - 1, "xs": S_FFB - 1, "bm": S_FFB - 1, "pt": S_FFB - 1, "att": S_FFB - 1,
          "ssm": S_FFB - 1, "ffb": S_FFB}
TSTAGES = [("n1", 4), ("ya", 2), ("yb", 2), ("mg", 4), ("n2", 4), ("idx", 2), ("ffa", 4), ("mix", 4),
           ("xs", 4), ("bm", 1), ("pt", 6), ("att", 2), ("ssm", 4), ("ffb", 4)]
T_AT, _n = {}, 0
for _name, _k in TSTAGES:
    T_AT[_name] = _n
    _n += _k


def reads_upto(i, who):
    return sum(1 for _, e in MAIN[:i + 1] if e == who)


def program(nc, x, panels1, experts, ffa, panels2, ffb, cols, w_low, w_gate_up, w_sgu, k12, w_dt,
            row_ln, row_post, row_small, row_lam, out):
    f32 = mybir.dt.float32
    u32 = mybir.dt.uint32
    ALU = mybir.AluOpType
    ACT = mybir.ActivationFunctionType
    AX = mybir.AxisListType.X
    f32r = mybir.dt.float32r
    bf16 = mybir.dt.bfloat16
    ctx = ExitStack()
    with ctx:
        def sb(name, shape, dt=f32):
            return ctx.enter_context(nc.sbuf_tensor(name, shape, dt))

        def sem(name):
            return ctx.enter_context(nc.semaphore(name))

        raw = sb("raw", [P, RING, ITEM])
        whi = sb("whi", [P, NBUF, PART], f32r)
        wlo = sb("wlo", [P, NBUF, PART], bf16)
        arena = sb("arena", [P, P * T])
        X = sb("X", [P, NT, D])
        XTh, XTl = sb("XTh", [P, NK, T], f32r), sb("XTl", [P, NK, T], f32r)
        XTb = sb("XTb", [P, NK, T], bf16)
        HAh, HAl = sb("HAh", [P, 2, T], f32r), sb("HAl", [P, 2, T], f32r)
        HAb = sb("HAb", [P, 2, T], bf16)
        sel = sb("sel", [P, 3, T])
        i1T, i2T, gT = sel[:, 0], sel[:, 1], sel[:, 2]
        ident = sb("ident", [P, P])
        iota = sb("iota", [P, P])
        C = sb("C", [P, NCOLS])
        nst = sb("nst", [P, 2, 10])
        hst = sb("hst", [P, 2, 2, 16])
        ps = ctx.enter_context(nc.psum_tensor("ps", [P, 8, 512], f32))

        def col(name, k=0):
            a, n = COLS[name]
            assert k < n
            return C[:, a + k:a + k + 1]

        class Cut:
            def __init__(self, at=0):
                self.at = at

            def __call__(self, *dims):
                n = math.prod(dims)
                v = arena[:, self.at:self.at + n]
                self.at += n
                assert self.at <= P * T, self.at
                if len(dims) == 2:
                    v = v.rearrange("p (a b) -> p a b", a=dims[0])
                if len(dims) == 3:
                    v = v.rearrange("p (a b c) -> p a b c", a=dims[0], b=dims[1])
                return v

        cut = Cut()
        XN = cut(NT, D)
        Kk, V, R, SU, SV = (cut(NT, 512) for _ in range(5))
        GA, GB = cut(NT, D), cut(NT, D)
        L, ZA, O, OSQ = (cut(NT, 512) for _ in range(4))
        ST = cut(4, GLA_H, P)
        QT = cut(4, T)
        LNG, LNB = cut(512), cut(512)
        WS = cut(4, P)
        YAT, YBT = cut(4, T), cut(4, T)
        MT = cut(NK, T)
        QP = cut(16, T)
        MDEC, WG, ALR = cut(P), cut(512), cut(T)
        C2 = cut(2)
        KS = cut(2, P)
        WL = cut(NK, LOWR)
        DEC = cut(16)
        BNS, MV = cut(NT, 6), cut(NT, 2)
        cut = Cut()
        SC = cut(16, NT, P)
        CAND = cut(NT, PEER_H, 256)
        OH = cut(P, TOPK)
        VAL = cut(NT, 16, TOPK)
        IDF = cut(NT, 16, TOPK)
        BEST = cut(NT, P)
        GS = cut(NT, P)
        IA, IB = cut(NT, P), cut(NT, P)
        I1S, I2S = cut(NT, P), cut(NT, P)
        IDX = cut(NT, 16, TOPK).bitcast(u32)
        CI = cut(NT, P).bitcast(u32)
        CIA = cut(NT, P).bitcast(u32)
        PST = cut(NT, PEER_H)
        G = arena[:, :].rearrange("p (c t) -> p c t", c=P)
        cut = Cut()
        XN2 = cut(NT, D)
        XRAW = cut(XC, T + CONVW - 1)
        XBC = cut(XC, T)
        Z = cut(NT, D)
        AQ, AK = cut(4, T), cut(4, T)
        AV = cut(NT, 512)
        XS, XD = cut(NT, D), cut(NT, D)
        PR = cut(4, 4, 384)
        AOUT = cut(NT, 512)
        YOFF = cut(D)
        BM = cut(2, P)
        CB = cut(4, P)
        MLE, MGT = cut(P), cut(P)
        DB = cut(384)
        WD = cut(NK, SSM_H)
        DT, DU, AD = cut(NT, SSM_H), cut(NT, SSM_H), cut(NT, SSM_H)
        ECUM = cut(3, SSM_H)
        SMALL = cut(3, SSM_H)
        LAM = cut(4, AT_D)
        LS = cut(8)
        AMAX, ASUM = cut(16, 2), cut(16, 2)
        PG = cut(D)
        SSTATE = cut(2, 512)
        TA0 = cut(SSM_H, P)
        prf = PR.rearrange("p a b c -> p (a b c)")
        AT = Cut(2048)(24, P)
        at_aout = 2048 + XC * (T + CONVW - 1) + XC * T + 2048 + 2048 + 1024 + 4096 + 6144
        TA = [TA0, Cut(at_aout)(SSM_H, P)]
        W = [XN2.rearrange("p a b -> p (a b)").rearrange("p (h s) -> p h s", h=SSM_H),
             prf[:, 0:2048].rearrange("p (h s) -> p h s", h=SSM_H)]
        XDS = prf[:, 2048:3072]
        ASQ = prf[:, 3072:4096].rearrange("p (t n) -> p t n", t=NT)
        SSQ = prf[:, 4096:6144].rearrange("p (t n) -> p t n", t=NT)
        MIXA = AQ
        MIXS = XBC[:, 0:8, :]
        HID, HAf = sel[:, 0:2], sel[:, 2]
        FG = XBC.rearrange("p c t -> p (c t)")[:, 0:D]
        ones_slot = (EXP0 + 2) % RING
        ONE1 = raw[:, ones_slot, 0:PART].rearrange("p (b j c) -> p b j c", b=2, j=4)
        ONE2 = raw[:, ones_slot, PART:ITEM].rearrange("p (b j c) -> p b j c", b=2, j=4)

        slot_ready = [sem(f"slot_ready{s}") for s in range(RING)]
        part_hi, part_lo, part_used = sem("part_hi"), sem("part_lo"), sem("part_used")
        raw_used, xt_hi, xt_lo, xt_b = sem("raw_used"), sem("xt_hi"), sem("xt_lo"), sem("xt_b")
        x_in, consts_in, rows_in = sem("x_in"), sem("consts_in"), sem("rows_in")
        final_in, post_in, mix_in, out_done = sem("final_in"), sem("post_in"), sem("mix_in"), sem("out_done")
        pool_const, pool_const2 = sem("pool_const"), sem("pool_const2")
        dve_step, act_step, dve_hidden = sem("dve_step"), sem("act_step"), sem("dve_hidden")
        main_done = sem("main_done")
        main_read = {"act": sem("main_read_act"), "dve": sem("main_read_dve")}
        t_done = sem("t_done")
        t_read = [sem("t_read_0"), sem("t_read_1")]
        norm_sq, norm_ms, norm_sd, norm_out = sem("norm_sq"), sem("norm_ms"), sem("norm_sd"), sem("norm_out")
        x_new = sem("x_new")
        gla_abs, gla_ln, gla_l, gla_e = sem("gla_abs"), sem("gla_ln"), sem("gla_l"), sem("gla_e")
        gla_kd, gla_state = sem("gla_kd"), sem("gla_state")
        head_ms, head_sd = sem("head_ms"), sem("head_sd")
        ya_ready, vn_ready, yb_ready, merged, masked = (sem("ya_ready"), sem("vn_ready"), sem("yb_ready"),
                                                        sem("merged"), sem("masked"))
        top_shift, top_exp, sel_ready = sem("top_shift"), sem("top_exp"), sem("sel_ready")
        one_ready, gate_mm, gate_out = sem("one_ready"), sem("gate_mm"), sem("gate_out")
        h_done, gelu_done, a_ready, a_used = sem("h_done"), sem("gelu_done"), sem("a_ready"), sem("a_used")
        gu_done, silu_done, fa_ready, fa_used = sem("gu_done"), sem("silu_done"), sem("fa_ready"), sem("fa_used")
        dt_abs, dt_ln, ad_ready = sem("dt_abs"), sem("dt_ln"), sem("ad_ready")
        conv_out, conv_silu = sem("conv_out"), sem("conv_silu")
        lam_sum, lam_exp = sem("lam_sum"), sem("lam_exp")
        att_max, att_exp, att_a, att_y = sem("att_max"), sem("att_exp"), sem("att_a"), sem("att_y")
        ta_ready, xd_ready, xskip_ready, xds_ready = (sem("ta_ready"), sem("xd_ready"), sem("xskip_ready"),
                                                      sem("xds_ready"))
        w_ready, ssm_y = sem("w_ready"), sem("ssm_y")

        def bank(name):
            return ps[:, MAIN_AT[name] % 4]

        def claim(pe, name):
            i = MAIN_AT[name] - 4
            if i >= 0:
                who = MAIN[i][1]
                pe.wait_ge(main_read[who], reads_upto(i, who))

        def read_out(eng, name):
            i = MAIN_AT[name]
            who = MAIN[i][1]
            eng.wait_ge(main_read[who], reads_upto(i, who))

        def arrived(eng, name):
            eng.wait_ge(main_done, MAIN_AT[name] + 1)
            return bank(name)

        def t_bank(stage, j):
            return ps[:, 6 + (T_AT[stage] + j) % 2]

        def t_claim(pe, stage, j):
            i = T_AT[stage] + j - 2
            if i >= 0:
                t_read_wait(pe, i)

        STREAMS = ["n1", "n2", "ffa", "mix", "ffb"]

        def t_read_wait(eng, i):
            for stage, pairs in TSTAGES:
                j = i - T_AT[stage]
                if 0 <= j < pairs:
                    if stage in STREAMS:
                        eng.wait_ge(xt_lo, 4 * STREAMS.index(stage) + j + 1)
                    else:
                        before = sum(1 for s2, n2 in TSTAGES if s2 not in STREAMS for k in range(n2)
                                     if T_AT[s2] + k <= i and (T_AT[s2] + k) % 2 == i % 2)
                        eng.wait_ge(t_read[i % 2], before)

        def t_read_all(eng, stage, pairs):
            last = T_AT[stage] + pairs - 1
            for i in ((last, last - 1) if pairs > 1 else (last,)):
                t_read_wait(eng, i)

        def t_mine(who, stage, pairs):
            return [j for j in range(pairs) if (T_AT[stage] + j) % 2 == who]

        def item_of(p):
            return p // 2 if p < S_WQ else p // 2 + 8 if p < S_FFB else p // 2 + 14

        def half(item, h):
            return raw[:, item % RING, PART * h:PART * h + PART]

        def wait_part_used(eng, p):
            kind, n = PART_END[p]
            if kind == "main":
                eng.wait_ge(main_done, MAIN_AT[n] + 1)
            else:
                eng.wait_ge({"part_used": part_used, "h_done": h_done, "a_used": a_used, "gu_done": gu_done,
                             "fa_used": fa_used}[kind], n)

        def round_part(act, p):
            act.wait_ge(slot_ready[item_of(p) % RING], 16 * (item_of(p) // RING + 1))
            if p >= NBUF:
                wait_part_used(act, p - NBUF)
            act.activation(whi[:, p % NBUF, :], half(item_of(p), p % 2), ACT.Copy).then_inc(part_hi, 1)

        def rest_part(dve, p):
            dve.wait_ge(part_hi, p + 1)
            dve.tensor_tensor(wlo[:, p % NBUF, :], half(item_of(p), p % 2), whi[:, p % NBUF, :].bitcast(f32),
                              ALU.subtract).then_inc(part_lo, 1)

        block = ctx.enter_context(nc.Block())

        @block.sync
        def _(sp):
            sp.dma_start(X[:, :, :], x.rearrange("a (n p) d -> p (a n) d", p=P)).then_inc(x_in, 16)

            def wait_item_used(item):
                if RAW1 <= item < WQ0:
                    j = item - RAW1
                    if j % 2 == 0:
                        sp.wait_ge(raw_used, j // 2 + 1)
                    else:
                        sp.wait_ge(main_done, MAIN_AT[("pa3", "pb3", "ho1", "ho3")[j // 2]] + 1)
                elif RAW2 <= item < FFB0:
                    j = item - RAW2
                    if j < 5:
                        sp.wait_ge(raw_used, 4 + j + 1)
                    else:
                        sp.wait_ge(main_done, MAIN_AT["wm3"] + 1)
                else:
                    p = 2 * (item if item < RAW1 else item - 8 if item < RAW2 else item - 14) + 1
                    sp.wait_ge(part_lo, p + 1)

            def load(item, src):
                if item >= RING:
                    wait_item_used(item - RING)
                sp.dma_start(raw[:, item % RING, :], src).then_inc(slot_ready[item % RING], 16)

            for j in range(EXP0):
                load(j, panels1[j])

            def stream(item0, count, src, split0):
                for j in range(RING):
                    if item0 + j == EXP0 + 2:
                        sp.wait_ge(gate_mm, T // 4)
                    load(item0 + j, src[j])
                turns = (count - RING) // RING
                with sp.Fori(0, turns, 1) as i:
                    for s in range(RING):
                        sp.wait_ge(part_lo, i * (2 * RING) + (split0 + 2 * s + 2))
                        sp.dma_start(raw[:, (item0 + s) % RING, :], src[i * RING + (RING + s)])\
                          .then_inc(slot_ready[(item0 + s) % RING], 16)
                for j in range(RING * (turns + 1), count):
                    load(item0 + j, src[j])

            stream(EXP0, P, experts, S_EXP)
            sp.dma_start(FG, row_post[0:1, :].broadcast_to([P, D])).then_inc(final_in, 16)
            stream(FFA0, FFI, ffa, S_FFA)
            for j in range(FFB0 - MIX0):
                load(MIX0 + j, panels2[j])
            stream(FFB0, FFI, ffb, S_FFB)
            sp.wait_ge(x_new, 6)
            sp.dma_start(out.rearrange("a (n p) d -> p (a n) d", p=P), X[:, :, :]).then_inc(out_done, 16)
            sp.wait_ge(out_done, 16)

        @block.gpsimd
        def _(pool):
            pool.iota(iota[:, :], pattern=[[1, P]], base=0, channel_multiplier=0,
                      allow_small_or_imprecise_dtypes=True).then_inc(pool_const, 1)
            pool.memset(ident[:, :], 0.0).then_inc(pool_const, 1)
            pool.memset(MDEC, 1.0).then_inc(pool_const, 1)
            pool.memset(C2, 1.0).then_inc(pool_const, 1)
            pool.memset(ALR[0:32, :], 1.0).then_inc(pool_const, 1)
            pool.wait_ge(pool_const, 5)
            pool.affine_select(out=ident[:, :], in_=ident[:, :], compare_op=ALU.not_equal, fill=1.0, base=0,
                               pattern=[[-1, P]], channel_multiplier=1).then_inc(pool_const, 1)
            pool.affine_select(out=MDEC, in_=MDEC, compare_op=ALU.is_gt, fill=0.0, base=0,
                               pattern=[[-1, P]], channel_multiplier=1).then_inc(pool_const, 1)
            pool.wait_ge(pool_const, 7)
            pool.affine_select(out=MDEC[:, 0:CH], in_=MDEC[:, 0:CH], compare_op=ALU.is_ge, fill=0.0, base=CH - 1,
                               pattern=[[0, CH]], channel_multiplier=-1).then_inc(pool_const, 1)
            pool.affine_select(out=C2[:, 0:1], in_=C2[:, 0:1], compare_op=ALU.is_ge, fill=0.0, base=CH - 1,
                               pattern=[[0, 1]], channel_multiplier=-1).then_inc(pool_const, 1)
            pool.affine_select(out=C2[:, 1:2], in_=C2[:, 1:2], compare_op=ALU.is_ge, fill=0.0, base=-CH,
                               pattern=[[0, 1]], channel_multiplier=1).then_inc(pool_const, 1)
            def stream_b(n):
                for j in range(4):
                    pool.wait_ge(xt_hi, 4 * n + j + 1)
                    pool.tensor_copy(XTb[:, 2 * j:2 * j + 2, :], XTh[:, 2 * j:2 * j + 2, :].bitcast(f32))\
                        .then_inc(xt_b, 1)

            pool.wait_ge(rows_in, 16 * 3)
            for g in range(4):
                pool.affine_select(out=WS[:, g, 0:CH], in_=WS[:, g, 0:CH], compare_op=ALU.is_ge, fill=0.0,
                                   base=CH - 1, pattern=[[0, CH]], channel_multiplier=-1).then_inc(masked, 1)
            stream_b(0)
            stream_b(1)

            pool.wait_ge(x_new, 2)
            pool.memset(MLE, 1.0).then_inc(pool_const2, 1)
            pool.memset(MGT, 1.0).then_inc(pool_const2, 1)
            pool.memset(XRAW[:, :, 0:CONVW - 1], 0.0).then_inc(pool_const2, 1)
            pool.iota(DB[:, 0:P], pattern=[[1, P]], base=0, channel_multiplier=-1,
                      allow_small_or_imprecise_dtypes=True).then_inc(pool_const2, 1)
            pool.iota(DB[:, P:384], pattern=[[1, T]], base=-P, channel_multiplier=-1,
                      allow_small_or_imprecise_dtypes=True).then_inc(pool_const2, 1)
            pool.wait_ge(pool_const2, 5)
            pool.affine_select(out=MLE, in_=MLE, compare_op=ALU.is_ge, fill=0.0, base=0,
                               pattern=[[1, P]], channel_multiplier=-1).then_inc(pool_const2, 1)
            pool.affine_select(out=MGT, in_=MGT, compare_op=ALU.is_gt, fill=0.0, base=0,
                               pattern=[[-1, P]], channel_multiplier=1).then_inc(pool_const2, 1)
            pool.affine_select(out=DB[:, 0:P], in_=DB[:, 0:P], compare_op=ALU.is_ge, fill=-1e32, base=0,
                               pattern=[[-1, P]], channel_multiplier=1).then_inc(pool_const2, 1)
            pool.affine_select(out=DB[:, P:384], in_=DB[:, P:384], compare_op=ALU.is_ge, fill=-1e32, base=P,
                               pattern=[[-1, T]], channel_multiplier=1).then_inc(pool_const2, 1)
            stream_b(2)
            stream_b(3)
            pool.wait_ge(pool_const2, 9)
            pool.wait_ge(ad_ready, 1)
            for c in range(2):
                pool.tensor_tensor(TA[c], MGT.unsqueeze(1).broadcast_to([P, SSM_H, P]),
                                   AD[:, c, :].unsqueeze(2).broadcast_to([P, SSM_H, P]), ALU.mult)\
                    .then_inc(ta_ready, 1)
            t_read_all(pool, "xs", 4)
            for c in range(2):
                xs = XS[:, c, :].rearrange("p (h n) -> p h n", h=SSM_H)
                pool.tensor_tensor(XD[:, c, :].rearrange("p (h n) -> p h n", h=SSM_H), xs,
                                   DT[:, c, :].unsqueeze(2).broadcast_to([P, SSM_H, SSM_P]), ALU.mult)\
                    .then_inc(xd_ready, 1)
            pool.wait_ge(xd_ready, 2)
            for c in range(2):
                xs = XS[:, c, :].rearrange("p (h n) -> p h n", h=SSM_H)
                pool.tensor_tensor(xs, xs, SMALL[:, 2, :].unsqueeze(2).broadcast_to([P, SSM_H, SSM_P]), ALU.mult)\
                    .then_inc(xskip_ready, 1)
            read_out(pool, "cum")
            pool.wait_ge(t_done, T_AT["pt"] + 6)
            pool.tensor_tensor(XDS.rearrange("p (h n) -> p h n", h=SSM_H),
                               XD[:, 0, :].rearrange("p (h n) -> p h n", h=SSM_H),
                               ECUM[:, 2, :].unsqueeze(2).broadcast_to([P, SSM_H, SSM_P]), ALU.mult)\
                .then_inc(xds_ready, 1)
            stream_b(4)

        @block.tensor
        def _(pe):
            def transposes(stage, srcs):
                for j in range((len(srcs) + 3) // 4):
                    t_claim(pe, stage, j)
                    for q, s in enumerate(srcs[4 * j:4 * j + 4]):
                        last = pe.transpose(t_bank(stage, j)[:, P * q:P * q + P], s, ident[:, :])
                    last.then_inc(t_done, 1)

            def tiles(src, n):
                return [src[:, tt, P * k:P * k + P] for k in range(n) for tt in range(NT)]

            def products(out, stationary, moving, w_moving, start, stop):
                (xh, xl, xb), (wh, wl) = (stationary, moving) if w_moving else (moving, stationary)
                for n, (w, x) in enumerate(((wh, xh), (wh, xl), (wl, xb))):
                    last = pe.matmul(out, x if w_moving else w, w if w_moving else x, start=start and n == 0,
                                     stop=stop and n == 2)
                return last

            def u_part(out, p):
                wh = whi[:, p % NBUF].rearrange("p (k e) -> p k e", k=NK)
                wl = wlo[:, p % NBUF].rearrange("p (k e) -> p k e", k=NK)
                for k in range(NK):
                    last = products(out, (wh[:, k], wl[:, k]), (XTh[:, k], XTl[:, k], XTb[:, k]), False,
                                    k == 0, k == NK - 1)
                return last

            def v_part(outs, p, b, start, stop):
                last = []
                for tt in range(NT):
                    t = slice(P * tt, P * tt + P)
                    for hf in range(2):
                        c = slice(512 * hf, 512 * hf + 512)
                        last.append(products(outs[2 * tt + hf], (HAh[:, b, t], HAl[:, b, t], HAb[:, b, t]),
                                             (whi[:, p % NBUF, c], wlo[:, p % NBUF, c]), True, start, stop))
                return last

            def by_token(names, p):
                for name in names:
                    claim(pe, name)
                for j in range(4):
                    pe.wait_ge(part_lo, p + j + 1)
                    for tt in range(NT):
                        t = slice(P * tt, P * tt + P)
                        for q in range(2):
                            k, c = 2 * j + q, slice(512 * q, 512 * q + 512)
                            last = products(bank(names[tt]), (XTh[:, k, t], XTl[:, k, t], XTb[:, k, t]),
                                            (whi[:, (p + j) % NBUF, c], wlo[:, (p + j) % NBUF, c]), True,
                                            k == 0, k == NK - 1)
                        if j == 3:
                            last.then_inc(main_done, 1)
                    if j < 3:
                        last.then_inc(part_used, 1)

            def by_feature(names, p):
                for c in range(2 * len(names)):
                    if c % 2 == 0:
                        claim(pe, names[c // 2])
                    pe.wait_ge(part_lo, p + c + 1)
                    u_part(bank(names[c // 2])[:, T * (c % 2):T * (c % 2) + T], p + c)\
                        .then_inc(main_done if c % 2 else part_used, 1)

            def raw_panel(names, items, acts, first=True, last_item=True):
                w512 = len(names) == 2
                for j, item in enumerate(items):
                    if j == 0 and first:
                        for name in names:
                            claim(pe, name)
                    pe.wait_ge(slot_ready[item % RING], 16 * (item // RING + 1))
                    w = raw[:, item % RING, :].rearrange("p (c n) -> p c n", n=512)
                    n_k = 4 if w512 else 2
                    end = last_item and j == len(items) - 1
                    for tt in range(NT):
                        for hf in range(1 if w512 else 2):
                            name = names[tt if w512 else 2 * tt + hf]
                            for k in range(n_k):
                                last = pe.matmul(bank(name), acts[j * n_k + k][:, P * tt:P * tt + P],
                                                 w[:, k if w512 else 2 * k + hf, :],
                                                 start=(first and j == 0 and k == 0), stop=(end and k == n_k - 1))
                            if end:
                                last.then_inc(main_done, 1)
                    if not end:
                        last.then_inc(raw_used, 1)

            def xt_ready(n):
                pe.wait_ge(xt_lo, 4 * n)
                pe.wait_ge(xt_b, 4 * n)

            pe.wait_ge(pool_const, 6)
            pe.wait_ge(norm_out, 1)
            transposes("n1", tiles(XN, NK))
            xt_ready(1)
            pe.wait_ge(consts_in, 16 * 4)
            claim(pe, "alr")
            for k in range(NK):
                for n, part in enumerate((XTh, XTl)):
                    last = pe.matmul(bank("alr")[0:LOWR, 0:T], WL[:, k, :], part[:, k, :].bitcast(f32),
                                     start=(k == 0 and n == 0), stop=(k == NK - 1 and n == 1))
            last.then_inc(main_done, 1)
            by_feature(["q0", "q1"], 0)
            read_out(pe, "alr")
            for tt in range(NT):
                claim(pe, f"z{tt}")
                pe.matmul(bank(f"z{tt}"), ALR[0:LOWR + 1, P * tt:P * tt + P], WG[0:LOWR + 1, :], start=True,
                          stop=True).then_inc(main_done, 1)
            by_token(["k0", "k1"], 4)
            by_token(["v0", "v1"], 8)
            pe.wait_ge(gla_l, 1)
            pe.wait_ge(pool_const, 10)
            for tt in range(NT):
                claim(pe, f"d{tt}")
                pe.matmul(bank(f"d{tt}"), MDEC, L[:, tt, :], start=True, stop=True).then_inc(main_done, 1)
            claim(pe, "tot")
            for tt in range(NT):
                for h in range(GLA_H):
                    c = 2 * (GLA_H * tt + h)
                    last = pe.matmul(bank("tot")[:, c:c + 2], L[:, tt, P * h:P * h + P], C2, start=True, stop=True)
            last.then_inc(main_done, 1)
            by_token(["r0", "r1"], 12)
            by_token(["su0", "su1"], 16)
            pe.wait_ge(gla_kd, 1)
            for n in range(4):
                claim(pe, f"kv{n}")
                rows = slice(CH * (n % 2), CH * (n % 2) + CH)
                for h in range(GLA_H):
                    last = pe.matmul(bank(f"kv{n}")[:, P * h:P * h + P], Kk[rows, n // 2, P * h:P * h + P],
                                     V[rows, n // 2, P * h:P * h + P], start=True, stop=True)
                last.then_inc(main_done, 1)
            by_token(["sv0", "sv1"], 20)
            pe.wait_ge(gla_state, 1)
            for tt in range(NT):
                for j, name in enumerate((f"oe{tt}", f"oo{tt}")):
                    claim(pe, name)
                    for h in range(GLA_H):
                        last = pe.matmul(bank(name)[:, P * h:P * h + P], QT[:, h, P * tt:P * tt + P],
                                         ST[:, 2 * tt + j, h, :],
                                         start=True, stop=True)
                    last.then_inc(main_done, 1)
            by_token(["ga00", "ga01"], 24)
            by_token(["ga10", "ga11"], 28)
            pe.wait_ge(vn_ready, 1)
            pe.wait_ge(masked, 4)
            for tt in range(NT):
                claim(pe, f"mx{tt}")
                for g in range(4):
                    last = pe.matmul(bank(f"mx{tt}")[:, P * g:P * g + P], WS[:, g, :], SV[:, tt, P * g:P * g + P],
                                     start=True, stop=True)
                last.then_inc(main_done, 1)
            by_token(["gb00", "gb01"], 32)
            by_token(["gb10", "gb11"], 36)
            pe.wait_ge(ya_ready, 1)
            transposes("ya", tiles(O, 4))
            pe.wait_ge(yb_ready, 1)
            transposes("yb", tiles(SU, 4))
            t_read_all(pe, "ya", 2)
            raw_panel([f"pa{i}" for i in range(4)], [RAW1, RAW1 + 1], [YAT[:, k] for k in range(4)])
            t_read_all(pe, "yb", 2)
            raw_panel([f"pb{i}" for i in range(4)], [RAW1 + 2, RAW1 + 3], [YBT[:, k] for k in range(4)])
            pe.wait_ge(merged, 1)
            transposes("mg", tiles(XN, NK))
            t_read_all(pe, "mg", 4)
            raw_panel(["ho0", "ho1"], [RAW1 + 4, RAW1 + 5], [MT[:, k] for k in range(NK)])
            raw_panel(["ho2", "ho3"], [RAW1 + 6, RAW1 + 7], [MT[:, k] for k in range(NK)])
            pe.wait_ge(norm_out, 2)
            transposes("n2", tiles(XN, NK))
            xt_ready(2)
            for h in range(PEER_H + 1):
                if h < PEER_H:
                    by_feature([f"wq{h}"], S_WQ + 2 * h)
                if h:
                    read_out(pe, f"wq{h - 1}")
                    claim(pe, f"sc{h - 1}")
                    for a in range(2):
                        for tt in range(NT):
                            c = P * (2 * a + tt)
                            last = pe.matmul(bank(f"sc{h - 1}")[:, c:c + P],
                                             QP[:, 2 * (h - 1) + a, P * tt:P * tt + P], KS[:, a, :], start=True,
                                             stop=True)
                    last.then_inc(main_done, 1)
            pe.wait_ge(sel_ready, 1)
            transposes("idx", [s[:, tt, :] for s in (I1S, I2S, GS) for tt in range(NT)])

            def gate_products(b):
                for j in range(4):
                    last = pe.matmul(ps[:, 4 + b, P * j:P * j + P], ONE1[:, b, j, :], ONE2[:, b, j, :], start=True,
                                     stop=True)
                last.then_inc(gate_mm, 1)

            for g in range(2):
                pe.wait_ge(one_ready, g + 1)
                gate_products(g)
            with pe.Fori(1, T // 8, 1) as pair:
                g = pair * 2
                for b in range(2):
                    pe.wait_ge(one_ready, g + (b + 1))
                    pe.wait_ge(gate_out, g + (b - 1))
                    gate_products(b)
            pe.wait_ge(gate_out, T // 4)

            exps = [bank(f"ex{i}") for i in range(4)]

            def hidden(p, b):
                u_part(ps[:, 4 + b, 0:T], p).then_inc(h_done, 1)

            def expert(n, u, b, start=False, wait_bank=True):
                pe.wait_ge(part_lo, n * 2 + (S_EXP + 3))
                pe.wait_ge(gelu_done, n + 1)
                hidden(u, b)
                output(n, u + 1, n * 2 + (S_EXP + 4), b, start)

            def output(n, p, lo, b, start=False, stop=False):
                pe.wait_ge(part_lo, lo)
                pe.wait_ge(a_ready, n + 1)
                last = v_part(exps, p, b, start, stop)
                if stop:
                    for ins in last:
                        ins.then_inc(main_done, 1)
                else:
                    last[-1].then_inc(a_used, 1)

            for i in range(4):
                claim(pe, f"ex{i}")
            for b in range(2):
                pe.wait_ge(part_lo, S_EXP + b + 1)
                hidden(S_EXP + b, b)
            UN = 2 * NBUF
            for n in range(UN):
                expert(n, S_EXP + 2 + 2 * n, n % 2, start=(n == 0))
            with pe.Fori(1, (P - 2) // UN, 1) as i:
                for s in range(UN):
                    expert(i * UN + s, S_EXP + 2 + 2 * s, s % 2)
            output(P - 2, S_EXP + 2 * P - 2, S_EXP + 2 * P - 1, 0)
            output(P - 1, S_EXP + 2 * P - 1, S_EXP + 2 * P, 1, stop=True)

            def feed_forward(s0, base, outs):
                fb = base

                def gate_up(f, p, lo, b, wait_bank=True):
                    pe.wait_ge(part_lo, lo)
                    if wait_bank:
                        pe.wait_ge(fa_ready, f + (fb - 1))
                    u_part(ps[:, 4 + b, 0:T], p).then_inc(part_used, 1)
                    pe.wait_ge(part_lo, lo + 1)
                    u_part(ps[:, 4 + b, T:2 * T], p + 1).then_inc(gu_done, 1)

                def down(f, p, lo, b, start=False, stop=False):
                    pe.wait_ge(part_lo, lo)
                    pe.wait_ge(fa_ready, f + (fb + 1))
                    last = v_part([bank(name) for name in outs], p, b, start, stop)
                    if stop:
                        for ins in last:
                            ins.then_inc(main_done, 1)
                    else:
                        last[-1].then_inc(fa_used, 1)

                for name in outs:
                    claim(pe, name)
                gate_up(0, s0, s0 + 1, 0, wait_bank=base > 0)

                def chunk(f, s, start=False):
                    gate_up(f + 1, s0 + 2 + 3 * s, f * 3 + (s0 + 3), (s + 1) % 2, wait_bank=not start)
                    down(f, s0 + 4 + 3 * s, f * 3 + (s0 + 5), s % 2, start=start)

                for f in range(2):
                    chunk(f, f, start=(f == 0))
                with pe.Fori(1, (NF - 2) // 2, 1) as i:
                    for s in range(2):
                        chunk(i * 2 + s, s)
                chunk(NF - 2, 0)
                down(NF - 1, s0 + 3 * NF - 1, s0 + 3 * NF, 1, stop=True)

            pe.wait_ge(norm_out, 3)
            transposes("ffa", tiles(XN2, NK))
            xt_ready(3)
            feed_forward(S_FFA, 0, [f"fa{i}" for i in range(4)])

            pe.wait_ge(norm_out, 4)
            transposes("mix", tiles(XN2, NK))
            xt_ready(4)
            pe.wait_ge(mix_in, 16 * 3)
            claim(pe, "dt")
            for tt in range(NT):
                for k in range(NK):
                    for n, part in enumerate((XTh, XTl)):
                        last = pe.matmul(bank("dt")[:, SSM_H * tt:SSM_H * tt + SSM_H],
                                         part[:, k, P * tt:P * tt + P].bitcast(f32), WD[:, k, :],
                                         start=(k == 0 and n == 0), stop=(k == NK - 1 and n == 1))
            last.then_inc(main_done, 1)
            for j in range(3):
                by_feature([f"xb{2 * j}", f"xb{2 * j + 1}"], S_MIX + 4 * j)
            for j in range(2):
                by_token([f"zz{2 * j}", f"zz{2 * j + 1}"], S_MIX + 12 + 4 * j)
            by_feature(["aq0", "aq1"], S_MIX + 20)
            by_feature(["ak0", "ak1"], S_MIX + 24)
            by_token(["av0", "av1"], S_MIX + 28)
            pe.wait_ge(conv_silu, 2)
            transposes("xs", [XBC[:, k, P * tt:P * tt + P] for k in range(8) for tt in range(NT)])
            transposes("bm", [XBC[:, 8 + g, 0:P] for g in range(2)])
            read_out(pe, "ak1")
            for i in range(16):
                r, g = i // 4, i % 4
                claim(pe, f"at{i}")
                rows = slice(AT_D * g, AT_D * g + AT_D)
                pe.matmul(bank(f"at{i}")[:, 0:P], AQ[rows, r, 0:P], AK[rows, r, 0:P], start=True, stop=True)
                pe.matmul(bank(f"at{i}")[:, P:384], AQ[rows, r, P:T], AK[rows, r, :], start=True,
                          stop=True).then_inc(main_done, 1)
            pe.wait_ge(ad_ready, 1)
            pe.wait_ge(pool_const2, 9)
            claim(pe, "cum")
            for n, (m, c) in enumerate(((MLE, 0), (MLE, 1), (MGT, 0))):
                last = pe.matmul(bank("cum")[:, SSM_H * n:SSM_H * n + SSM_H], m, AD[:, c, :], start=True, stop=True)
            last.then_inc(main_done, 1)
            claim(pe, "cb")
            for c in range(2):
                for g in range(2):
                    last = pe.matmul(bank("cb")[:, P * (2 * c + g):P * (2 * c + g) + P],
                                     XBC[:, 8 + g, P * c:P * c + P], XBC[:, 10 + g, P * c:P * c + P], start=True,
                                     stop=True)
            last.then_inc(main_done, 1)

            def between_tokens(c):
                pe.wait_ge(ta_ready, c + 1)
                for q in range(4):
                    claim(pe, f"ss{4 * c + q}")
                    for j in range(4):
                        last = pe.matmul(bank(f"ss{4 * c + q}")[:, P * j:P * j + P], TA[c][:, 4 * q + j, :], MLE,
                                         start=True, stop=True)
                    last.then_inc(main_done, 1)

            between_tokens(0)
            pe.wait_ge(att_a, 1)
            transposes("pt", [PR[:, h // 2, 2 * (h % 2), P * j:P * j + P] for h in range(AT_H) for j in range(3)])
            between_tokens(1)
            pe.wait_ge(xd_ready, 2)
            for c in range(2):
                pe.wait_ge(w_ready, 2 * c + 2)
                for g in range(2):
                    name = f"yd{2 * c + g}"
                    claim(pe, name)
                    for j in range(8):
                        h = 8 * g + j
                        last = pe.matmul(bank(name)[:, SSM_P * j:SSM_P * j + SSM_P], W[c][:, h, :],
                                         XD[:, c, SSM_P * h:SSM_P * h + SSM_P], start=True, stop=True)
                    last.then_inc(main_done, 1)
            pe.wait_ge(xds_ready, 1)
            t_read_all(pe, "bm", 1)
            for g in range(2):
                claim(pe, f"st{g}")
                pe.matmul(bank(f"st{g}"), BM[:, g, :], XDS[:, 512 * g:512 * g + 512], start=True,
                          stop=True).then_inc(main_done, 1)
            read_out(pe, "st1")
            for g in range(2):
                claim(pe, f"yo{g}")
                pe.matmul(bank(f"yo{g}"), XBC[:, 10 + g, P:T], SSTATE[:, g, :], start=True,
                          stop=True).then_inc(main_done, 1)
            t_read_all(pe, "pt", 6)
            read_out(pe, "av1")
            for tt in range(NT):
                claim(pe, f"ao{tt}")
                for h in range(AT_H):
                    for j in range(tt + 1):
                        last = pe.matmul(bank(f"ao{tt}")[:, AT_V * h:AT_V * h + AT_V], AT[:, 3 * h + tt + j, :],
                                         AV[:, j, AT_V * h:AT_V * h + AT_V], start=(j == 0), stop=(j == tt))
                last.then_inc(main_done, 1)
            pe.wait_ge(att_y, 1)
            transposes("att", tiles(AOUT, 4))
            pe.wait_ge(ssm_y, 1)
            transposes("ssm", tiles(XS, NK))
            t_read_all(pe, "att", 2)
            names = [f"wm{i}" for i in range(4)]
            raw_panel(names, [RAW2, RAW2 + 1], [MIXA[:, k] for k in range(4)], last_item=False)
            t_read_all(pe, "ssm", 4)
            raw_panel(names, [RAW2 + 2 + j for j in range(4)], [MIXS[:, k] for k in range(NK)], first=False)
            pe.wait_ge(norm_out, 5)
            transposes("ffb", tiles(XN2, NK))
            xt_ready(5)
            feed_forward(S_FFB, NF, [f"fb{i}" for i in range(4)])

        @block.scalar
        def _(act):
            steps = [0]
            parts = [0]

            def split_to(p):
                for q in range(parts[0], p + 1):
                    round_part(act, q)
                parts[0] = max(parts[0], p + 1)

            def limit(p):
                for end in (S_WQ, S_FFB, S_END):
                    if p < end:
                        return min(p + 2, end - 1)

            def take(name):
                split_to(limit(USE_PART[name]))
                act.wait_ge(main_done, MAIN_AT[name] + 1)
                return bank(name)

            def after(name):
                split_to(limit(USE_PART[name]))
                read_out(act, name)

            def turned_pair(stage, j):
                split_to(limit(T_PART[stage]))
                act.wait_ge(t_done, T_AT[stage] + j + 1)

            def link(ins):
                steps[0] += 1
                ins.then_inc(act_step, 1)
                act.wait_ge(act_step, steps[0])

            def read_done(ins):
                ins.then_inc(main_read["act"], 1)

            def norm_stats(i, parts):
                for n, part in enumerate(parts):
                    w = part.shape[-1]
                    last = act.activation(XN.rearrange("p t d -> p (t d)")[:, w * n:w * n + w], part, ACT.Square,
                                          accum_out=nst[:, i % 2, n:n + 1])
                last.then_inc(norm_sq, 1)
                act.wait_ge(norm_ms, i + 1)
                act.activation(nst[:, i % 2, 6:8], nst[:, i % 2, 4:6], ACT.Sqrt).then_inc(norm_sd, 1)

            def head_root(i, n):
                act.wait_ge(head_ms, i + 1)
                act.activation(hst[:, i % 2, 1, 0:n], hst[:, i % 2, 0, 0:n], ACT.Sqrt).then_inc(head_sd, 1)

            def turned(stage, pairs, dst, gain=None):
                for j in t_mine(1, stage, pairs):
                    turned_pair(stage, j)
                    for q in range(2):
                        k = 2 * j + q
                        last = act.activation(dst[:, k, :], t_bank(stage, j)[:, T * q:T * q + T], ACT.Copy,
                                              scale=1.0 if gain is None else gain(k))
                    last.then_inc(t_read[1], 1)

            def stream_hi(stage, gain):
                for j in range(4):
                    turned_pair(stage, j)
                    for q in range(2):
                        k = 2 * j + q
                        last = act.activation(XTh[:, k, :], t_bank(stage, j)[:, T * q:T * q + T], ACT.Copy,
                                              scale=col(gain, k))
                    last.then_inc(xt_hi, 1)

            act.dma_start(C[:, :], cols).then_inc(consts_in, 16)
            act.dma_start(WL, w_low).then_inc(consts_in, 16)
            act.dma_start(WG[0:LOWR + 1, :], w_gate_up).then_inc(consts_in, 16)
            act.dma_start(KS, k12).then_inc(consts_in, 16)
            act.dma_start(LNG, row_ln[0:1, :].broadcast_to([P, 512])).then_inc(rows_in, 16)
            act.dma_start(LNB, row_ln[1:2, :].broadcast_to([P, 512])).then_inc(rows_in, 16)
            act.dma_start(WS, w_sgu).then_inc(rows_in, 16)

            act.wait_ge(x_in, 16)
            norm_stats(0, [X[:, tt, :] for tt in range(NT)])
            act.wait_ge(consts_in, 16 * 4)
            stream_hi("n1", "norm1")
            split_to(5)
            act.wait_ge(gla_abs, 1)
            link(act.activation(ZA, ZA, ACT.Exp, scale=-1.0))
            act.activation(ZA, ZA, ACT.Ln, bias=1.0).then_inc(gla_ln, 1)
            act.wait_ge(gla_l, 1)
            for tt in range(NT):
                b = take(f"d{tt}")
                read_done(act.activation(ZA[:, tt, :], b, ACT.Exp, scale=1.0 / GLA_TAU))
            b = take("tot")
            read_done(act.activation(DEC, b[:, 0:16], ACT.Exp, scale=1.0 / GLA_TAU))
            for tt in range(NT):
                b = take(f"r{tt}")
                read_done(act.activation(R[:, tt, :], b, ACT.Silu))
            for name, dst in (("su", SU), ("sv", SV)):
                for tt in range(NT):
                    b = take(f"{name}{tt}")
                    read_done(act.activation(dst[:, tt, :], b, ACT.Gelu_apprx_tanh))
            head_root(0, NT)
            head_root(1, 8)
            for name, dst in (("ga", GA), ("gb", GB)):
                for hf in range(2):
                    for tt in range(NT):
                        b = take(f"{name}{hf}{tt}")
                        read_done(act.activation(dst[:, tt, 512 * hf:512 * hf + 512], b, ACT.Sigmoid))
            turned("ya", 2, YAT, lambda k: col("gla", k))
            turned("yb", 2, YBT)
            turned("mg", 4, MT)
            act.wait_ge(x_new, 1)
            norm_stats(1, [X[:, tt, :] for tt in range(NT)])
            stream_hi("n2", "norm2")
            for h in range(PEER_H + 1):
                if h < PEER_H:
                    b = take(f"wq{h}")
                    read_done(act.activation(QP[:, 2 * h:2 * h + 2, :], b.rearrange("p (c t) -> p c t", c=2),
                                             ACT.Copy))
                if h:
                    b = take(f"sc{h - 1}")
                    read_done(act.activation(SC[:, 2 * h - 2:2 * h].rearrange("p a t k -> p (a t k)"), b, ACT.Copy))
            act.wait_ge(top_shift, 1)
            act.activation(GS, GS, ACT.Exp).then_inc(top_exp, 1)
            turned_pair("idx", 1)
            act.activation(gT, t_bank("idx", 1)[:, 0:T], ACT.Copy).then_inc(t_read[1], 1)

            def gate_copy(g, b):
                src = ps[:, 4 + b, :].rearrange("p (j c) -> p c j", j=4)
                act.activation(G[:, :, bass.ds(g * 4, 4)], src, ACT.Copy).then_inc(gate_out, 1)

            with act.Fori(0, T // 8, 1) as pair:
                g = pair * 2
                for b in range(2):
                    act.wait_ge(gate_mm, g + (b + 1))
                    gate_copy(g + b, b)

            def expert_gelu(n, b, wait_read=True):
                act.wait_ge(h_done, n + 1)
                if wait_read:
                    act.wait_ge(a_ready, n - 1)
                act.activation(HID[:, b, :], ps[:, 4 + b, 0:T], ACT.Gelu_apprx_tanh).then_inc(gelu_done, 1)

            UN = 2 * NBUF
            for n in range(UN):
                split_to(S_EXP + 3 + 2 * n)
                expert_gelu(n, n % 2, wait_read=(n >= 2))
            with act.Fori(1, (P - 2) // UN, 1) as i:
                for s in range(UN):
                    n, p = i * UN + s, S_EXP + 2 + 2 * s
                    act.wait_ge(slot_ready[item_of(p) % RING], i * (2 * 16) + 16 * (item_of(p) // RING + 1))
                    act.wait_ge(a_used, n - 1)
                    act.activation(whi[:, p % NBUF, :], half(item_of(p), 0), ACT.Copy).then_inc(part_hi, 1)
                    act.wait_ge(h_done, n + 2)
                    act.activation(whi[:, (p + 1) % NBUF, :], half(item_of(p), 1), ACT.Copy).then_inc(part_hi, 1)
                    expert_gelu(n, s % 2)
            parts[0] = S_EXP + 2 * P - 2
            split_to(S_EXP + 2 * P - 2)
            expert_gelu(P - 2, 0)
            split_to(S_EXP + 2 * P - 1)
            expert_gelu(P - 1, 1)
            split_to(S_FFA + 1)
            act.wait_ge(x_new, 2)
            norm_stats(2, [X[:, tt, :] for tt in range(NT)])
            act.wait_ge(x_new, 3)
            norm_stats(3, [X[:, tt, :] for tt in range(NT)])
            act.dma_start(PG, row_post[1:2, :].broadcast_to([P, D])).then_inc(post_in, 16)
            act.dma_start(WD, w_dt).then_inc(mix_in, 16)
            act.dma_start(SMALL, row_small.rearrange("(o a) n -> o a n", o=1).broadcast_to([P, 3, SSM_H]))\
               .then_inc(mix_in, 16)
            act.dma_start(LAM, row_lam.rearrange("(o a) n -> o a n", o=1).broadcast_to([P, 4, AT_D]))\
               .then_inc(mix_in, 16)
            stream_hi("ffa", "ffa")

            def feed_forward(s0, base):
                def silu(f, b, wait_read=True):
                    act.wait_ge(gu_done, f + (base + 1))
                    if wait_read:
                        act.wait_ge(fa_ready, f + (base - 1))
                    act.activation(HID[:, b, :], ps[:, 4 + b, 0:T], ACT.Silu).then_inc(silu_done, 1)

                used = NF - 1 if base else 0
                counted = FFB_COUNT if base else FFA_COUNT
                split_to(s0 + 4)
                silu(0, 0, wait_read=False)
                split_to(s0 + 7)
                silu(1, 1, wait_read=False)
                with act.Fori(1, NF // 2 - 1, 1) as i:
                    for s in range(2):
                        f, p = i * 2 + s, s0 + 2 + 3 * s
                        for j in range(3):
                            q = p + j
                            act.wait_ge(slot_ready[item_of(q) % RING], i * 16 + 16 * (item_of(q) // RING + 1))
                            if j == 0:
                                act.wait_ge(part_used, f + (counted + 1))
                            elif j == 1:
                                act.wait_ge(gu_done, f + (base + 1))
                            else:
                                act.wait_ge(fa_used, f + used)
                            act.activation(whi[:, q % NBUF, :], half(item_of(q), q % 2), ACT.Copy)\
                               .then_inc(part_hi, 1)
                        silu(f, s)
                parts[0] = s0 + 3 * NF - 4
                split_to(s0 + 3 * NF - 2)
                silu(NF - 2, 0)
                split_to(s0 + 3 * NF - 1)
                silu(NF - 1, 1)
                if not base:
                    split_to(S_MIX + 1)

            feed_forward(S_FFA, 0)
            norm_stats(4, [take(f"fa{i}") for i in range(4)])
            act.wait_ge(x_new, 4)
            act.dma_start(PG, row_post[2:3, :].broadcast_to([P, D])).then_inc(post_in, 16)
            norm_stats(5, [X[:, tt, :] for tt in range(NT)])
            stream_hi("mix", "mix")
            act.wait_ge(dt_abs, 1)
            link(act.activation(DU, DU, ACT.Exp, scale=-1.0))
            act.activation(DU, DU, ACT.Ln, bias=1.0)
            act.activation(SMALL[:, 1, :], SMALL[:, 1, :], ACT.Exp).then_inc(dt_ln, 1)
            act.wait_ge(lam_sum, 1)
            act.activation(LS[:, 2:4], LS[:, 0:2], ACT.Exp).then_inc(lam_exp, 1)
            act.wait_ge(pool_const2, 3)
            for i in range(0, 6, 2):
                b = take(f"xb{i}")
                read_done(act.activation(XRAW[:, 2 * i:2 * i + 2, CONVW - 1:], b.rearrange("p (c t) -> p c t", c=2),
                                         ACT.Copy))
            for j in range(2):
                for tt in range(NT):
                    b = take(f"zz{2 * j + tt}")
                    read_done(act.activation(Z[:, tt, 512 * j:512 * j + 512], b, ACT.Silu))
            act.wait_ge(conv_out, 1)
            act.activation(XBC[:, 0:8, :], XBC[:, 0:8, :], ACT.Silu).then_inc(conv_silu, 1)
            act.activation(XBC[:, 8:12, :], XBC[:, 8:12, :], ACT.Silu).then_inc(conv_silu, 1)
            for tt in range(NT):
                b = take(f"av{tt}")
                read_done(act.activation(AV[:, tt, :], b, ACT.Copy))

            def to_tokens(j):
                turned_pair("xs", j)
                b = t_bank("xs", j).rearrange("p (k t n) -> p t k n", k=2, t=NT)
                dst = XS[:, :, T * j:T * j + T].rearrange("p t (k n) -> p t k n", k=2)
                act.activation(dst, b, ACT.Copy).then_inc(t_read[1], 1)

            for j in t_mine(1, "xs", 4):
                to_tokens(j)
            for j in t_mine(1, "bm", 1):
                turned_pair("bm", 0)
                act.activation(BM, t_bank("bm", 0)[:, 0:2 * P].rearrange("p (g n) -> p g n", g=2), ACT.Copy)\
                   .then_inc(t_read[1], 1)
            b = take("cum")
            read_done(act.activation(ECUM, b[:, 0:3 * SSM_H].rearrange("p (a h) -> p a h", a=3), ACT.Exp))

            def decays(c):
                for q in range(4):
                    b = take(f"ss{4 * c + q}")
                    read_done(act.activation(W[c][:, 4 * q:4 * q + 4, :], b.rearrange("p (j l) -> p j l", j=4),
                                             ACT.Exp))

            decays(0)
            act.wait_ge(att_max, 1)
            for i in range(16):
                r, g = i // 4, i % 4
                for tt, seg in enumerate((slice(0, P), slice(P, 384))):
                    last = act.activation(PR[:, r, g, seg], PR[:, r, g, seg], ACT.Exp, bias=AMAX[:, i, tt:tt + 1],
                                          accum_out=ASUM[:, i, tt:tt + 1])
            last.then_inc(att_exp, 1)
            for j in t_mine(1, "pt", 6):
                turned_pair("pt", j)
                act.activation(AT[:, 4 * j:4 * j + 4, :], t_bank("pt", j).rearrange("p (a q) -> p a q", a=4),
                               ACT.Copy).then_inc(t_read[1], 1)
            decays(1)
            for g in range(2):
                b = take(f"st{g}")
                read_done(act.activation(SSTATE[:, g, :], b, ACT.Copy))
            head_root(2, 16)
            turned("att", 2, MIXA, lambda k: col("subln"))
            head_root(3, 4)
            turned("ssm", 4, MIXS, lambda k: col("ssm", k))
            norm_stats(6, [take(f"wm{i}") for i in range(4)])
            act.wait_ge(x_new, 5)
            act.dma_start(PG, row_post[3:4, :].broadcast_to([P, D])).then_inc(post_in, 16)
            norm_stats(7, [X[:, tt, :] for tt in range(NT)])
            stream_hi("ffb", "ffb")
            feed_forward(S_FFB, NF)
            norm_stats(8, [take(f"fb{i}") for i in range(4)])

        @block.vector
        def _(dve):
            steps = [0]
            parts = [0]

            def split_to(p):
                for q in range(parts[0], p + 1):
                    rest_part(dve, q)
                parts[0] = max(parts[0], p + 1)

            def limit(p):
                for end in (S_WQ, S_FFB, S_END):
                    if p < end:
                        return min(p + 2, end - 1)

            def take(name):
                split_to(limit(USE_PART[name]))
                dve.wait_ge(main_done, MAIN_AT[name] + 1)
                return bank(name)

            def after(name):
                split_to(limit(USE_PART[name]))
                read_out(dve, name)

            def turned_pair(stage, j):
                split_to(limit(T_PART[stage]))
                dve.wait_ge(t_done, T_AT[stage] + j + 1)

            def link(ins):
                steps[0] += 1
                ins.then_inc(dve_step, 1)
                dve.wait_ge(dve_step, steps[0])

            def read_done(ins):
                ins.then_inc(main_read["dve"], 1)

            def norm_scale(i, parts, gain=1.0):
                dve.wait_ge(norm_sq, i + 1)
                if parts == 4:
                    s = nst[:, i % 2, 0:4].rearrange("p (t h) -> p t h", t=2)
                    link(dve.tensor_tensor(nst[:, i % 2, 4:6], s[:, :, 0], s[:, :, 1], ALU.add))
                    src = nst[:, i % 2, 4:6]
                else:
                    src = nst[:, i % 2, 0:2]
                dve.tensor_scalar(nst[:, i % 2, 4:6], src, 1.0 / D, EPS, ALU.mult, ALU.add).then_inc(norm_ms, 1)
                dve.wait_ge(norm_sd, i + 1)
                link(dve.reciprocal(nst[:, i % 2, 8:10], nst[:, i % 2, 6:8]))
                if gain != 1.0:
                    link(dve.tensor_scalar(nst[:, i % 2, 8:10], nst[:, i % 2, 8:10], gain, None, ALU.mult))

            def pre_norm(i, dst):
                norm_scale(i, 2)
                for tt in range(NT):
                    last = dve.tensor_scalar(dst[:, tt, :], X[:, tt, :], nst[:, i % 2, 8 + tt:9 + tt], None, ALU.mult)
                last.then_inc(norm_out, 1)

            def post_norm(i, names, gain, loads):
                norm_scale(i, 4, gain)
                dve.wait_ge(post_in, 16 * loads)
                for n, name in enumerate(names):
                    tt, hf = n // 2, n % 2
                    read_done(dve.scalar_tensor_tensor(XN2[:, tt, 512 * hf:512 * hf + 512], bank(name),
                                                       nst[:, i % 2, 8 + tt:9 + tt], PG[:, 512 * hf:512 * hf + 512],
                                                       ALU.mult, ALU.mult))
                dve.wait_ge(main_read["dve"], reads_upto(MAIN_AT[names[-1]], "dve"))
                dve.tensor_tensor(X[:, :, :], X[:, :, :], XN2, ALU.add).then_inc(x_new, 1)

            def head_scale(i, n, width, gain=1.0):
                dve.tensor_scalar(hst[:, i % 2, 0, 0:n], hst[:, i % 2, 0, 0:n], 1.0 / width, EPS, ALU.mult, ALU.add)\
                   .then_inc(head_ms, 1)
                dve.wait_ge(head_sd, i + 1)
                link(dve.reciprocal(hst[:, i % 2, 1, 0:n], hst[:, i % 2, 1, 0:n]))
                if gain != 1.0:
                    link(dve.tensor_scalar(hst[:, i % 2, 1, 0:n], hst[:, i % 2, 1, 0:n], gain, None, ALU.mult))
                return hst[:, i % 2, 1, 0:n]

            def turned(stage, pairs, dst, gain=None):
                for j in t_mine(0, stage, pairs):
                    turned_pair(stage, j)
                    for q in range(2):
                        k = 2 * j + q
                        src = t_bank(stage, j)[:, T * q:T * q + T]
                        if gain is None:
                            last = dve.tensor_copy(dst[:, k, :], src)
                        else:
                            last = dve.tensor_scalar(dst[:, k, :], src, gain(k), None, ALU.mult)
                    last.then_inc(t_read[0], 1)

            def stream_lo(stage, gain, n):
                for j in range(4):
                    turned_pair(stage, j)
                    dve.wait_ge(xt_hi, 4 * n + j + 1)
                    for q in range(2):
                        k = 2 * j + q
                        last = dve.scalar_tensor_tensor(XTl[:, k, :], t_bank(stage, j)[:, T * q:T * q + T],
                                                        col(gain, k), XTh[:, k, :].bitcast(f32), ALU.mult,
                                                        ALU.subtract)
                    last.then_inc(xt_lo, 1)

            pre_norm(0, XN)
            dve.wait_ge(consts_in, 16 * 4)
            stream_lo("n1", "norm1", 0)
            dve.wait_ge(pool_const, 5)
            b = take("alr")
            read_done(dve.tensor_copy(ALR[0:LOWR, :], b[0:LOWR, 0:T]))
            for j in range(2):
                b = take(f"q{j}")
                read_done(dve.tensor_scalar(QT[:, 2 * j:2 * j + 2, :], b.rearrange("p (c t) -> p c t", c=2),
                                            float(P) ** -0.5, None, ALU.mult))
            for tt in range(NT):
                b = take(f"z{tt}")
                link(dve.tensor_scalar(L[:, tt, :], b, 0.0, None, ALU.min))
                read_done(dve.scalar_tensor_tensor(ZA[:, tt, :], L[:, tt, :], -2.0, b, ALU.mult, ALU.add))
            after("z1")
            dve.sem_inc(gla_abs, 1)
            for name, dst in (("k", Kk), ("v", V)):
                for tt in range(NT):
                    if name == "k" and tt == 0:
                        dve.wait_ge(gla_ln, 1)
                        dve.tensor_tensor(L, L, ZA, ALU.subtract).then_inc(gla_l, 1)
                    b = take(f"{name}{tt}")
                    read_done(dve.tensor_copy(dst[:, tt, :], b))
            after("d1")
            after("k1")
            dve.tensor_tensor(Kk, Kk, ZA, ALU.mult).then_inc(gla_kd, 1)
            after("tot")
            for n in range(4):
                b = take(f"kv{n}")
                if n == 0:
                    ins = dve.tensor_copy(ST[:, 0], b.rearrange("p (h v) -> p h v", h=GLA_H))
                else:
                    for h in range(GLA_H):
                        c = 2 * (GLA_H * (n // 2) + h) + n % 2
                        ins = dve.scalar_tensor_tensor(ST[:, n, h, :], ST[:, n - 1, h, :], DEC[:, c:c + 1],
                                                       b[:, P * h:P * h + P], ALU.mult, ALU.add)
                read_done(ins)
                after(f"kv{n}")
            dve.sem_inc(gla_state, 1)
            dve.wait_ge(rows_in, 16 * 3)
            after("sv1")
            for tt in range(NT):
                ins = dve.bn_stats(BNS[:, tt, :], SV[:, tt, :])
            link(ins)
            for tt in range(NT):
                ins = dve.bn_aggr(MV[:, tt, :], BNS[:, tt, :])
            link(ins)
            link(dve.tensor_copy(hst[:, 0 % 2, 0, 0:NT], MV[:, :, 1]))
            rs = head_scale(0, NT, 1.0)
            for tt in range(NT):
                ins = dve.tensor_scalar(SV[:, tt, :], SV[:, tt, :], MV[:, tt, 0:1], rs[:, tt:tt + 1], ALU.subtract,
                                        ALU.mult)
            link(ins)
            link(dve.tensor_tensor(SV, SV, LNG.unsqueeze(1).broadcast_to([P, NT, 512]), ALU.mult))
            dve.tensor_tensor(SV, SV, LNB.unsqueeze(1).broadcast_to([P, NT, 512]), ALU.add).then_inc(vn_ready, 1)
            for tt in range(NT):
                for j, name in enumerate((f"oe{tt}", f"oo{tt}")):
                    b = take(name)
                    rows = slice(CH * j, CH * j + CH)
                    read_done(dve.tensor_copy(O[rows, tt, :], b[rows, :]))
            after("oo1")
            link(dve.tensor_tensor(OSQ, O, O, ALU.mult))
            link(dve.tensor_reduce(hst[:, 1 % 2, 0, 0:8], OSQ.rearrange("p t (h v) -> p (t h) v", h=GLA_H), AX, ALU.add))
            rs = head_scale(1, 8, P)
            o8 = O.rearrange("p t (h v) -> p (t h) v", h=GLA_H)
            link(dve.tensor_tensor(o8, o8, rs.unsqueeze(2).broadcast_to([P, 8, P]), ALU.mult))
            dve.tensor_tensor(O, O, R, ALU.mult).then_inc(ya_ready, 1)
            for tt in range(NT):
                b = take(f"mx{tt}")
                for g in range(4):
                    ins = dve.scalar_tensor_tensor(SU[:, tt, P * g:P * g + P], b[:, P * g:P * g + P],
                                                   col("sgub", g), SU[:, tt, P * g:P * g + P], ALU.add, ALU.mult)
                read_done(ins)
            after("mx1")
            dve.sem_inc(yb_ready, 1)
            turned("ya", 2, YAT, lambda k: col("gla", k))
            turned("yb", 2, YBT)
            for name, gate in (("pa", GA), ("pb", GB)):
                for i in range(4):
                    tt, hf = i // 2, i % 2
                    b = take(f"{name}{i}")
                    g = gate[:, tt, 512 * hf:512 * hf + 512]
                    if i == 0:
                        after("ga11" if name == "pa" else "gb11")
                    read_done(dve.tensor_tensor(g, g, b, ALU.mult))
            after("pb3")
            dve.tensor_tensor(XN, GA, GB, ALU.add).then_inc(merged, 1)
            turned("mg", 4, MT)
            for i in range(4):
                hf, tt = i // 2, i % 2
                b = take(f"ho{i}")
                xp = X[:, tt, 512 * hf:512 * hf + 512]
                read_done(dve.tensor_tensor(xp, xp, b, ALU.add))
            after("ho3")
            dve.sem_inc(x_new, 1)
            pre_norm(1, XN)
            stream_lo("n2", "norm2", 1)
            def top16(rows, values, indices):
                n = len(rows)
                for k in range(n):
                    ins = dve.max(values[k][:, 0:8], rows[k])
                link(ins)
                for k in range(n):
                    ins = dve.max_index(indices[k][:, 0:8], values[k][:, 0:8], rows[k])
                link(ins)
                for k in range(n):
                    ins = dve.match_replace(rows[k], values[k][:, 0:8], rows[k], NEG)
                link(ins)
                for k in range(n):
                    ins = dve.max(values[k][:, 8:16], rows[k])
                link(ins)
                for k in range(n):
                    ins = dve.max_index(indices[k][:, 8:16], values[k][:, 8:16], rows[k])
                link(ins)

            four = [P, PEER_H, TOPK, TOPK]
            sq = [P, TOPK, TOPK]
            for h in range(PEER_H):
                after(f"sc{h}")
                rows = [(tt, 2 * h + a) for a in range(2) for tt in range(NT)]
                top16([SC[:, hp, tt, :] for tt, hp in rows], [VAL[:, tt, hp, :] for tt, hp in rows],
                      [IDX[:, tt, hp, :] for tt, hp in rows])
                for tt in range(NT):
                    ins = dve.tensor_tensor(CAND[:, tt, h, :].rearrange("p (a b) -> p a b", a=TOPK),
                                            VAL[:, tt, 2 * h, :].unsqueeze(2).broadcast_to(sq),
                                            VAL[:, tt, 2 * h + 1, :].unsqueeze(1).broadcast_to(sq), ALU.add)
                link(ins)
                ranks = slice(TOPK * h, TOPK * h + TOPK)
                top16([CAND[:, tt, h, :] for tt in range(NT)], [BEST[:, tt, ranks] for tt in range(NT)],
                      [CI[:, tt, ranks] for tt in range(NT)])
            link(dve.tensor_copy(IDF, IDX))
            best = BEST.rearrange("p t (h k) -> p (t h) k", h=PEER_H)
            gs = GS.rearrange("p t (h k) -> p (t h) k", h=PEER_H)
            dve.tensor_tensor(gs, best, best[:, :, 0:1].broadcast_to([P, NT * PEER_H, TOPK]), ALU.subtract)\
               .then_inc(top_shift, 1)
            dve.tensor_scalar(CIA, CI, 4, None, ALU.logical_shift_right)
            link(dve.tensor_scalar(CI, CI, 15, None, ALU.bitwise_and))
            dve.tensor_copy(IA, CIA)
            link(dve.tensor_copy(IB, CI))
            for tt in range(NT):
                for side, (rank, dst) in enumerate(((IA, I1S), (IB, I2S))):
                    three = [P, P, TOPK]
                    link(dve.tensor_tensor(OH, rank[:, tt, :].unsqueeze(2).broadcast_to(three),
                                           iota[:, 0:TOPK].unsqueeze(1).broadcast_to(three), ALU.is_equal))
                    oh = OH.rearrange("p (h k) j -> p h k j", h=PEER_H)
                    idf = IDF[:, tt].rearrange("p (h s) k -> p h s k", s=2)[:, :, side, :]
                    link(dve.tensor_tensor(oh, oh, idf.unsqueeze(2).broadcast_to(four), ALU.mult))
                    link(dve.tensor_reduce(dst[:, tt, :], OH, AX, ALU.add))
            dve.wait_ge(top_exp, 1)
            pst = PST.rearrange("p t h -> p (t h)")
            link(dve.tensor_reduce(pst, gs, AX, ALU.add))
            link(dve.reciprocal(pst, pst))
            dve.tensor_tensor(gs, gs, pst.unsqueeze(2).broadcast_to([P, NT * PEER_H, TOPK]), ALU.mult)\
               .then_inc(sel_ready, 1)
            turned_pair("idx", 0)
            dve.tensor_copy(i1T, t_bank("idx", 0)[:, 0:T])
            link(dve.tensor_copy(i2T, t_bank("idx", 0)[:, T:2 * T]))
            dve.sem_inc(t_read[0], 1)
            t_read_wait(dve, T_AT["idx"] + 1)

            def one_hots(g, b):
                for j in range(4):
                    t1 = bass.ds(g * 4 + j, 1)
                    dve.tensor_scalar(ONE1[:, b, j, :], iota[:, :], i1T[:, t1], None, ALU.is_equal)
                    ins = dve.tensor_scalar(ONE2[:, b, j, :], iota[:, :], i2T[:, t1], gT[:, t1], ALU.is_equal,
                                            ALU.mult)
                ins.then_inc(one_ready, 1)

            for g in range(2):
                one_hots(g, g)
            with dve.Fori(1, T // 8, 1) as pair:
                g = pair * 2
                for b in range(2):
                    dve.wait_ge(gate_mm, g + (b - 1))
                    one_hots(g + b, b)

            def expert_gate(n, b, wait_used=True):
                dve.wait_ge(gelu_done, n + 1)
                if wait_used or n:
                    dve.wait_ge(a_ready, n)
                dve.tensor_tensor(HAf, HID[:, b, :], G[:, n, :], ALU.mult).then_inc(dve_hidden, 1)
                dve.wait_ge(dve_hidden, n * 2 + 1)
                if wait_used:
                    dve.wait_ge(a_used, n - 1)
                dve.tensor_copy(HAb[:, b, :], HAf)
                dve.tensor_copy(HAh[:, b, :], HAf).then_inc(dve_hidden, 1)
                dve.wait_ge(dve_hidden, n * 2 + 2)
                dve.tensor_tensor(HAl[:, b, :], HAf, HAh[:, b, :].bitcast(f32), ALU.subtract).then_inc(a_ready, 1)

            UN = 2 * NBUF
            for n in range(UN):
                split_to(S_EXP + 2 + 2 * n)
                expert_gate(n, n % 2, wait_used=(n >= 2))
                split_to(S_EXP + 3 + 2 * n)
            with dve.Fori(1, (P - 2) // UN, 1) as i:
                for s in range(UN):
                    n, p = i * UN + s, S_EXP + 2 + 2 * s
                    for j in range(2):
                        dve.wait_ge(part_hi, n * 2 + (S_EXP + 3 + j))
                        dve.tensor_tensor(wlo[:, (p + j) % NBUF, :], half(item_of(p), j),
                                          whi[:, (p + j) % NBUF, :].bitcast(f32), ALU.subtract).then_inc(part_lo, 1)
                        if j == 0:
                            expert_gate(n, s % 2)
            parts[0] = S_EXP + 2 * P - 2
            split_to(S_EXP + 2 * P - 2)
            expert_gate(P - 2, 0)
            split_to(S_EXP + 2 * P - 1)
            expert_gate(P - 1, 1)
            split_to(S_FFA + 1)
            for i in range(4):
                tt, hf = i // 2, i % 2
                b = take(f"ex{i}")
                xp = X[:, tt, 512 * hf:512 * hf + 512]
                read_done(dve.tensor_tensor(xp, xp, b, ALU.add))
            after("ex3")
            dve.sem_inc(x_new, 1)
            norm_scale(2, 2)
            dve.wait_ge(final_in, 16)
            for tt in range(NT):
                ins = dve.scalar_tensor_tensor(X[:, tt, :], X[:, tt, :], nst[:, 2 % 2, 8 + tt:9 + tt], FG, ALU.mult,
                                               ALU.mult)
            ins.then_inc(x_new, 1)
            dve.wait_ge(x_new, 3)

            def feed_forward(s0, base):
                used = NF - 1 if base else 0

                def times_up(f, b, wait_used=True):
                    dve.wait_ge(silu_done, f + (base + 1))
                    if wait_used or f or base:
                        dve.wait_ge(fa_ready, f + base)
                    dve.tensor_tensor(HAf, HID[:, b, :], ps[:, 4 + b, T:2 * T], ALU.mult).then_inc(dve_hidden, 1)
                    dve.wait_ge(dve_hidden, f * 2 + (2 * (P + base) + 1))
                    if wait_used:
                        dve.wait_ge(fa_used, f + (used - 1))
                    dve.tensor_copy(HAb[:, b, :], HAf)
                    dve.tensor_copy(HAh[:, b, :], HAf).then_inc(dve_hidden, 1)
                    dve.wait_ge(dve_hidden, f * 2 + (2 * (P + base) + 2))
                    dve.tensor_tensor(HAl[:, b, :], HAf, HAh[:, b, :].bitcast(f32), ALU.subtract)\
                       .then_inc(fa_ready, 1)

                split_to(s0 + 4)
                times_up(0, 0, wait_used=False)
                split_to(s0 + 7)
                times_up(1, 1, wait_used=False)
                with dve.Fori(1, NF // 2 - 1, 1) as i:
                    for s in range(2):
                        f, p = i * 2 + s, s0 + 2 + 3 * s
                        for j in range(3):
                            q = p + j
                            dve.wait_ge(part_hi, f * 3 + (s0 + 3 + j))
                            dve.tensor_tensor(wlo[:, q % NBUF, :], half(item_of(q), q % 2),
                                              whi[:, q % NBUF, :].bitcast(f32), ALU.subtract).then_inc(part_lo, 1)
                        times_up(f, s)
                parts[0] = s0 + 3 * NF - 4
                split_to(s0 + 3 * NF - 2)
                times_up(NF - 2, 0)
                split_to(s0 + 3 * NF - 1)
                times_up(NF - 1, 1)
                if not base:
                    split_to(S_MIX + 1)

            pre_norm(3, XN2)
            stream_lo("ffa", "ffa", 2)
            feed_forward(S_FFA, 0)
            post_norm(4, [f"fa{i}" for i in range(4)], 0.5, 1)
            dve.wait_ge(x_new, 4)
            pre_norm(5, XN2)
            stream_lo("mix", "mix", 3)
            dve.wait_ge(mix_in, 16 * 3)
            b = take("dt")
            read_done(dve.tensor_tensor(DT, b[:, 0:2 * SSM_H].rearrange("p (t h) -> p t h", t=NT),
                                        SMALL[:, 0, :].unsqueeze(1).broadcast_to([P, NT, SSM_H]), ALU.add))
            after("dt")
            dve.scalar_tensor_tensor(DU, DT, -1.0, DT, ALU.mult, ALU.max).then_inc(dt_abs, 1)
            link(dve.tensor_scalar(DT, DT, 0.0, None, ALU.max))
            lam = LAM.rearrange("p (a b) n -> p a b n", a=2)
            link(dve.tensor_tensor(lam[:, :, 0, :], lam[:, :, 0, :], lam[:, :, 1, :], ALU.mult))
            dve.tensor_reduce(LS[:, 0:2], lam[:, :, 0, :], AX, ALU.add).then_inc(lam_sum, 1)
            dve.wait_ge(dt_ln, 1)
            link(dve.tensor_tensor(DT, DT, DU, ALU.add))
            ins = dve.scalar_tensor_tensor(AD, DT, -1.0, SMALL[:, 1, :].unsqueeze(1).broadcast_to([P, NT, SSM_H]),
                                           ALU.mult, ALU.mult)
            ins.then_inc(ad_ready, 1)
            dve.wait_ge(lam_exp, 1)
            link(dve.tensor_tensor(LS[:, 4:5], LS[:, 3:4], LS[:, 2:3], ALU.subtract))
            link(dve.tensor_scalar(LS[:, 5:6], LS[:, 4:5], -LAMBDA_INIT, None, ALU.add))
            dve.wait_ge(pool_const2, 3)
            for i in range(1, 6, 2):
                b = take(f"xb{i}")
                read_done(dve.tensor_copy(XRAW[:, 2 * i:2 * i + 2, CONVW - 1:], b.rearrange("p (c t) -> p c t", c=2)))
            after("xb4")
            after("xb5")
            for c in range(XC):
                ins = dve.tensor_scalar(XBC[:, c, :], XRAW[:, c, 0:T], col("convw", CONVW * c), col("convb", c),
                                        ALU.mult, ALU.add)
            link(ins)
            for w in range(1, CONVW):
                for c in range(XC):
                    ins = dve.scalar_tensor_tensor(XBC[:, c, :], XRAW[:, c, w:w + T], col("convw", CONVW * c + w),
                                                   XBC[:, c, :], ALU.mult, ALU.add)
                if w < CONVW - 1:
                    link(ins)
            ins.then_inc(conv_out, 1)
            for name, dst, scale in (("aq", AQ, float(AT_D) ** -0.5), ("ak", AK, 1.0)):
                for j in range(2):
                    b = take(f"{name}{j}")
                    read_done(dve.tensor_scalar(dst[:, 2 * j:2 * j + 2, :], b.rearrange("p (c t) -> p c t", c=2),
                                                scale, None, ALU.mult))
            for j in t_mine(0, "xs", 4):
                turned_pair("xs", j)
                b = t_bank("xs", j).rearrange("p (k t n) -> p t k n", k=2, t=NT)
                dst = XS[:, :, T * j:T * j + T].rearrange("p t (k n) -> p t k n", k=2)
                dve.tensor_copy(dst, b).then_inc(t_read[0], 1)
            for j in t_mine(0, "bm", 1):
                turned_pair("bm", 0)
                dve.tensor_copy(BM, t_bank("bm", 0)[:, 0:2 * P].rearrange("p (g n) -> p g n", g=2))\
                   .then_inc(t_read[0], 1)
            dve.wait_ge(pool_const2, 9)
            for i in range(16):
                r, g = i // 4, i % 4
                h = 2 * r + g // 2
                b = take(f"at{i}")
                read_done(dve.scalar_tensor_tensor(PR[:, r, g, :], DB, 2.0 ** (-8.0 * (h + 1) / AT_H), b[:, 0:384],
                                                   ALU.mult, ALU.add))
            b = take("cb")
            read_done(dve.tensor_tensor(CB, b.rearrange("p (a l) -> p a l", a=4),
                                        MLE.unsqueeze(1).broadcast_to([P, 4, P]), ALU.mult))
            after("cb")
            pr = PR.rearrange("p r g n -> p (r g) n")
            dve.tensor_reduce(AMAX[:, :, 0], pr[:, :, 0:P], AX, ALU.max, negate=True)
            dve.tensor_reduce(AMAX[:, :, 1], pr[:, :, P:384], AX, ALU.max, negate=True).then_inc(att_max, 1)

            def weights(c):
                after(f"ss{4 * c + 3}")
                for g in range(2):
                    w = W[c][:, 8 * g:8 * g + 8, :]
                    dve.tensor_tensor(w, w, CB[:, 2 * c + g, :].unsqueeze(1).broadcast_to([P, 8, P]), ALU.mult)\
                       .then_inc(w_ready, 1)

            weights(0)
            dve.wait_ge(att_exp, 1)
            link(dve.reciprocal(ASUM, ASUM))
            second = ASUM.rearrange("p (h b) t -> p h b t", b=2)[:, :, 1, :]
            link(dve.tensor_scalar(second, second, LS[:, 5:6], None, ALU.mult))
            segs = (slice(0, P), slice(P, 384))
            for i in range(1, 16, 2):
                for tt, seg in enumerate(segs):
                    p2 = PR[:, i // 4, i % 4, seg]
                    ins = dve.tensor_scalar(p2, p2, ASUM[:, i, tt:tt + 1], None, ALU.mult)
            link(ins)
            for i in range(0, 16, 2):
                for tt, seg in enumerate(segs):
                    p1 = PR[:, i // 4, i % 4, seg]
                    ins = dve.scalar_tensor_tensor(p1, p1, ASUM[:, i, tt:tt + 1], PR[:, i // 4, i % 4 + 1, seg],
                                                   ALU.mult, ALU.add)
            ins.then_inc(att_a, 1)
            for j in t_mine(0, "pt", 6):
                turned_pair("pt", j)
                dve.tensor_copy(AT[:, 4 * j:4 * j + 4, :], t_bank("pt", j).rearrange("p (a q) -> p a q", a=4))\
                   .then_inc(t_read[0], 1)
            weights(1)
            dve.wait_ge(xskip_ready, 2)
            for i in range(4):
                c, g = i // 2, i % 2
                b = take(f"yd{i}")
                y = XS[:, c, 512 * g:512 * g + 512]
                read_done(dve.tensor_tensor(y, y, b, ALU.add))
            for g in range(2):
                b = take(f"yo{g}")
                e = ECUM[:, 1, 8 * g:8 * g + 8].unsqueeze(2).broadcast_to([P, 8, SSM_P])
                read_done(dve.tensor_tensor(YOFF[:, 512 * g:512 * g + 512].rearrange("p (h n) -> p h n", h=8),
                                            b.rearrange("p (h n) -> p h n", h=8), e, ALU.mult))
            for tt in range(NT):
                b = take(f"ao{tt}")
                read_done(dve.tensor_copy(AOUT[:, tt, :], b))
            after("ao1")
            link(dve.tensor_tensor(ASQ, AOUT, AOUT, ALU.mult))
            link(dve.tensor_reduce(hst[:, 2 % 2, 0, 0:16], ASQ.rearrange("p t (h v) -> p (t h) v", h=AT_H), AX, ALU.add))
            rs = head_scale(2, 16, AT_V, 1.0 - LAMBDA_INIT)
            a16 = AOUT.rearrange("p t (h v) -> p (t h) v", h=AT_H)
            dve.tensor_tensor(a16, a16, rs.unsqueeze(2).broadcast_to([P, 16, AT_V]), ALU.mult).then_inc(att_y, 1)
            turned("att", 2, MIXA, lambda k: col("subln"))
            link(dve.tensor_tensor(XS[:, 1, :], XS[:, 1, :], YOFF, ALU.add))
            link(dve.tensor_tensor(XS, XS, Z, ALU.mult))
            link(dve.tensor_tensor(SSQ, XS, XS, ALU.mult))
            link(dve.tensor_reduce(hst[:, 3 % 2, 0, 0:4], SSQ.rearrange("p t (g n) -> p (t g) n", g=2), AX, ALU.add))
            rs = head_scale(3, 4, 512)
            y4 = XS.rearrange("p t (g n) -> p (t g) n", g=2)
            dve.tensor_tensor(y4, y4, rs.unsqueeze(2).broadcast_to([P, 4, 512]), ALU.mult).then_inc(ssm_y, 1)
            turned("ssm", 4, MIXS, lambda k: col("ssm", k))
            post_norm(6, [f"wm{i}" for i in range(4)], 1.0, 2)
            dve.wait_ge(x_new, 5)
            pre_norm(7, XN2)
            stream_lo("ffb", "ffb", 4)
            feed_forward(S_FFB, NF)
            post_norm(8, [f"fb{i}" for i in range(4)], 0.5, 3)


def kernel(**inputs):
    import numpy as np
    import concourse.bacc as bacc
    from concourse.bass_utils import run_bass_kernel_spmd as run

    a = {k: np.asarray(v) for k, v in inputs.items()}

    def items(parts):
        return parts.reshape(-1, 2, P, PART).transpose(0, 2, 1, 3).reshape(-1, P, ITEM)

    def tok(w):
        return items(w.reshape(4, 2, P, 512).transpose(0, 2, 1, 3).reshape(4, P, PART))

    def feat(w):
        return items(w.reshape(NK, P, 4, P).transpose(2, 1, 0, 3).reshape(4, P, PART))

    def wide(w):
        return items(w.reshape(4, P, D))

    def features(v, n):
        return v.reshape(n, P).T

    w_in = a["w_in"][0]
    at1 = {"q": 0, "k": 512, "v": 1024, "r": 1536, "su": 2064, "sv": 2576, "ga0": 3088, "ga1": 3600, "gb0": 4112,
           "gb1": 4624}
    p1 = [(feat if n == "q" else tok)(w_in[:, c:c + 512]) for n, c in at1.items()]
    p1 += [wide(a["w_branch_a"][0]), wide(a["w_branch_b"][0])]
    p1 += [tok(a["w_out"][0][:, 512 * j:512 * j + 512]) for j in range(2)]
    p1 += [feat(a["peer_wq"][0][:, 512 * j:512 * j + 512]) for j in range(4)]
    u = a["peer_u"][0].reshape(P, P, NK, P).transpose(1, 3, 2, 0).reshape(P, P, PART)
    v = a["peer_v"][0].reshape(P, P, D).transpose(1, 0, 2)
    between = np.stack([u[2:], v[:-2]], axis=1).reshape(-1, P, PART)
    experts = items(np.concatenate([u[:2], between, v[-2:]]))

    def ffn(n):
        gu = np.stack([a[f"ffn{n}_w_{w}_2"][0].reshape(NK, P, NF, P).transpose(2, 1, 0, 3).reshape(NF, P, PART)
                       for w in ("gate", "up")], axis=1)
        down = a[f"ffn{n}_w_down_2"][0].reshape(NF, 1, P, D)
        steps = np.concatenate([gu[1:], down[:-1]], axis=1).reshape(-1, P, PART)
        return items(np.concatenate([gu[0], steps, down[-1]]))

    w2 = a["w_in_2"][0]
    at2 = {"xbc0": 2560, "xbc1": 3072, "xbc2": 3584, "z0": 1536, "z1": 2048, "aq": 0, "ak": 512, "av": 1024}
    p2 = [(feat if n[0] in "xa" and n != "av" else tok)(w2[:, c:c + 512]) for n, c in at2.items()]
    p2 += [wide(a["w_out_2"][0][512 * j:512 * j + 512]) for j in range(3)]
    cols = np.concatenate([
        features(a["norm1_g"][0], 8), features(a["norm2_g"][0], 8), features(a["gla_norm_g"][0], 4),
        features(a["ffn1_pre_g_2"][0], 8), features(a["mix_pre_g_2"][0], 8), features(a["ffn2_pre_g_2"][0], 8),
        np.tile(a["attn_subln_g_2"][0], 2)[:, None], features(a["ssm_norm_g_2"][0], 8),
        a["conv_w_2"][0].reshape(CONVW, XC, P).transpose(2, 1, 0).reshape(P, -1),
        features(a["conv_b_2"][0], XC), a["sgu_b"][0].T], axis=1)
    arrays = {
        "x": a["x"], "panels1": np.concatenate(p1), "experts": experts, "ffa": ffn(1), "panels2": np.concatenate(p2),
        "ffb": ffn(2), "cols": cols,
        "w_low": w_in[:, 2048:2064].reshape(NK, P, LOWR).transpose(1, 0, 2),
        "w_gate_up": np.concatenate([a["w_gate_up"][0], a["b_gate"]]),
        "w_sgu": a["sgu_w"][0].transpose(2, 0, 1),
        "k12": np.stack([a["peer_k1"][0].T, a["peer_k2"][0].T], axis=1),
        "w_dt": w2[:, 4096:4112].reshape(NK, P, SSM_H).transpose(1, 0, 2),
        "row_ln": np.concatenate([a["sgu_ln_g"], a["sgu_ln_b"]]),
        "row_post": np.stack([a["final_g"], a["ffn1_post_g_2"][0], a["mix_post_g_2"][0], a["ffn2_post_g_2"][0]]),
        "row_small": np.concatenate([a["dt_bias_2"], a["a_log_2"], a["d_skip_2"]]),
        "row_lam": np.concatenate([a[f"lambda_{n}_2"] for n in ("q1", "k1", "q2", "k2")]),
    }
    arrays = {f"in_{n}": np.ascontiguousarray(v) for n, v in arrays.items()}
    nc = bacc.Bacc("TRN2", target_bir_lowering=False, num_devices=1)
    args = [nc.dram_tensor(n, v.shape, mybir.dt.from_np(v.dtype), kind="ExternalInput").ap()
            for n, v in arrays.items()]
    out = nc.dram_tensor("out", (1, T, D), mybir.dt.float32, kind="ExternalOutput").ap()
    program(nc, *args, out)
    r = run(nc, [arrays], core_ids=[0])
    return r.results[0]["out"]
```

```python
import math
from contextlib import ExitStack

import concourse.bass as bass
from concourse import mybir

P = 128
T, D = 256, 1024
NT, NK = T // P, D // P
RING = 3
PART = 1024
ITEM = 2 * PART
NBUF = 3
EPS = 1e-6
GLA_H, GLA_TAU, CH = 4, 16.0, 64
LOWR = 16
PEER_H, TOPK, NKEYS = 8, 16, 128
ONES = 8
BY_ACT = 6
NEG = -3.0e38
FF = 2816
NF = FF // P
AT_H, AT_D, AT_V = 8, 32, 64
LAMBDA_INIT = 0.8 - 0.6 * math.exp(0.0)
SSM_H, SSM_G, SSM_P = 16, 2, 64
XC = 12
CONVW = 4
NORM_PARTS = [2, 2, 2, 2, 4, 2, 4, 2, 4]

PANELS1 = ["q", "k", "v", "r", "su", "sv", "ga0", "ga1", "gb0", "gb1", "wa", "wb", "wo0", "wo1",
           "wq0", "wq1", "wq2", "wq3"]
PANELS2 = ["aq", "ak", "av", "xbc0", "xbc1", "xbc2", "z0", "z1", "wm0", "wm1", "wm2"]
EXP0 = 2 * len(PANELS1)
FFA0 = EXP0 + P
FFI = 3 * NF // 2
MIX0 = FFA0 + FFI
RAW2 = MIX0 + 2 * 8
FFB0 = RAW2 + 2 * 3
ITEMS = FFB0 + FFI
S_WA, S_WB, S_WO, S_WQ, S_EXP = (4 * n for n in (10, 11, 12, 14, 18))
EARLY = 24
S_PRE = S_EXP + EARLY
S_LATE = S_EXP + 2 * EARLY
UN = 2 * NBUF
S_FFA = S_EXP + 2 * P
S_MIX = S_FFA + 3 * NF
S_XB, S_ZZ = S_MIX + 12, S_MIX + 24
S_WM = S_MIX + 32
S_FFB = S_WM + 8
S_END = S_FFB + 3 * NF

COLS = {}
_at = 0
for _name, _n in (("norm1", 8), ("norm2", 8), ("gla", 4), ("ffa", 8), ("mix", 8), ("ffb", 8), ("subln", 1),
                  ("ssm", 8), ("convw", XC * CONVW), ("convb", XC), ("sgub", 4)):
    COLS[_name] = (_at, _n)
    _at += _n
NCOLS = _at

PART_END = {}
MAIN, USE_PART = [], {}
_parts, _counted = 0, 0


def _part(main=None, other=None):
    global _parts, _counted
    if main is None and other is None:
        _counted += 1
        PART_END[_parts] = ("part_used", _counted)
    else:
        PART_END[_parts] = other or ("main", main)
    _parts += 1


def _use(*names_who):
    for name, who in names_who:
        USE_PART[name] = _parts - 1
        MAIN.append((name, who))


def _by_feature(a, b, wa, wb):
    _part(), _part(main=a), _use((a, wa)), _part(), _part(main=b), _use((b, wb))


def _by_token(a, b, who):
    _part(), _part(), _part(), _part(main=b), _use((a, who), (b, who))


_use(("alr", "dve"))
_by_feature("q0", "q1", "dve", "dve")
_use(("z0", "dve"), ("z1", "dve"))
_by_token("k0", "k1", "dve")
_by_token("v0", "v1", "dve")
_use(("d0", "act"), ("d1", "act"), ("tot", "act"))
_by_token("r0", "r1", "act")
_by_token("su0", "su1", "act")
_use(*[(f"kv{n}", "dve") for n in range(4)])
_by_token("sv0", "sv1", "act")
_use(*[(n, "dve") for n in ("oe0", "oo0", "oe1", "oo1")])
_by_token("ga00", "ga01", "act")
_by_token("ga10", "ga11", "act")
_use(("mx0", "dve"), ("mx1", "dve"))
_by_token("gb00", "gb01", "act")
_by_token("gb10", "gb11", "act")
assert _parts == S_WA


def _wide(name, count):
    for _ in range(count - 1):
        _part()
    _part(main=f"{name}3")
    _use(*[(f"{name}{i}", "dve") for i in range(4)])


_wide("pa", 4)
_wide("pb", 4)
_by_token("ho0", "ho1", "dve")
_by_token("ho2", "ho3", "dve")
assert _parts == S_WQ
for _h in range(8):
    _part(), _part(main=f"wq{_h}"), _use((f"wq{_h}", "act"))
    if _h:
        _use((f"sc{_h - 1}", "act"))
_use(("sc7", "act"))
assert _parts == S_EXP
for _n in range(EARLY):
    _part(other=("h_done", _n + 1))
for _n in range(EARLY):
    _part(other=("a_used", _n + 1))
assert _parts == S_LATE and EARLY % UN == 0 and (P - 2 - EARLY) % UN == 0
_part(other=("h_done", EARLY + 1)), _part(other=("h_done", EARLY + 2))
for _n in range(EARLY, P - 2):
    _part(other=("h_done", _n + 3)), _part(other=("a_used", _n + 1))
_part(other=("a_used", P - 1)), _part(main="ex3")
_use(*[(f"ex{i}", "dve") for i in range(4)])


def _feed_forward(base, last):
    _part(), _part(other=("gu_done", base + 1))
    for f in range(NF - 1):
        _part(), _part(other=("gu_done", base + f + 2)), _part(other=("fa_used", (NF - 1) * (base > 0) + f + 1))
    _part(main=last + "3")
    _use(*[(f"{last}{i}", "dve") for i in range(4)])


assert _parts == S_FFA
FFA_COUNT = _counted
_feed_forward(0, "fa")
_use(("dt", "dve"))
_by_feature("aq0", "aq1", "dve", "dve")
_by_feature("ak0", "ak1", "dve", "dve")
_by_token("av0", "av1", "act")
_use(*[(f"at{i}", "dve") for i in range(16)])
for _j in range(3):
    _by_feature(f"xb{2 * _j}", f"xb{2 * _j + 1}", "act", "dve")
_by_token("zz0", "zz1", "act")
_by_token("zz2", "zz3", "act")
_use(("cum", "act"), ("cb", "dve"), *[(f"ss{i}", "act") for i in range(8)],
     *[(f"yd{i}", "dve") for i in range(4)], ("st0", "act"), ("st1", "act"), ("yo0", "dve"), ("yo1", "dve"),
     ("ao0", "dve"), ("ao1", "dve"))
assert _parts == S_WM
_wide("wm", 8)
assert _parts == S_FFB
FFB_COUNT = _counted
_feed_forward(NF, "fb")
assert _parts == S_END
MAIN_AT = {name: i for i, (name, _) in enumerate(MAIN)}
T_PART = {"n1": -1, "ya": S_WA - 1, "yb": S_WA + 3, "mg": S_WO - 1, "n2": S_WQ - 1, "idx": S_PRE - 1,
          "ffa": S_FFA - 1, "mix": S_MIX - 1, "xs": S_WM - 1, "bm": S_WM - 1, "pt": S_WM - 1, "att": S_WM - 1,
          "ssm": S_WM, "ffb": S_FFB - 1}
TSTAGES = [("n1", 4), ("ya", 2), ("yb", 2), ("mg", 4), ("n2", 4), ("idx", 2), ("ffa", 4), ("mix", 4),
           ("xs", 4), ("bm", 1), ("pt", 6), ("att", 2), ("ssm", 4), ("ffb", 4)]
T_AT, _n = {}, 0
for _name, _k in TSTAGES:
    T_AT[_name] = _n
    _n += _k
STREAMS = {"n1": (0, "norm1"), "ya": (0, "gla"), "yb": (4, None), "mg": (0, None), "n2": (0, "norm2"),
           "ffa": (0, "ffa"), "mix": (0, "mix"), "ssm": (0, "ssm"), "ffb": (0, "ffb")}
STREAM_AT, _n = {}, 0
for _name, _k in TSTAGES:
    if _name in STREAMS:
        STREAM_AT[_name] = _n
        _n += _k


def reads_upto(i, who):
    return sum(1 for _, e in MAIN[:i + 1] if e == who)


def program(nc, x, panels1, experts, ffa, panels2, ffb, cols, w_low, w_gate_up, w_sgu, k12, w_dt,
            row_ln, row_post, row_small, row_lam, out):
    f32 = mybir.dt.float32
    u32 = mybir.dt.uint32
    ALU = mybir.AluOpType
    ACT = mybir.ActivationFunctionType
    AX = mybir.AxisListType.X
    f32r = mybir.dt.float32r
    bf16 = mybir.dt.bfloat16
    ctx = ExitStack()
    with ctx:
        def sb(name, shape, dt=f32):
            return ctx.enter_context(nc.sbuf_tensor(name, shape, dt))

        def sem(name):
            return ctx.enter_context(nc.semaphore(name))

        raw = sb("raw", [P, RING, ITEM])
        whi = sb("whi", [P, NBUF, PART], f32r)
        wlo = sb("wlo", [P, NBUF, PART], bf16)
        arena = sb("arena", [P, P * T])
        X = sb("X", [P, NT, D])
        XTh, XTl = sb("XTh", [P, NK, T], f32r), sb("XTl", [P, NK, T], f32r)
        XTb = sb("XTb", [P, NK, T], bf16)
        HAh, HAl = sb("HAh", [P, 2, T], f32r), sb("HAl", [P, 2, T], f32r)
        HAb = sb("HAb", [P, 2, T], bf16)
        sel = sb("sel", [P, 3, T])
        i1T, i2T, gT = sel[:, 0], sel[:, 1], sel[:, 2]
        ident = sb("ident", [P, P])
        iota = sb("iota", [P, P])
        C = sb("C", [P, NCOLS])
        nst = sb("nst", [P, 2, 10])
        hst = sb("hst", [P, 2, 2, 16])
        warm = sb("warm", [P, 4])
        ps = ctx.enter_context(nc.psum_tensor("ps", [P, 8, 512], f32))

        def col(name, k=0):
            a, n = COLS[name]
            assert k < n
            return C[:, a + k:a + k + 1]

        class Cut:
            def __init__(self, at=0):
                self.at = at

            def __call__(self, *dims):
                n = math.prod(dims)
                v = arena[:, self.at:self.at + n]
                self.at += n
                assert self.at <= P * T, self.at
                if len(dims) == 2:
                    v = v.rearrange("p (a b) -> p a b", a=dims[0])
                if len(dims) == 3:
                    v = v.rearrange("p (a b c) -> p a b c", a=dims[0], b=dims[1])
                return v

        QP_AT = 24000
        cut = Cut()
        XN = cut(NT, D)
        Kk, V, R, SU, SV = (cut(NT, 512) for _ in range(5))
        GA, GB = cut(NT, D), cut(NT, D)
        L, ZA, O, OSQ = (cut(NT, 512) for _ in range(4))
        ST = cut(4, GLA_H, P)
        QT = cut(4, T)
        LNG, LNB = cut(512), cut(512)
        WS = cut(4, P)
        cut = Cut(QP_AT)
        QP = cut(16, T)
        MDEC, WG, ALR = cut(P), cut(512), cut(T)
        C2 = cut(2)
        KS = cut(2, P)
        WL = cut(NK, LOWR)
        DEC = cut(16)
        BNS, MV = cut(NT, 6), cut(NT, 2)
        cut = Cut(EARLY * T)
        SC = cut(16, NT, P)
        CAND = cut(NT, PEER_H, 256)
        PICK = cut(TOPK * NT * P // 2).bitcast(bf16).rearrange("p (j n) -> p j n", j=TOPK)
        VAL = cut(NT, 16, TOPK)
        IDF = cut(NT, 16, TOPK)
        BEST = cut(NT, P)
        GS = cut(NT, P)
        IA, IB = cut(NT, P), cut(NT, P)
        I1S, I2S = cut(NT, P), cut(NT, P)
        IDX = cut(NT, 16, TOPK).bitcast(u32)
        CI = cut(NT, P).bitcast(u32)
        CIA = cut(NT, P).bitcast(u32)
        PST = cut(NT, PEER_H)
        assert cut.at <= QP_AT
        G = arena[:, :].rearrange("p (c t) -> p c t", c=P)
        cut = Cut()
        XN2 = cut(NT, D)
        XRAW = cut(XC, T + CONVW - 1)
        XBC = cut(XC, T)
        Z = cut(NT, D)
        AQ, AK = cut(4, T), cut(4, T)
        AV = cut(NT, 512)
        XS, XD = cut(NT, D), cut(NT, D)
        PR = cut(4, 4, 384)
        AOUT = cut(NT, 512)
        YOFF = cut(D)
        BM = cut(2, P)
        CB = cut(4, P)
        MLE, MGT = cut(P), cut(P)
        DB = cut(384)
        WD = cut(NK, SSM_H)
        DT, DU, AD = cut(NT, SSM_H), cut(NT, SSM_H), cut(NT, SSM_H)
        ECUM = cut(3, SSM_H)
        SMALL = cut(3, SSM_H)
        LAM = cut(4, AT_D)
        LS = cut(8)
        AMAX, ASUM = cut(16, 2), cut(16, 2)
        PG = cut(D)
        SSTATE = cut(2, 512)
        TA0 = cut(SSM_H, P)
        prf = PR.rearrange("p a b c -> p (a b c)")
        AT = Cut(2048)(24, P)
        at_aout = 2048 + XC * (T + CONVW - 1) + XC * T + 2048 + 2048 + 1024 + 4096 + 6144
        TA = [TA0, Cut(at_aout)(SSM_H, P)]
        W = [XN2.rearrange("p a b -> p (a b)").rearrange("p (h s) -> p h s", h=SSM_H),
             prf[:, 0:2048].rearrange("p (h s) -> p h s", h=SSM_H)]
        XDS = prf[:, 2048:3072]
        ASQ = prf[:, 3072:4096].rearrange("p (t n) -> p t n", t=NT)
        SSQ = prf[:, 4096:6144].rearrange("p (t n) -> p t n", t=NT)
        MIXA = AQ
        HID, HAf = sel[:, 0:2], sel[:, 2]
        FG = XBC.rearrange("p c t -> p (c t)")[:, 0:D]
        ones_item = EXP0 + EARLY // 2 + 2
        ones_slot = ones_item % RING
        b1 = (S_PRE + 1) % NBUF
        ONE1 = whi[:, b1:b1 + 2].rearrange("p b (j c) -> p b j c", j=ONES)
        HOT2 = wlo[:, b1:b1 + 2].rearrange("p b (j c) -> p b j c", j=ONES)
        ONE2 = raw[:, ones_slot].rearrange("p (b j c) -> p b j c", b=2, j=ONES)

        slot_ready = [sem(f"slot_ready{s}") for s in range(RING)]
        part_hi, part_lo, part_used = sem("part_hi"), sem("part_lo"), sem("part_used")
        raw_used, xt_hi, xt_lo, xt_b = sem("raw_used"), sem("xt_hi"), sem("xt_lo"), sem("xt_b")
        x_in = [sem(f"x_in{tt}") for tt in range(NT)]
        cols_in, low_in, consts_in, rows_in = sem("cols_in"), sem("low_in"), sem("consts_in"), sem("rows_in")
        final_in, post_in, mix_in, out_done = sem("final_in"), sem("post_in"), sem("mix_in"), sem("out_done")
        pool_const, pool_const2 = sem("pool_const"), sem("pool_const2")
        dve_step, act_step, dve_hidden = sem("dve_step"), sem("act_step"), sem("dve_hidden")
        main_done = sem("main_done")
        main_read = {"act": sem("main_read_act"), "dve": sem("main_read_dve")}
        t_done = sem("t_done")
        t_read = [sem("t_read_0"), sem("t_read_1")]
        norm_sq, norm_ms, norm_sd, norm_out = sem("norm_sq"), sem("norm_ms"), sem("norm_sd"), sem("norm_out")
        x_new, x_half = sem("x_new"), sem("x_half")
        gla_abs, gla_ln, gla_l, gla_e = sem("gla_abs"), sem("gla_ln"), sem("gla_l"), sem("gla_e")
        gla_kd, gla_state = sem("gla_kd"), sem("gla_state")
        head_ms, head_sd = sem("head_ms"), sem("head_sd")
        ya_ready, vn_ready, yb_ready, merged, masked = (sem("ya_ready"), sem("vn_ready"), sem("yb_ready"),
                                                        sem("merged"), sem("masked"))
        top_shift, top_exp, sel_ready = sem("top_shift"), sem("top_exp"), sem("sel_ready")
        hot_ready, one_ready, one_scaled = sem("hot_ready"), sem("one_ready"), sem("one_scaled")
        gate_mm, gate_out, gate_mul = sem("gate_mm"), sem("gate_out"), sem("gate_mul")
        h_done, gelu_done, a_ready, a_used = sem("h_done"), sem("gelu_done"), sem("a_ready"), sem("a_used")
        gu_done, silu_done, fa_ready, fa_used = sem("gu_done"), sem("silu_done"), sem("fa_ready"), sem("fa_used")
        dt_abs, dt_ln, ad_ready = sem("dt_abs"), sem("dt_ln"), sem("ad_ready")
        conv_out, conv_silu = sem("conv_out"), sem("conv_silu")
        lam_sum, lam_exp = sem("lam_sum"), sem("lam_exp")
        att_max, att_exp, att_a, att_y = sem("att_max"), sem("att_exp"), sem("att_a"), sem("att_y")
        ta_ready, xd_ready, xskip_ready, xds_ready = (sem("ta_ready"), sem("xd_ready"), sem("xskip_ready"),
                                                      sem("xds_ready"))
        w_ready, ssm_gated, ssm_sq, ssm_y = sem("w_ready"), sem("ssm_gated"), sem("ssm_sq"), sem("ssm_y")

        def bank(name):
            return ps[:, MAIN_AT[name] % 4]

        def claim(pe, name):
            i = MAIN_AT[name] - 4
            if i >= 0:
                who = MAIN[i][1]
                pe.wait_ge(main_read[who], reads_upto(i, who))

        def read_out(eng, name):
            i = MAIN_AT[name]
            who = MAIN[i][1]
            eng.wait_ge(main_read[who], reads_upto(i, who))

        def arrived(eng, name):
            eng.wait_ge(main_done, MAIN_AT[name] + 1)
            return bank(name)

        def t_bank(stage, j):
            return ps[:, 6 + (T_AT[stage] + j) % 2]

        def t_claim(pe, stage, j):
            i = T_AT[stage] + j - 2
            if i >= 0:
                t_read_wait(pe, i)

        def t_read_wait(eng, i):
            for stage, pairs in TSTAGES:
                j = i - T_AT[stage]
                if 0 <= j < pairs:
                    if stage in STREAMS:
                        eng.wait_ge(xt_lo, STREAM_AT[stage] + j + 1)
                    else:
                        before = sum(1 for s2, n2 in TSTAGES if s2 not in STREAMS for k in range(n2)
                                     if T_AT[s2] + k <= i and (T_AT[s2] + k) % 2 == i % 2)
                        eng.wait_ge(t_read[i % 2], before)

        def t_read_all(eng, stage, pairs):
            last = T_AT[stage] + pairs - 1
            for i in ((last, last - 1) if pairs > 1 else (last,)):
                t_read_wait(eng, i)

        def t_mine(who, stage, pairs):
            return [j for j in range(pairs) if (T_AT[stage] + j) % 2 == who]

        def item_of(p):
            return p // 2 if p < S_WM else p // 2 + 2

        def half(item, h):
            return raw[:, item % RING, PART * h:PART * h + PART]

        def wait_part_used(eng, p):
            kind, n = PART_END[p]
            if kind == "main":
                eng.wait_ge(main_done, MAIN_AT[n] + 1)
            else:
                eng.wait_ge({"part_used": part_used, "h_done": h_done, "a_used": a_used, "gu_done": gu_done,
                             "fa_used": fa_used}[kind], n)

        def round_part(act, p):
            act.wait_ge(slot_ready[item_of(p) % RING], 16 * (item_of(p) // RING + 1))
            if p >= NBUF:
                wait_part_used(act, p - NBUF)
            act.activation(whi[:, p % NBUF, :], half(item_of(p), p % 2), ACT.Copy).then_inc(part_hi, 1)

        def rest_part(eng, p):
            eng.wait_ge(part_hi, p + 1)
            eng.tensor_tensor(wlo[:, p % NBUF, :], half(item_of(p), p % 2), whi[:, p % NBUF, :].bitcast(f32),
                              ALU.subtract).then_inc(part_lo, 1)

        block = ctx.enter_context(nc.Block())

        @block.sync
        def _(sp):
            for tt in range(NT):
                sp.dma_start(X[:, tt, :], x[0, P * tt:P * tt + P, :]).then_inc(x_in[tt], 16)
            sp.dma_start(C[:, :], cols).then_inc(cols_in, 16)
            sp.dma_start(WL, w_low).then_inc(low_in, 16)

            def wait_item_used(item):
                if item in (RAW2, RAW2 + 1):
                    sp.wait_ge(raw_used, item - RAW2 + 1)
                else:
                    p = 2 * (item if item < RAW2 else item - 2) + 1
                    sp.wait_ge(part_lo, p + 1)

            def load(item, src):
                if item >= RING:
                    wait_item_used(item - RING)
                sp.dma_start(raw[:, item % RING, :], src).then_inc(slot_ready[item % RING], 16)

            for j in range(EXP0):
                load(j, panels1[j])

            def stream(item0, count, src, split0):
                for j in range(RING):
                    if item0 + j == ones_item:
                        sp.wait_ge(gate_mm, T // ONES)
                    load(item0 + j, src[j])
                turns = (count - RING) // RING
                with sp.Fori(0, turns, 1) as i:
                    for s in range(RING):
                        sp.wait_ge(part_lo, i * (2 * RING) + (split0 + 2 * s + 2))
                        sp.dma_start(raw[:, (item0 + s) % RING, :], src[i * RING + (RING + s)])\
                          .then_inc(slot_ready[(item0 + s) % RING], 16)
                for j in range(RING * (turns + 1), count):
                    load(item0 + j, src[j])

            stream(EXP0, EARLY // 2, experts, S_EXP)
            stream(EXP0 + EARLY // 2, P - EARLY // 2, experts[EARLY // 2:], S_PRE)
            sp.dma_start(FG, row_post[0:1, :].broadcast_to([P, D])).then_inc(final_in, 16)
            stream(FFA0, FFI, ffa, S_FFA)
            for j in range(FFB0 - MIX0):
                load(MIX0 + j, panels2[j])
            stream(FFB0, FFI, ffb, S_FFB)
            for tt, (done, n) in enumerate(((x_half, 4), (x_new, 6))):
                sp.wait_ge(done, n)
                sp.dma_start(out[0, P * tt:P * tt + P, :], X[:, tt, :]).then_inc(out_done, 16)
            sp.wait_ge(out_done, 16 * NT)

        @block.gpsimd
        def _(pool):
            pool.iota(iota[:, :], pattern=[[1, P]], base=0, channel_multiplier=0,
                      allow_small_or_imprecise_dtypes=True).then_inc(pool_const, 1)
            pool.memset(ident[:, :], 0.0).then_inc(pool_const, 1)
            pool.memset(MDEC, 1.0).then_inc(pool_const, 1)
            pool.memset(C2, 1.0).then_inc(pool_const, 1)
            pool.memset(ALR[0:32, :], 1.0).then_inc(pool_const, 1)
            pool.wait_ge(pool_const, 5)
            pool.affine_select(out=ident[:, :], in_=ident[:, :], compare_op=ALU.not_equal, fill=1.0, base=0,
                               pattern=[[-1, P]], channel_multiplier=1).then_inc(pool_const, 1)
            pool.affine_select(out=MDEC, in_=MDEC, compare_op=ALU.is_gt, fill=0.0, base=0,
                               pattern=[[-1, P]], channel_multiplier=1).then_inc(pool_const, 1)
            pool.wait_ge(pool_const, 7)
            pool.affine_select(out=MDEC[:, 0:CH], in_=MDEC[:, 0:CH], compare_op=ALU.is_ge, fill=0.0, base=CH - 1,
                               pattern=[[0, CH]], channel_multiplier=-1).then_inc(pool_const, 1)
            pool.affine_select(out=C2[:, 0:1], in_=C2[:, 0:1], compare_op=ALU.is_ge, fill=0.0, base=CH - 1,
                               pattern=[[0, 1]], channel_multiplier=-1).then_inc(pool_const, 1)
            pool.affine_select(out=C2[:, 1:2], in_=C2[:, 1:2], compare_op=ALU.is_ge, fill=0.0, base=-CH,
                               pattern=[[0, 1]], channel_multiplier=1).then_inc(pool_const, 1)
            pool.wait_ge(rows_in, 16 * 3)
            for g in range(4):
                pool.affine_select(out=WS[:, g, 0:CH], in_=WS[:, g, 0:CH], compare_op=ALU.is_ge, fill=0.0,
                                   base=CH - 1, pattern=[[0, CH]], channel_multiplier=-1).then_inc(masked, 1)
            for i in range(4):
                tt, c = i // 2, slice(512 * (i % 2), 512 * (i % 2) + 512)
                read_out(pool, f"pb{i}")
                pool.tensor_tensor(XN[:, tt, c], GA[:, tt, c], GB[:, tt, c], ALU.add).then_inc(merged, 1)
            pool.wait_ge(part_lo, S_WQ)
            for p in range(S_WQ, S_PRE):
                rest_part(pool, p)

            pool.wait_ge(x_new, 2)
            pool.memset(MLE, 1.0).then_inc(pool_const2, 1)
            pool.memset(MGT, 1.0).then_inc(pool_const2, 1)
            pool.memset(XRAW[:, :, 0:CONVW - 1], 0.0).then_inc(pool_const2, 1)
            pool.iota(DB[:, 0:P], pattern=[[1, P]], base=0, channel_multiplier=-1,
                      allow_small_or_imprecise_dtypes=True).then_inc(pool_const2, 1)
            pool.iota(DB[:, P:384], pattern=[[1, T]], base=-P, channel_multiplier=-1,
                      allow_small_or_imprecise_dtypes=True).then_inc(pool_const2, 1)
            pool.wait_ge(pool_const2, 5)
            pool.affine_select(out=MLE, in_=MLE, compare_op=ALU.is_ge, fill=0.0, base=0,
                               pattern=[[1, P]], channel_multiplier=-1).then_inc(pool_const2, 1)
            pool.affine_select(out=MGT, in_=MGT, compare_op=ALU.is_gt, fill=0.0, base=0,
                               pattern=[[-1, P]], channel_multiplier=1).then_inc(pool_const2, 1)
            pool.affine_select(out=DB[:, 0:P], in_=DB[:, 0:P], compare_op=ALU.is_ge, fill=-1e32, base=0,
                               pattern=[[-1, P]], channel_multiplier=1).then_inc(pool_const2, 1)
            pool.affine_select(out=DB[:, P:384], in_=DB[:, P:384], compare_op=ALU.is_ge, fill=-1e32, base=P,
                               pattern=[[-1, T]], channel_multiplier=1).then_inc(pool_const2, 1)
            pool.wait_ge(part_lo, S_ZZ)
            for p in range(S_ZZ, S_WM):
                rest_part(pool, p)
            pool.wait_ge(pool_const2, 9)
            pool.wait_ge(ad_ready, 1)
            for c in range(2):
                pool.tensor_tensor(TA[c], MGT.unsqueeze(1).broadcast_to([P, SSM_H, P]),
                                   AD[:, c, :].unsqueeze(2).broadcast_to([P, SSM_H, P]), ALU.mult)\
                    .then_inc(ta_ready, 1)
            t_read_all(pool, "xs", 4)
            for c in range(2):
                xs = XS[:, c, :].rearrange("p (h n) -> p h n", h=SSM_H)
                pool.tensor_tensor(XD[:, c, :].rearrange("p (h n) -> p h n", h=SSM_H), xs,
                                   DT[:, c, :].unsqueeze(2).broadcast_to([P, SSM_H, SSM_P]), ALU.mult)\
                    .then_inc(xd_ready, 1)
            pool.wait_ge(xd_ready, 2)
            for c in range(2):
                xs = XS[:, c, :].rearrange("p (h n) -> p h n", h=SSM_H)
                pool.tensor_tensor(xs, xs, SMALL[:, 2, :].unsqueeze(2).broadcast_to([P, SSM_H, SSM_P]), ALU.mult)\
                    .then_inc(xskip_ready, 1)
            read_out(pool, "cum")
            pool.wait_ge(t_done, T_AT["pt"] + 6)
            pool.tensor_tensor(XDS.rearrange("p (h n) -> p h n", h=SSM_H),
                               XD[:, 0, :].rearrange("p (h n) -> p h n", h=SSM_H),
                               ECUM[:, 2, :].unsqueeze(2).broadcast_to([P, SSM_H, SSM_P]), ALU.mult)\
                .then_inc(xds_ready, 1)

        @block.tensor
        def _(pe):
            def transposes(stage, srcs, norm=None):
                for j in range((len(srcs) + 3) // 4):
                    t_claim(pe, stage, j)
                    four = list(enumerate(srcs[4 * j:4 * j + 4]))
                    for n, (q, s) in enumerate(four[0::2] + four[1::2]):
                        if norm is not None and j == 0 and n in (0, 2):
                            pe.wait_ge(norm_out, 2 * norm + n // 2 + 1)
                        last = pe.transpose(t_bank(stage, j)[:, P * q:P * q + P], s, ident[:, :])
                    last.then_inc(t_done, 1)

            def tiles(src, n):
                return [src[:, tt, P * k:P * k + P] for k in range(n) for tt in range(NT)]

            def products(out, stationary, moving, w_moving, start, stop):
                (xh, xl, xb), (wh, wl) = (stationary, moving) if w_moving else (moving, stationary)
                for n, (w, x) in enumerate(((wh, xh), (wh, xl), (wl, xb))):
                    last = pe.matmul(out, x if w_moving else w, w if w_moving else x, start=start and n == 0,
                                     stop=stop and n == 2)
                return last

            chunks_of = [None]

            def chunk_in(k):
                stage = chunks_of[0]
                if stage and k % 2 == 0:
                    n = STREAM_AT[stage] + (k - STREAMS[stage][0]) // 2 + 1
                    pe.wait_ge(xt_lo, n)
                    pe.wait_ge(xt_b, n)
                if stage and k + 1 == STREAMS[stage][0] + 2 * dict(TSTAGES)[stage]:
                    chunks_of[0] = None

            def u_part(out, p):
                wh = whi[:, p % NBUF].rearrange("p (k e) -> p k e", k=NK)
                wl = wlo[:, p % NBUF].rearrange("p (k e) -> p k e", k=NK)
                for k in range(NK):
                    chunk_in(k)
                    last = products(out, (wh[:, k], wl[:, k]), (XTh[:, k], XTl[:, k], XTb[:, k]), False,
                                    k == 0, k == NK - 1)
                return last

            def v_part(outs, p, acts, start, stop):
                last = []
                for tt in range(NT):
                    t = slice(P * tt, P * tt + P)
                    for hf in range(2):
                        c = slice(512 * hf, 512 * hf + 512)
                        last.append(products(outs[2 * tt + hf], tuple(a[:, t] for a in acts),
                                             (whi[:, p % NBUF, c], wlo[:, p % NBUF, c]), True, start, stop))
                return last

            def hidden_acts(b):
                return HAh[:, b], HAl[:, b], HAb[:, b]

            def wide_panel(names, p, chunks, start=True):
                for n, k in enumerate(chunks):
                    stop = n == len(chunks) - 1
                    pe.wait_ge(part_lo, p + n + 1)
                    chunk_in(k)
                    last = v_part([bank(name) for name in names], p + n, (XTh[:, k], XTl[:, k], XTb[:, k]),
                                  start and n == 0, stop)
                    if stop:
                        for ins in last:
                            ins.then_inc(main_done, 1)
                    else:
                        last[-1].then_inc(part_used, 1)

            def by_token(names, p):
                for name in names:
                    claim(pe, name)
                for j in range(4):
                    pe.wait_ge(part_lo, p + j + 1)
                    for tt in range(NT):
                        t = slice(P * tt, P * tt + P)
                        for q in range(2):
                            k, c = 2 * j + q, slice(512 * q, 512 * q + 512)
                            chunk_in(k)
                            last = products(bank(names[tt]), (XTh[:, k, t], XTl[:, k, t], XTb[:, k, t]),
                                            (whi[:, (p + j) % NBUF, c], wlo[:, (p + j) % NBUF, c]), True,
                                            k == 0, k == NK - 1)
                        if j == 3:
                            last.then_inc(main_done, 1)
                    if j < 3:
                        last.then_inc(part_used, 1)

            def by_feature(names, p):
                for c in range(2 * len(names)):
                    if c % 2 == 0:
                        claim(pe, names[c // 2])
                    pe.wait_ge(part_lo, p + c + 1)
                    u_part(bank(names[c // 2])[:, T * (c % 2):T * (c % 2) + T], p + c)\
                        .then_inc(main_done if c % 2 else part_used, 1)

            def raw_panel(names, items, acts):
                for name in names:
                    claim(pe, name)
                for j, item in enumerate(items):
                    pe.wait_ge(slot_ready[item % RING], 16 * (item // RING + 1))
                    w = raw[:, item % RING, :].rearrange("p (c n) -> p c n", n=512)
                    for tt in range(NT):
                        for hf in range(2):
                            for k in range(2):
                                last = pe.matmul(bank(names[2 * tt + hf]), acts[2 * j + k][:, P * tt:P * tt + P],
                                                 w[:, 2 * k + hf, :], start=(j == 0 and k == 0), stop=False)
                    last.then_inc(raw_used, 1)

            def new_stream(stage):
                chunks_of[0] = stage

            pe.wait_ge(pool_const, 6)
            transposes("n1", tiles(XN, NK), norm=0)
            new_stream("n1")
            pe.wait_ge(low_in, 16)
            claim(pe, "alr")
            for k in range(NK):
                chunk_in(k)
                for n, part in enumerate((XTh, XTl)):
                    last = pe.matmul(bank("alr")[0:LOWR, 0:T], WL[:, k, :], part[:, k, :].bitcast(f32),
                                     start=(k == 0 and n == 0), stop=(k == NK - 1 and n == 1))
            last.then_inc(main_done, 1)
            by_feature(["q0", "q1"], 0)
            read_out(pe, "alr")
            pe.wait_ge(consts_in, 16 * 2)
            for tt in range(NT):
                claim(pe, f"z{tt}")
                pe.matmul(bank(f"z{tt}"), ALR[0:LOWR + 1, P * tt:P * tt + P], WG[0:LOWR + 1, :], start=True,
                          stop=True).then_inc(main_done, 1)
            by_token(["k0", "k1"], 4)
            by_token(["v0", "v1"], 8)
            pe.wait_ge(gla_l, 1)
            pe.wait_ge(pool_const, 10)
            for tt in range(NT):
                claim(pe, f"d{tt}")
                pe.matmul(bank(f"d{tt}"), MDEC, L[:, tt, :], start=True, stop=True).then_inc(main_done, 1)
            claim(pe, "tot")
            for tt in range(NT):
                for h in range(GLA_H):
                    c = 2 * (GLA_H * tt + h)
                    last = pe.matmul(bank("tot")[:, c:c + 2], L[:, tt, P * h:P * h + P], C2, start=True, stop=True)
            last.then_inc(main_done, 1)
            by_token(["r0", "r1"], 12)
            by_token(["su0", "su1"], 16)
            pe.wait_ge(gla_kd, 1)
            for n in range(4):
                claim(pe, f"kv{n}")
                rows = slice(CH * (n % 2), CH * (n % 2) + CH)
                for h in range(GLA_H):
                    last = pe.matmul(bank(f"kv{n}")[:, P * h:P * h + P], Kk[rows, n // 2, P * h:P * h + P],
                                     V[rows, n // 2, P * h:P * h + P], start=True, stop=True)
                last.then_inc(main_done, 1)
            by_token(["sv0", "sv1"], 20)
            pe.wait_ge(gla_state, 1)
            for tt in range(NT):
                for j, name in enumerate((f"oe{tt}", f"oo{tt}")):
                    claim(pe, name)
                    for h in range(GLA_H):
                        last = pe.matmul(bank(name)[:, P * h:P * h + P], QT[:, h, P * tt:P * tt + P],
                                         ST[:, 2 * tt + j, h, :],
                                         start=True, stop=True)
                    last.then_inc(main_done, 1)
            by_token(["ga00", "ga01"], 24)
            by_token(["ga10", "ga11"], 28)
            pe.wait_ge(vn_ready, 1)
            pe.wait_ge(masked, 4)
            for tt in range(NT):
                claim(pe, f"mx{tt}")
                for g in range(4):
                    last = pe.matmul(bank(f"mx{tt}")[:, P * g:P * g + P], WS[:, g, :], SV[:, tt, P * g:P * g + P],
                                     start=True, stop=True)
                last.then_inc(main_done, 1)
            by_token(["gb00", "gb01"], 32)
            by_token(["gb10", "gb11"], 36)
            pe.wait_ge(ya_ready, 1)
            transposes("ya", tiles(O, 4))
            def claim_all(names):
                for name in names:
                    claim(pe, name)

            pa, pb = [[f"{n}{i}" for i in range(4)] for n in ("pa", "pb")]
            claim_all(pa)
            new_stream("ya")
            wide_panel(pa, S_WA, range(4))
            pe.wait_ge(yb_ready, 1)
            transposes("yb", tiles(SU, 4))
            claim_all(pb)
            new_stream("yb")
            wide_panel(pb, S_WB, range(4, 8))
            pe.wait_ge(merged, 4)
            transposes("mg", tiles(XN, NK))
            new_stream("mg")
            by_token(["ho0", "ho1"], S_WO)
            by_token(["ho2", "ho3"], S_WO + 4)
            transposes("n2", tiles(XN, NK), norm=1)
            new_stream("n2")
            for h in range(PEER_H + 1):
                if h < PEER_H:
                    by_feature([f"wq{h}"], S_WQ + 2 * h)
                if h:
                    read_out(pe, f"wq{h - 1}")
                    claim(pe, f"sc{h - 1}")
                    for a in range(2):
                        for tt in range(NT):
                            c = P * (2 * a + tt)
                            last = pe.matmul(bank(f"sc{h - 1}")[:, c:c + P],
                                             QP[:, 2 * (h - 1) + a, P * tt:P * tt + P], KS[:, a, :], start=True,
                                             stop=True)
                    last.then_inc(main_done, 1)
            def hidden(p, b):
                u_part(ps[:, 4 + b, 0:T], p).then_inc(h_done, 1)

            for n in range(UN):
                pe.wait_ge(part_lo, S_EXP + n + 1)
                if n >= 2:
                    pe.wait_ge(gelu_done, n - 1)
                hidden(S_EXP + n, n % 2)
            with pe.Fori(1, EARLY // UN, 1) as i:
                for s in range(UN):
                    pe.wait_ge(part_lo, i * UN + (S_EXP + s + 1))
                    pe.wait_ge(gelu_done, i * UN + (s - 1))
                    hidden(S_EXP + s, s % 2)

            pe.wait_ge(sel_ready, 1)
            transposes("idx", [s[:, tt, :] for s in (I1S, I2S, GS) for tt in range(NT)])

            def gate_products(b):
                for j in range(ONES):
                    last = pe.matmul(ps[:, 4 + 2 * b + j // 4, P * (j % 4):P * (j % 4) + P],
                                     ONE1[:, b, j, :].bitcast(f32), ONE2[:, b, j, :], start=True, stop=True)
                last.then_inc(gate_mm, 1)

            pe.wait_ge(gelu_done, EARLY)
            for g in range(2):
                pe.wait_ge(one_ready, g + 1)
                pe.wait_ge(one_scaled, g + 1)
                gate_products(g)
            with pe.Fori(1, T // (2 * ONES), 1) as pair:
                g = pair * 2
                for b in range(2):
                    pe.wait_ge(one_ready, g + (b + 1))
                    pe.wait_ge(one_scaled, g + (b + 1))
                    pe.wait_ge(gate_out, g + (b - 1))
                    pe.wait_ge(gate_mul, g + (b - 1))
                    gate_products(b)
            pe.wait_ge(gate_out, T // ONES)
            pe.wait_ge(gate_mul, T // ONES)

            exps = [bank(f"ex{i}") for i in range(4)]

            def expert(n, u, b):
                pe.wait_ge(part_lo, n * 2 + (S_EXP + 3))
                pe.wait_ge(gelu_done, n + 1)
                hidden(u, b)
                output(n, u + 1, n * 2 + (S_EXP + 4), b)

            def output(n, p, lo, b, start=False, stop=False):
                pe.wait_ge(part_lo, lo)
                pe.wait_ge(a_ready, n + 1)
                last = v_part(exps, p, hidden_acts(b), start, stop)
                if stop:
                    for ins in last:
                        ins.then_inc(main_done, 1)
                else:
                    last[-1].then_inc(a_used, 1)

            for i in range(4):
                claim(pe, f"ex{i}")
            for n in range(UN):
                output(n, S_PRE + n, S_PRE + n + 1, n % 2, start=(n == 0))
            with pe.Fori(1, EARLY // UN, 1) as i:
                for s in range(UN):
                    output(i * UN + s, S_PRE + s, i * UN + (S_PRE + s + 1), s % 2)
            for b in range(2):
                pe.wait_ge(part_lo, S_LATE + b + 1)
                hidden(S_LATE + b, b)
            with pe.Fori(0, (P - 2 - EARLY) // UN, 1) as i:
                for s in range(UN):
                    expert(i * UN + (EARLY + s), S_LATE + 2 + 2 * s, s % 2)
            output(P - 2, S_EXP + 2 * P - 2, S_EXP + 2 * P - 1, 0)
            output(P - 1, S_EXP + 2 * P - 1, S_EXP + 2 * P, 1, stop=True)

            def feed_forward(s0, base, outs):
                fb = base

                def gate_up(f, p, lo, b, wait_bank=True):
                    pe.wait_ge(part_lo, lo)
                    if wait_bank:
                        pe.wait_ge(fa_ready, f + (fb - 1))
                    u_part(ps[:, 4 + b, 0:T], p).then_inc(part_used, 1)
                    pe.wait_ge(part_lo, lo + 1)
                    u_part(ps[:, 4 + b, T:2 * T], p + 1).then_inc(gu_done, 1)

                def down(f, p, lo, b, start=False, stop=False):
                    pe.wait_ge(part_lo, lo)
                    pe.wait_ge(fa_ready, f + (fb + 1))
                    last = v_part([bank(name) for name in outs], p, hidden_acts(b), start, stop)
                    if stop:
                        for ins in last:
                            ins.then_inc(main_done, 1)
                    else:
                        last[-1].then_inc(fa_used, 1)

                for name in outs:
                    claim(pe, name)
                gate_up(0, s0, s0 + 1, 0, wait_bank=base > 0)

                def chunk(f, s, start=False):
                    gate_up(f + 1, s0 + 2 + 3 * s, f * 3 + (s0 + 3), (s + 1) % 2, wait_bank=not start)
                    down(f, s0 + 4 + 3 * s, f * 3 + (s0 + 5), s % 2, start=start)

                for f in range(2):
                    chunk(f, f, start=(f == 0))
                with pe.Fori(1, (NF - 2) // 2, 1) as i:
                    for s in range(2):
                        chunk(i * 2 + s, s)
                chunk(NF - 2, 0)
                down(NF - 1, s0 + 3 * NF - 1, s0 + 3 * NF, 1, stop=True)

            transposes("ffa", tiles(XN2, NK), norm=2)
            new_stream("ffa")
            feed_forward(S_FFA, 0, [f"fa{i}" for i in range(4)])

            transposes("mix", tiles(XN2, NK), norm=3)
            new_stream("mix")
            pe.wait_ge(mix_in, 16 * 3)
            claim(pe, "dt")
            for tt in range(NT):
                for k in range(NK):
                    chunk_in(k)
                    for n, part in enumerate((XTh, XTl)):
                        last = pe.matmul(bank("dt")[:, SSM_H * tt:SSM_H * tt + SSM_H],
                                         part[:, k, P * tt:P * tt + P].bitcast(f32), WD[:, k, :],
                                         start=(k == 0 and n == 0), stop=(k == NK - 1 and n == 1))
            last.then_inc(main_done, 1)
            by_feature(["aq0", "aq1"], S_MIX)
            by_feature(["ak0", "ak1"], S_MIX + 4)
            by_token(["av0", "av1"], S_MIX + 8)
            read_out(pe, "ak1")
            for i in range(16):
                r, g = i // 4, i % 4
                claim(pe, f"at{i}")
                rows = slice(AT_D * g, AT_D * g + AT_D)
                pe.matmul(bank(f"at{i}")[:, 0:P], AQ[rows, r, 0:P], AK[rows, r, 0:P], start=True, stop=True)
                pe.matmul(bank(f"at{i}")[:, P:384], AQ[rows, r, P:T], AK[rows, r, :], start=True,
                          stop=True).then_inc(main_done, 1)
            for j in range(3):
                by_feature([f"xb{2 * j}", f"xb{2 * j + 1}"], S_XB + 4 * j)
            for j in range(2):
                by_token([f"zz{2 * j}", f"zz{2 * j + 1}"], S_ZZ + 4 * j)
            pe.wait_ge(conv_silu, 2)
            transposes("xs", [XBC[:, k, P * tt:P * tt + P] for k in range(8) for tt in range(NT)])
            transposes("bm", [XBC[:, 8 + g, 0:P] for g in range(2)])
            pe.wait_ge(ad_ready, 1)
            pe.wait_ge(pool_const2, 9)
            claim(pe, "cum")
            for n, (m, c) in enumerate(((MLE, 0), (MLE, 1), (MGT, 0))):
                last = pe.matmul(bank("cum")[:, SSM_H * n:SSM_H * n + SSM_H], m, AD[:, c, :], start=True, stop=True)
            last.then_inc(main_done, 1)
            claim(pe, "cb")
            for c in range(2):
                for g in range(2):
                    last = pe.matmul(bank("cb")[:, P * (2 * c + g):P * (2 * c + g) + P],
                                     XBC[:, 8 + g, P * c:P * c + P], XBC[:, 10 + g, P * c:P * c + P], start=True,
                                     stop=True)
            last.then_inc(main_done, 1)

            def between_tokens(c):
                pe.wait_ge(ta_ready, c + 1)
                for q in range(4):
                    claim(pe, f"ss{4 * c + q}")
                    for j in range(4):
                        last = pe.matmul(bank(f"ss{4 * c + q}")[:, P * j:P * j + P], TA[c][:, 4 * q + j, :], MLE,
                                         start=True, stop=True)
                    last.then_inc(main_done, 1)

            between_tokens(0)
            pe.wait_ge(att_a, 1)
            transposes("pt", [PR[:, h // 2, 2 * (h % 2), P * j:P * j + P] for h in range(AT_H) for j in range(3)])
            between_tokens(1)
            pe.wait_ge(xd_ready, 2)
            for c in range(2):
                pe.wait_ge(w_ready, 2 * c + 2)
                for g in range(2):
                    name = f"yd{2 * c + g}"
                    claim(pe, name)
                    for j in range(8):
                        h = 8 * g + j
                        last = pe.matmul(bank(name)[:, SSM_P * j:SSM_P * j + SSM_P], W[c][:, h, :],
                                         XD[:, c, SSM_P * h:SSM_P * h + SSM_P], start=True, stop=True)
                    last.then_inc(main_done, 1)
            pe.wait_ge(xds_ready, 1)
            t_read_all(pe, "bm", 1)
            for g in range(2):
                claim(pe, f"st{g}")
                pe.matmul(bank(f"st{g}"), BM[:, g, :], XDS[:, 512 * g:512 * g + 512], start=True,
                          stop=True).then_inc(main_done, 1)
            read_out(pe, "st1")
            for g in range(2):
                claim(pe, f"yo{g}")
                pe.matmul(bank(f"yo{g}"), XBC[:, 10 + g, P:T], SSTATE[:, g, :], start=True,
                          stop=True).then_inc(main_done, 1)
            t_read_all(pe, "pt", 6)
            read_out(pe, "av1")
            for tt in range(NT):
                claim(pe, f"ao{tt}")
                for h in range(AT_H):
                    for j in range(tt + 1):
                        last = pe.matmul(bank(f"ao{tt}")[:, AT_V * h:AT_V * h + AT_V], AT[:, 3 * h + tt + j, :],
                                         AV[:, j, AT_V * h:AT_V * h + AT_V], start=(j == 0), stop=(j == tt))
                last.then_inc(main_done, 1)
            pe.wait_ge(att_y, 1)
            transposes("att", tiles(AOUT, 4))
            t_read_all(pe, "att", 2)
            names = [f"wm{i}" for i in range(4)]
            raw_panel(names, [RAW2, RAW2 + 1], [MIXA[:, k] for k in range(4)])
            pe.wait_ge(ssm_y, 1)
            transposes("ssm", tiles(XS, NK))
            new_stream("ssm")
            wide_panel(names, S_WM, range(NK), start=False)
            transposes("ffb", tiles(XN2, NK), norm=4)
            new_stream("ffb")
            feed_forward(S_FFB, NF, [f"fb{i}" for i in range(4)])

        @block.scalar
        def _(act):
            steps = [0]
            parts = [0]

            def split_to(p):
                for q in range(parts[0], p + 1):
                    round_part(act, q)
                parts[0] = max(parts[0], p + 1)

            def limit(p):
                for end in (S_PRE, S_WM, S_END):
                    if p < end:
                        return min(p + 2, end - 1)

            def take(name):
                split_to(limit(USE_PART[name]))
                act.wait_ge(main_done, MAIN_AT[name] + 1)
                return bank(name)

            def after(name):
                split_to(limit(USE_PART[name]))
                read_out(act, name)

            def turned_pair(stage, j):
                split_to(limit(T_PART[stage]))
                act.wait_ge(t_done, T_AT[stage] + j + 1)

            def link(ins):
                steps[0] += 1
                ins.then_inc(act_step, 1)
                act.wait_ge(act_step, steps[0])

            def read_done(ins):
                ins.then_inc(main_read["act"], 1)

            def norm_stats(i, parts, arrive=None):
                for n, part in enumerate(parts):
                    if arrive:
                        arrive[n]()
                    w = part.shape[-1]
                    act.activation(XN.rearrange("p t d -> p (t d)")[:, w * n:w * n + w], part, ACT.Square,
                                   accum_out=nst[:, i % 2, n:n + 1]).then_inc(norm_sq, 1)
                act.wait_ge(norm_ms, i + 1)
                act.activation(nst[:, i % 2, 6:8], nst[:, i % 2, 4:6], ACT.Sqrt).then_inc(norm_sd, 1)

            def warm_root(i):
                act.activation(warm[:, i:i + 1], ident[:, 0:1], ACT.Sqrt)

            def head_root(i, n):
                act.wait_ge(head_ms, i + 1)
                act.activation(hst[:, i % 2, 1, 0:n], hst[:, i % 2, 0, 0:n], ACT.Sqrt).then_inc(head_sd, 1)

            def turned(stage, pairs, dst, gain=None):
                for j in t_mine(1, stage, pairs):
                    turned_pair(stage, j)
                    for q in range(2):
                        k = 2 * j + q
                        last = act.activation(dst[:, k, :], t_bank(stage, j)[:, T * q:T * q + T], ACT.Copy,
                                              scale=1.0 if gain is None else gain(k))
                    last.then_inc(t_read[1], 1)

            def stream_hi(stage):
                c0, gain = STREAMS[stage]
                for j in range(dict(TSTAGES)[stage]):
                    turned_pair(stage, j)
                    for q in range(2):
                        k = 2 * j + q
                        last = act.activation(XTh[:, c0 + k, :], t_bank(stage, j)[:, T * q:T * q + T], ACT.Copy,
                                              scale=col(gain, k) if gain else 1.0)
                    last.then_inc(xt_hi, 1)

            act.dma_start(WG[0:LOWR + 1, :], w_gate_up).then_inc(consts_in, 16)
            act.dma_start(KS, k12).then_inc(consts_in, 16)
            act.dma_start(LNG, row_ln[0:1, :].broadcast_to([P, 512])).then_inc(rows_in, 16)
            act.dma_start(LNB, row_ln[1:2, :].broadcast_to([P, 512])).then_inc(rows_in, 16)
            act.dma_start(WS, w_sgu).then_inc(rows_in, 16)

            act.wait_ge(pool_const, 6)
            warm_root(0)
            norm_stats(0, [X[:, tt, :] for tt in range(NT)], [lambda tt=tt: act.wait_ge(x_in[tt], 16) for tt in range(NT)])
            act.wait_ge(cols_in, 16)
            stream_hi("n1")
            split_to(6)
            act.wait_ge(gla_abs, 1)
            link(act.activation(ZA, ZA, ACT.Exp, scale=-1.0))
            act.activation(ZA, ZA, ACT.Ln, bias=1.0).then_inc(gla_ln, 1)
            act.wait_ge(gla_l, 1)
            for tt in range(NT):
                b = take(f"d{tt}")
                read_done(act.activation(ZA[:, tt, :], b, ACT.Exp, scale=1.0 / GLA_TAU))
            b = take("tot")
            read_done(act.activation(DEC, b[:, 0:16], ACT.Exp, scale=1.0 / GLA_TAU))
            for tt in range(NT):
                b = take(f"r{tt}")
                read_done(act.activation(R[:, tt, :], b, ACT.Silu))
            for name, dst in (("su", SU), ("sv", SV)):
                for tt in range(NT):
                    b = take(f"{name}{tt}")
                    read_done(act.activation(dst[:, tt, :], b, ACT.Gelu_apprx_tanh))
            head_root(0, NT)
            split_to(28)
            head_root(1, 8)
            for name, dst in (("ga", GA), ("gb", GB)):
                for hf in range(2):
                    for tt in range(NT):
                        b = take(f"{name}{hf}{tt}")
                        read_done(act.activation(dst[:, tt, 512 * hf:512 * hf + 512], b, ACT.Sigmoid))
            stream_hi("ya")
            stream_hi("yb")
            stream_hi("mg")
            split_to(S_WQ + 1)
            tiles = [X[:, tt, :] for tt in range(NT)]
            norm_stats(1, tiles, [lambda: read_out(act, "ho2"), lambda: read_out(act, "ho3")])
            stream_hi("n2")
            for h in range(PEER_H + 1):
                if h < PEER_H:
                    b = take(f"wq{h}")
                    read_done(act.activation(QP[:, 2 * h:2 * h + 2, :], b.rearrange("p (c t) -> p c t", c=2),
                                             ACT.Copy))
                if h:
                    b = take(f"sc{h - 1}")
                    read_done(act.activation(SC[:, 2 * h - 2:2 * h].rearrange("p a t k -> p (a t k)"), b, ACT.Copy))
            def early_gelu(n, b):
                act.wait_ge(h_done, n + 1)
                act.activation(G[:, n, :], ps[:, 4 + b, 0:T], ACT.Gelu_apprx_tanh).then_inc(gelu_done, 1)

            for n in range(UN):
                split_to(S_EXP + n + 2)
                early_gelu(n, n % 2)
            with act.Fori(1, EARLY // UN - 1, 1) as i:
                for s in range(UN):
                    n, p = i * UN + s, S_EXP + s + 2
                    act.wait_ge(slot_ready[item_of(p) % RING], i * 16 + 16 * (item_of(p) // RING + 1))
                    act.wait_ge(h_done, n)
                    act.activation(whi[:, p % NBUF, :], half(item_of(p), p % 2), ACT.Copy).then_inc(part_hi, 1)
                    early_gelu(n, s % 2)
            parts[0] = S_PRE - UN + 2
            for n in range(EARLY - UN, EARLY):
                split_to(min(S_EXP + n + 2, S_PRE - 1))
                early_gelu(n, n % 2)
            split_to(S_PRE)
            act.wait_ge(top_shift, 1)
            act.activation(GS, GS, ACT.Exp).then_inc(top_exp, 1)
            turned_pair("idx", 1)
            act.activation(gT, t_bank("idx", 1)[:, 0:T], ACT.Copy).then_inc(t_read[1], 1)

            t_read_wait(act, T_AT["idx"] + 1)

            def gate_scale(g, b):
                act.wait_ge(hot_ready, g + 1)
                for j in range(BY_ACT):
                    last = act.activation(ONE2[:, b, j, :], HOT2[:, b, j, :], ACT.Copy,
                                          scale=gT[:, bass.ds(g * ONES + j, 1)])
                last.then_inc(one_scaled, 1)

            def gate_copy(g, b):
                act.wait_ge(gate_mm, g + 1)
                src = ps[:, 4 + 2 * b:6 + 2 * b, :].rearrange("p k (j c) -> p c (k j)", j=4)
                act.activation(G[:, EARLY:, bass.ds(g * ONES, ONES)], src[:, EARLY:], ACT.Copy).then_inc(gate_out, 1)

            act.wait_ge(part_lo, S_PRE)
            gate_scale(0, 0)
            gate_scale(1, 1)
            gate_copy(0, 0)
            with act.Fori(1, T // (2 * ONES), 1) as pair:
                g = pair * 2
                for b in range(2):
                    gate_scale(g + b, b)
                    gate_copy(g + (b - 1), 1 - b)
            gate_copy(T // ONES - 1, 1)

            def expert_gelu(n, b):
                act.wait_ge(h_done, n + 1)
                act.wait_ge(a_ready, n - 1)
                act.activation(HID[:, b, :], ps[:, 4 + b, 0:T], ACT.Gelu_apprx_tanh).then_inc(gelu_done, 1)

            split_to(S_PRE + UN - 1)
            with act.Fori(1, EARLY // UN, 1) as i:
                for s in range(UN):
                    n, p = i * UN + s, S_PRE + s
                    act.wait_ge(slot_ready[item_of(p) % RING], i * 16 + 16 * (item_of(p) // RING + 1))
                    act.wait_ge(a_used, n - 2)
                    act.activation(whi[:, p % NBUF, :], half(item_of(p), p % 2), ACT.Copy).then_inc(part_hi, 1)
            parts[0] = S_LATE
            for n in range(EARLY, EARLY + UN):
                split_to(S_EXP + 3 + 2 * n)
                expert_gelu(n, n % 2)
            with act.Fori(1, (P - 2 - EARLY) // UN, 1) as i:
                for s in range(UN):
                    n, p = i * UN + (EARLY + s), S_LATE + 2 + 2 * s
                    act.wait_ge(slot_ready[item_of(p) % RING], i * (2 * 16) + 16 * (item_of(p) // RING + 1))
                    act.wait_ge(a_used, n - 1)
                    act.activation(whi[:, p % NBUF, :], half(item_of(p), 0), ACT.Copy).then_inc(part_hi, 1)
                    act.wait_ge(h_done, n + 2)
                    act.activation(whi[:, (p + 1) % NBUF, :], half(item_of(p), 1), ACT.Copy).then_inc(part_hi, 1)
                    expert_gelu(n, s % 2)
            parts[0] = S_EXP + 2 * P - 2
            split_to(S_EXP + 2 * P - 2)
            expert_gelu(P - 2, 0)
            split_to(S_EXP + 2 * P - 1)
            expert_gelu(P - 1, 1)
            split_to(S_FFA + 1)
            warm_root(1)
            norm_stats(2, tiles, [lambda: read_out(act, "ex1"), lambda: read_out(act, "ex3")])
            norm_stats(3, tiles, [lambda: act.wait_ge(x_half, 1), lambda: act.wait_ge(x_new, 3)])
            act.dma_start(PG, row_post[1:2, :].broadcast_to([P, D])).then_inc(post_in, 16)
            act.dma_start(WD, w_dt).then_inc(mix_in, 16)
            act.dma_start(SMALL, row_small.rearrange("(o a) n -> o a n", o=1).broadcast_to([P, 3, SSM_H]))\
               .then_inc(mix_in, 16)
            act.dma_start(LAM, row_lam.rearrange("(o a) n -> o a n", o=1).broadcast_to([P, 4, AT_D]))\
               .then_inc(mix_in, 16)
            stream_hi("ffa")

            def feed_forward(s0, base):
                def silu(f, b, wait_read=True):
                    act.wait_ge(gu_done, f + (base + 1))
                    if wait_read:
                        act.wait_ge(fa_ready, f + (base - 1))
                    act.activation(HID[:, b, :], ps[:, 4 + b, 0:T], ACT.Silu).then_inc(silu_done, 1)

                used = NF - 1 if base else 0
                counted = FFB_COUNT if base else FFA_COUNT
                split_to(s0 + 4)
                silu(0, 0, wait_read=False)
                split_to(s0 + 7)
                silu(1, 1, wait_read=False)
                with act.Fori(1, NF // 2 - 1, 1) as i:
                    for s in range(2):
                        f, p = i * 2 + s, s0 + 2 + 3 * s
                        for j in range(3):
                            q = p + j
                            act.wait_ge(slot_ready[item_of(q) % RING], i * 16 + 16 * (item_of(q) // RING + 1))
                            if j == 0:
                                act.wait_ge(part_used, f + (counted + 1))
                            elif j == 1:
                                act.wait_ge(gu_done, f + (base + 1))
                            else:
                                act.wait_ge(fa_used, f + used)
                            act.activation(whi[:, q % NBUF, :], half(item_of(q), q % 2), ACT.Copy)\
                               .then_inc(part_hi, 1)
                        silu(f, s)
                parts[0] = s0 + 3 * NF - 4
                split_to(s0 + 3 * NF - 2)
                silu(NF - 2, 0)
                split_to(s0 + 3 * NF - 1)
                silu(NF - 1, 1)
                if not base:
                    split_to(S_MIX + 1)

            feed_forward(S_FFA, 0)
            products_of = lambda name: ([bank(f"{name}{i}") for i in range(4)],
                                        [lambda i=i: take(f"{name}{i}") for i in range(4)])
            warm_root(2)
            norm_stats(4, *products_of("fa"))
            norm_stats(5, tiles, [lambda: act.wait_ge(x_half, 2), lambda: act.wait_ge(x_new, 4)])
            act.dma_start(PG, row_post[2:3, :].broadcast_to([P, D])).then_inc(post_in, 16)
            stream_hi("mix")
            act.wait_ge(dt_abs, 1)
            link(act.activation(DU, DU, ACT.Exp, scale=-1.0))
            act.activation(DU, DU, ACT.Ln, bias=1.0)
            act.activation(SMALL[:, 1, :], SMALL[:, 1, :], ACT.Exp).then_inc(dt_ln, 1)
            act.wait_ge(lam_sum, 1)
            act.activation(LS[:, 2:4], LS[:, 0:2], ACT.Exp).then_inc(lam_exp, 1)
            for tt in range(NT):
                b = take(f"av{tt}")
                read_done(act.activation(AV[:, tt, :], b, ACT.Copy))

            split_to(S_XB + 3)
            act.wait_ge(att_max, 1)
            for i in range(16):
                if i % 3 == 2:
                    split_to(min(parts[0], S_XB + 7))
                r, g = i // 4, i % 4
                for tt, seg in enumerate((slice(0, P), slice(P, 384))):
                    last = act.activation(PR[:, r, g, seg], PR[:, r, g, seg], ACT.Exp, bias=AMAX[:, i, tt:tt + 1],
                                          accum_out=ASUM[:, i, tt:tt + 1])
            last.then_inc(att_exp, 1)
            act.wait_ge(pool_const2, 3)
            for i in range(0, 6, 2):
                b = take(f"xb{i}")
                read_done(act.activation(XRAW[:, 2 * i:2 * i + 2, CONVW - 1:], b.rearrange("p (c t) -> p c t", c=2),
                                         ACT.Copy))
            for j in range(2):
                for tt in range(NT):
                    b = take(f"zz{2 * j + tt}")
                    read_done(act.activation(Z[:, tt, 512 * j:512 * j + 512], b, ACT.Silu))
            act.wait_ge(conv_out, 1)
            act.activation(XBC[:, 0:8, :], XBC[:, 0:8, :], ACT.Silu).then_inc(conv_silu, 1)
            act.wait_ge(conv_out, 2)
            act.activation(XBC[:, 8:12, :], XBC[:, 8:12, :], ACT.Silu).then_inc(conv_silu, 1)
            def to_tokens(j):
                turned_pair("xs", j)
                b = t_bank("xs", j).rearrange("p (k t n) -> p t k n", k=2, t=NT)
                dst = XS[:, :, T * j:T * j + T].rearrange("p t (k n) -> p t k n", k=2)
                act.activation(dst, b, ACT.Copy).then_inc(t_read[1], 1)

            for j in t_mine(1, "xs", 4):
                to_tokens(j)
            for j in t_mine(1, "bm", 1):
                turned_pair("bm", 0)
                act.activation(BM, t_bank("bm", 0)[:, 0:2 * P].rearrange("p (g n) -> p g n", g=2), ACT.Copy)\
                   .then_inc(t_read[1], 1)
            b = take("cum")
            read_done(act.activation(ECUM, b[:, 0:3 * SSM_H].rearrange("p (a h) -> p a h", a=3), ACT.Exp))

            def decays(c):
                for q in range(4):
                    b = take(f"ss{4 * c + q}")
                    read_done(act.activation(W[c][:, 4 * q:4 * q + 4, :], b.rearrange("p (j l) -> p j l", j=4),
                                             ACT.Exp))

            decays(0)
            for j in t_mine(1, "pt", 6):
                turned_pair("pt", j)
                act.activation(AT[:, 4 * j:4 * j + 4, :], t_bank("pt", j).rearrange("p (a q) -> p a q", a=4),
                               ACT.Copy).then_inc(t_read[1], 1)
            decays(1)
            for g in range(2):
                b = take(f"st{g}")
                read_done(act.activation(SSTATE[:, g, :], b, ACT.Copy))
            for tt in range(NT):
                act.wait_ge(ssm_gated, tt + 1)
                for g in range(2):
                    c = slice(512 * g, 512 * g + 512)
                    last = act.activation(SSQ[:, tt, c], XS[:, tt, c], ACT.Square,
                                          accum_out=hst[:, 3 % 2, 0, 2 * tt + g:2 * tt + g + 1])
            last.then_inc(ssm_sq, 1)
            head_root(2, 16)
            turned("att", 2, MIXA, lambda k: col("subln"))
            head_root(3, 4)
            stream_hi("ssm")
            norm_stats(6, *products_of("wm"))
            norm_stats(7, tiles, [lambda: act.wait_ge(x_half, 3), lambda: act.wait_ge(x_new, 5)])
            act.dma_start(PG, row_post[3:4, :].broadcast_to([P, D])).then_inc(post_in, 16)
            stream_hi("ffb")
            feed_forward(S_FFB, NF)
            warm_root(3)
            norm_stats(8, *products_of("fb"))

        @block.vector
        def _(dve):
            steps = [0]
            parts = [0]

            def split_to(p):
                for q in range(parts[0], p + 1):
                    if not (S_WQ <= q < S_PRE or S_ZZ <= q < S_WM):
                        rest_part(dve, q)
                parts[0] = max(parts[0], p + 1)

            def limit(p):
                for end in (S_PRE, S_WM, S_END):
                    if p < end:
                        return min(p + 2, end - 1)

            def take(name):
                split_to(limit(USE_PART[name]))
                dve.wait_ge(main_done, MAIN_AT[name] + 1)
                return bank(name)

            def after(name):
                split_to(limit(USE_PART[name]))
                read_out(dve, name)

            def turned_pair(stage, j):
                split_to(limit(T_PART[stage]))
                dve.wait_ge(t_done, T_AT[stage] + j + 1)

            def link(ins):
                steps[0] += 1
                ins.then_inc(dve_step, 1)
                dve.wait_ge(dve_step, steps[0])

            def read_done(ins):
                ins.then_inc(main_read["dve"], 1)

            def norm_mean(i, parts):
                dve.wait_ge(norm_sq, sum(NORM_PARTS[:i + 1]))
                src = nst[:, i % 2, 0:2]
                if parts == 4:
                    s = nst[:, i % 2, 0:4].rearrange("p (t h) -> p t h", t=2)
                    src = nst[:, i % 2, 4:6]
                    link(dve.tensor_tensor(src, s[:, :, 0], s[:, :, 1], ALU.add))
                dve.tensor_scalar(nst[:, i % 2, 4:6], src, 1.0 / D, EPS, ALU.mult, ALU.add).then_inc(norm_ms, 1)

            def norm_root(i, gain=1.0):
                dve.wait_ge(norm_sd, i + 1)
                link(dve.reciprocal(nst[:, i % 2, 8:10], nst[:, i % 2, 6:8]))
                if gain != 1.0:
                    link(dve.tensor_scalar(nst[:, i % 2, 8:10], nst[:, i % 2, 8:10], gain, None, ALU.mult))

            def pre_norm(i, dst):
                norm_mean(i, 2)
                norm_root(i)
                for tt in range(NT):
                    last = dve.tensor_scalar(dst[:, tt, :], X[:, tt, :], nst[:, i % 2, 8 + tt:9 + tt], None, ALU.mult)
                    last.then_inc(norm_out, 1)

            def post_norm(i, names, gain, loads):
                dve.wait_ge(post_in, 16 * loads)
                for n, name in enumerate(names):
                    tt, hf = n // 2, n % 2
                    take(name)
                    dve.wait_ge(norm_sq, sum(NORM_PARTS[:i]) + n + 1)
                    if n == len(names) - 1:
                        norm_mean(i, 4)
                    read_done(dve.tensor_tensor(XN2[:, tt, 512 * hf:512 * hf + 512], bank(name),
                                                PG[:, 512 * hf:512 * hf + 512], ALU.mult))
                norm_root(i, gain)
                dve.wait_ge(main_read["dve"], reads_upto(MAIN_AT[names[-1]], "dve"))
                for tt, done in enumerate((x_half, x_new)):
                    dve.scalar_tensor_tensor(X[:, tt, :], XN2[:, tt, :], nst[:, i % 2, 8 + tt:9 + tt], X[:, tt, :],
                                             ALU.mult, ALU.add).then_inc(done, 1)

            def head_scale(i, n, width, gain=1.0):
                dve.tensor_scalar(hst[:, i % 2, 0, 0:n], hst[:, i % 2, 0, 0:n], 1.0 / width, EPS, ALU.mult, ALU.add)\
                   .then_inc(head_ms, 1)
                dve.wait_ge(head_sd, i + 1)
                link(dve.reciprocal(hst[:, i % 2, 1, 0:n], hst[:, i % 2, 1, 0:n]))
                if gain != 1.0:
                    link(dve.tensor_scalar(hst[:, i % 2, 1, 0:n], hst[:, i % 2, 1, 0:n], gain, None, ALU.mult))
                return hst[:, i % 2, 1, 0:n]

            def turned(stage, pairs, dst, gain=None):
                for j in t_mine(0, stage, pairs):
                    turned_pair(stage, j)
                    for q in range(2):
                        k = 2 * j + q
                        src = t_bank(stage, j)[:, T * q:T * q + T]
                        if gain is None:
                            last = dve.tensor_copy(dst[:, k, :], src)
                        else:
                            last = dve.tensor_scalar(dst[:, k, :], src, gain(k), None, ALU.mult)
                    last.then_inc(t_read[0], 1)

            def stream_lo(stage):
                c0, gain = STREAMS[stage]
                for j in range(dict(TSTAGES)[stage]):
                    turned_pair(stage, j)
                    dve.wait_ge(xt_hi, STREAM_AT[stage] + j + 1)
                    for q in range(2):
                        k = 2 * j + q
                        last = dve.scalar_tensor_tensor(XTl[:, c0 + k, :], t_bank(stage, j)[:, T * q:T * q + T],
                                                        col(gain, k) if gain else 1.0,
                                                        XTh[:, c0 + k, :].bitcast(f32), ALU.mult, ALU.subtract)
                    last.then_inc(xt_lo, 1)
                    k = c0 + 2 * j
                    dve.tensor_copy(XTb[:, k:k + 2, :], XTh[:, k:k + 2, :].bitcast(f32)).then_inc(xt_b, 1)

            for tt in range(NT):
                dve.wait_ge(x_in[tt], 16)
            pre_norm(0, XN)
            dve.wait_ge(cols_in, 16)
            stream_lo("n1")
            dve.wait_ge(pool_const, 5)
            b = take("alr")
            read_done(dve.tensor_copy(ALR[0:LOWR, :], b[0:LOWR, 0:T]))
            for j in range(2):
                b = take(f"q{j}")
                read_done(dve.tensor_scalar(QT[:, 2 * j:2 * j + 2, :], b.rearrange("p (c t) -> p c t", c=2),
                                            float(P) ** -0.5, None, ALU.mult))
            for tt in range(NT):
                b = take(f"z{tt}")
                link(dve.tensor_scalar(L[:, tt, :], b, 0.0, None, ALU.min))
                read_done(dve.scalar_tensor_tensor(ZA[:, tt, :], L[:, tt, :], -2.0, b, ALU.mult, ALU.add))
            after("z1")
            dve.sem_inc(gla_abs, 1)
            for name, dst in (("k", Kk), ("v", V)):
                for tt in range(NT):
                    if name == "k" and tt == 0:
                        split_to(6)
                        dve.wait_ge(gla_ln, 1)
                        dve.tensor_tensor(L, L, ZA, ALU.subtract).then_inc(gla_l, 1)
                    b = take(f"{name}{tt}")
                    read_done(dve.tensor_copy(dst[:, tt, :], b))
            after("d1")
            after("k1")
            dve.tensor_tensor(Kk, Kk, ZA, ALU.mult).then_inc(gla_kd, 1)
            after("tot")
            for n in range(4):
                b = take(f"kv{n}")
                if n == 0:
                    ins = dve.tensor_copy(ST[:, 0], b.rearrange("p (h v) -> p h v", h=GLA_H))
                else:
                    for h in range(GLA_H):
                        c = 2 * (GLA_H * (n // 2) + h) + n % 2
                        ins = dve.scalar_tensor_tensor(ST[:, n, h, :], ST[:, n - 1, h, :], DEC[:, c:c + 1],
                                                       b[:, P * h:P * h + P], ALU.mult, ALU.add)
                read_done(ins)
                after(f"kv{n}")
            dve.sem_inc(gla_state, 1)
            for tt in range(NT):
                for j, name in enumerate((f"oe{tt}", f"oo{tt}")):
                    b = take(name)
                    rows = slice(CH * j, CH * j + CH)
                    read_done(dve.tensor_copy(O[rows, tt, :], b[rows, :]))
            dve.wait_ge(rows_in, 16 * 3)
            after("sv1")
            for tt in range(NT):
                ins = dve.bn_stats(BNS[:, tt, :], SV[:, tt, :])
            link(ins)
            for tt in range(NT):
                ins = dve.bn_aggr(MV[:, tt, :], BNS[:, tt, :])
            link(ins)
            link(dve.tensor_copy(hst[:, 0 % 2, 0, 0:NT], MV[:, :, 1]))
            rs = head_scale(0, NT, 1.0)
            split_to(26)
            for tt in range(NT):
                ins = dve.tensor_scalar(SV[:, tt, :], SV[:, tt, :], MV[:, tt, 0:1], rs[:, tt:tt + 1], ALU.subtract,
                                        ALU.mult)
            link(ins)
            link(dve.tensor_tensor(SV, SV, LNG.unsqueeze(1).broadcast_to([P, NT, 512]), ALU.mult))
            dve.tensor_tensor(SV, SV, LNB.unsqueeze(1).broadcast_to([P, NT, 512]), ALU.add).then_inc(vn_ready, 1)
            split_to(27)
            after("oo1")
            link(dve.tensor_tensor(OSQ, O, O, ALU.mult))
            split_to(28)
            link(dve.tensor_reduce(hst[:, 1 % 2, 0, 0:8], OSQ.rearrange("p t (h v) -> p (t h) v", h=GLA_H), AX, ALU.add))
            rs = head_scale(1, 8, P)
            o8 = O.rearrange("p t (h v) -> p (t h) v", h=GLA_H)
            link(dve.tensor_tensor(o8, o8, rs.unsqueeze(2).broadcast_to([P, 8, P]), ALU.mult))
            dve.tensor_tensor(O, O, R, ALU.mult).then_inc(ya_ready, 1)
            for tt in range(NT):
                b = take(f"mx{tt}")
                for g in range(4):
                    ins = dve.scalar_tensor_tensor(SU[:, tt, P * g:P * g + P], b[:, P * g:P * g + P],
                                                   col("sgub", g), SU[:, tt, P * g:P * g + P], ALU.add, ALU.mult)
                read_done(ins)
            after("mx1")
            dve.sem_inc(yb_ready, 1)
            stream_lo("ya")
            for name, gate in (("pa", GA), ("pb", GB)):
                for i in range(4):
                    tt, hf = i // 2, i % 2
                    b = take(f"{name}{i}")
                    g = gate[:, tt, 512 * hf:512 * hf + 512]
                    if i == 0:
                        after("ga11" if name == "pa" else "gb11")
                    read_done(dve.tensor_tensor(g, g, b, ALU.mult))
                if name == "pa":
                    stream_lo("yb")
            stream_lo("mg")
            for i in range(4):
                hf, tt = i // 2, i % 2
                b = take(f"ho{i}")
                xp = X[:, tt, 512 * hf:512 * hf + 512]
                read_done(dve.tensor_tensor(xp, xp, b, ALU.add))
            after("ho3")
            dve.sem_inc(x_new, 1)
            pre_norm(1, XN)
            stream_lo("n2")
            def top16(rows, values, indices):
                n = len(rows)
                for k in range(n):
                    ins = dve.max(values[k][:, 0:8], rows[k])
                link(ins)
                for k in range(n):
                    ins = dve.max_index(indices[k][:, 0:8], values[k][:, 0:8], rows[k])
                link(ins)
                for k in range(n):
                    ins = dve.match_replace(rows[k], values[k][:, 0:8], rows[k], NEG)
                link(ins)
                for k in range(n):
                    ins = dve.max(values[k][:, 8:16], rows[k])
                link(ins)
                for k in range(n):
                    ins = dve.max_index(indices[k][:, 8:16], values[k][:, 8:16], rows[k])
                link(ins)

            sq = [P, TOPK, TOPK]
            for h in range(PEER_H):
                after(f"sc{h}")
                rows = [(tt, 2 * h + a) for a in range(2) for tt in range(NT)]
                top16([SC[:, hp, tt, :] for tt, hp in rows], [VAL[:, tt, hp, :] for tt, hp in rows],
                      [IDX[:, tt, hp, :] for tt, hp in rows])
                for tt in range(NT):
                    ins = dve.tensor_tensor(CAND[:, tt, h, :].rearrange("p (a b) -> p a b", a=TOPK),
                                            VAL[:, tt, 2 * h, :].unsqueeze(2).broadcast_to(sq),
                                            VAL[:, tt, 2 * h + 1, :].unsqueeze(1).broadcast_to(sq), ALU.add)
                link(ins)
                ranks = slice(TOPK * h, TOPK * h + TOPK)
                top16([CAND[:, tt, h, :] for tt in range(NT)], [BEST[:, tt, ranks] for tt in range(NT)],
                      [CI[:, tt, ranks] for tt in range(NT)])
            link(dve.tensor_copy(IDF, IDX))
            best = BEST.rearrange("p t (h k) -> p (t h) k", h=PEER_H)
            gs = GS.rearrange("p t (h k) -> p (t h) k", h=PEER_H)
            dve.tensor_tensor(gs, best, best[:, :, 0:1].broadcast_to([P, NT * PEER_H, TOPK]), ALU.subtract)\
               .then_inc(top_shift, 1)
            dve.tensor_scalar(CIA, CI, 4, None, ALU.logical_shift_right)
            link(dve.tensor_scalar(CI, CI, 15, None, ALU.bitwise_and))
            dve.tensor_copy(IA, CIA)
            link(dve.tensor_copy(IB, CI))
            ranks3 = [P, NT * PEER_H, TOPK]
            for side, (rank, dst) in enumerate(((IA, I1S), (IB, I2S))):
                rank = rank.rearrange("p t (h k) -> p (t h) k", h=PEER_H)
                idf = IDF.rearrange("p t (h s) k -> p (t h) s k", s=2)[:, :, side, :]
                for j in range(TOPK):
                    ins = dve.scalar_tensor_tensor(PICK[:, j, :].rearrange("p (n k) -> p n k", k=TOPK), rank, float(j),
                                                   idf[:, :, j:j + 1].broadcast_to(ranks3), ALU.is_equal, ALU.mult)
                link(ins)
                for n in (8, 4, 2):
                    link(dve.tensor_tensor(PICK[:, 0:n, :], PICK[:, 0:n, :], PICK[:, n:2 * n, :], ALU.add))
                link(dve.tensor_tensor(dst.rearrange("p t k -> p (t k)"), PICK[:, 0, :], PICK[:, 1, :], ALU.add))
            dve.wait_ge(top_exp, 1)
            pst = PST.rearrange("p t h -> p (t h)")
            link(dve.tensor_reduce(pst, gs, AX, ALU.add))
            link(dve.reciprocal(pst, pst))
            dve.tensor_tensor(gs, gs, pst.unsqueeze(2).broadcast_to([P, NT * PEER_H, TOPK]), ALU.mult)\
               .then_inc(sel_ready, 1)
            dve.wait_ge(gelu_done, EARLY)
            split_to(S_PRE)
            turned_pair("idx", 0)
            dve.tensor_copy(i1T, t_bank("idx", 0)[:, 0:T])
            link(dve.tensor_copy(i2T, t_bank("idx", 0)[:, T:2 * T]))
            dve.sem_inc(t_read[0], 1)
            t_read_wait(dve, T_AT["idx"] + 1)

            def gate_times(g, b):
                dve.wait_ge(gate_out, g + 1)
                src = ps[:, 4 + 2 * b:6 + 2 * b, :].rearrange("p k (j c) -> p c (k j)", j=4)[:, 0:EARLY]
                early = G[:, 0:EARLY, bass.ds(g * ONES, ONES)]
                dve.tensor_tensor(early, early, src, ALU.mult).then_inc(gate_mul, 1)

            def one_hots(g, b, first=False):
                def hots(out, idx, n):
                    shape = [P, n, P]
                    return dve.tensor_tensor(out, iota[:, :].unsqueeze(1).broadcast_to(shape),
                                             idx[:, bass.ds(g * ONES, n)].unsqueeze(2).broadcast_to(shape),
                                             ALU.is_equal)

                hots(HOT2[:, b, 0:BY_ACT, :], i2T, BY_ACT).then_inc(hot_ready, 1)
                hots(ONE1[:, b], i1T, ONES)
                if not first:
                    gate_times(g + (-2), b)
                for j in range(BY_ACT, ONES):
                    t1 = bass.ds(g * ONES + j, 1)
                    ins = dve.tensor_scalar(ONE2[:, b, j, :], iota[:, :], i2T[:, t1], gT[:, t1], ALU.is_equal,
                                            ALU.mult)
                ins.then_inc(one_ready, 1)

            for g in range(2):
                one_hots(g, g, first=True)
            with dve.Fori(1, T // (2 * ONES), 1) as pair:
                g = pair * 2
                for b in range(2):
                    dve.wait_ge(gate_mm, g + (b - 1))
                    one_hots(g + b, b)
            for b in range(2):
                gate_times(T // ONES - 2 + b, b)
            dve.wait_ge(gate_mul, T // ONES)

            def early_hidden(n, b, wait_used=True):
                if wait_used:
                    dve.wait_ge(a_used, n - 1)
                dve.tensor_copy(HAb[:, b, :], G[:, n, :])
                dve.tensor_copy(HAh[:, b, :], G[:, n, :]).then_inc(dve_hidden, 1)
                dve.wait_ge(dve_hidden, n + 1)
                dve.tensor_tensor(HAl[:, b, :], G[:, n, :], HAh[:, b, :].bitcast(f32), ALU.subtract).then_inc(a_ready, 1)

            for n in range(UN):
                early_hidden(n, n % 2, wait_used=(n >= 2))
                split_to(S_PRE + n + 1)
            with dve.Fori(1, EARLY // UN, 1) as i:
                for s in range(UN):
                    n, p = i * UN + s, S_PRE + s + 1
                    early_hidden(n, s % 2)
                    dve.wait_ge(part_hi, n + (S_PRE + 2))
                    dve.tensor_tensor(wlo[:, p % NBUF, :], half(item_of(p), p % 2), whi[:, p % NBUF, :].bitcast(f32),
                                      ALU.subtract).then_inc(part_lo, 1)
            parts[0] = S_LATE + 1

            def expert_gate(n, b):
                dve.wait_ge(gelu_done, n + 1)
                dve.wait_ge(a_ready, n)
                dve.tensor_tensor(HAf, HID[:, b, :], G[:, n, :], ALU.mult).then_inc(dve_hidden, 1)
                dve.wait_ge(dve_hidden, n * 2 + (1 - EARLY))
                dve.wait_ge(a_used, n - 1)
                dve.tensor_copy(HAb[:, b, :], HAf)
                dve.tensor_copy(HAh[:, b, :], HAf).then_inc(dve_hidden, 1)
                dve.wait_ge(dve_hidden, n * 2 + (2 - EARLY))
                dve.tensor_tensor(HAl[:, b, :], HAf, HAh[:, b, :].bitcast(f32), ALU.subtract).then_inc(a_ready, 1)

            for n in range(EARLY, EARLY + UN):
                split_to(S_EXP + 2 + 2 * n)
                expert_gate(n, n % 2)
                split_to(S_EXP + 3 + 2 * n)
            with dve.Fori(1, (P - 2 - EARLY) // UN, 1) as i:
                for s in range(UN):
                    n, p = i * UN + (EARLY + s), S_LATE + 2 + 2 * s
                    for j in range(2):
                        dve.wait_ge(part_hi, n * 2 + (S_EXP + 3 + j))
                        dve.tensor_tensor(wlo[:, (p + j) % NBUF, :], half(item_of(p), j),
                                          whi[:, (p + j) % NBUF, :].bitcast(f32), ALU.subtract).then_inc(part_lo, 1)
                        if j == 0:
                            expert_gate(n, s % 2)
            parts[0] = S_EXP + 2 * P - 2
            split_to(S_EXP + 2 * P - 2)
            expert_gate(P - 2, 0)
            split_to(S_EXP + 2 * P - 1)
            expert_gate(P - 1, 1)
            split_to(S_FFA + 1)
            for i in range(4):
                tt, hf = i // 2, i % 2
                b = take(f"ex{i}")
                xp = X[:, tt, 512 * hf:512 * hf + 512]
                read_done(dve.tensor_tensor(xp, xp, b, ALU.add))
            after("ex3")
            dve.sem_inc(x_new, 1)
            norm_mean(2, 2)
            norm_root(2)
            dve.wait_ge(final_in, 16)
            for tt, done in enumerate((x_half, x_new)):
                dve.scalar_tensor_tensor(X[:, tt, :], X[:, tt, :], nst[:, 2 % 2, 8 + tt:9 + tt], FG, ALU.mult,
                                         ALU.mult).then_inc(done, 1)
            dve.wait_ge(x_half, 1)
            dve.wait_ge(x_new, 3)

            def feed_forward(s0, base):
                used = NF - 1 if base else 0

                def times_up(f, b, wait_used=True):
                    dve.wait_ge(silu_done, f + (base + 1))
                    if wait_used or f or base:
                        dve.wait_ge(fa_ready, f + base)
                    dve.tensor_tensor(HAf, HID[:, b, :], ps[:, 4 + b, T:2 * T], ALU.mult).then_inc(dve_hidden, 1)
                    dve.wait_ge(dve_hidden, f * 2 + (2 * (P + base) - EARLY + 1))
                    if wait_used:
                        dve.wait_ge(fa_used, f + (used - 1))
                    dve.tensor_copy(HAb[:, b, :], HAf)
                    dve.tensor_copy(HAh[:, b, :], HAf).then_inc(dve_hidden, 1)
                    dve.wait_ge(dve_hidden, f * 2 + (2 * (P + base) - EARLY + 2))
                    dve.tensor_tensor(HAl[:, b, :], HAf, HAh[:, b, :].bitcast(f32), ALU.subtract)\
                       .then_inc(fa_ready, 1)

                split_to(s0 + 4)
                times_up(0, 0, wait_used=False)
                split_to(s0 + 7)
                times_up(1, 1, wait_used=False)
                with dve.Fori(1, NF // 2 - 1, 1) as i:
                    for s in range(2):
                        f, p = i * 2 + s, s0 + 2 + 3 * s
                        for j in range(3):
                            q = p + j
                            dve.wait_ge(part_hi, f * 3 + (s0 + 3 + j))
                            dve.tensor_tensor(wlo[:, q % NBUF, :], half(item_of(q), q % 2),
                                              whi[:, q % NBUF, :].bitcast(f32), ALU.subtract).then_inc(part_lo, 1)
                        times_up(f, s)
                parts[0] = s0 + 3 * NF - 4
                split_to(s0 + 3 * NF - 2)
                times_up(NF - 2, 0)
                split_to(s0 + 3 * NF - 1)
                times_up(NF - 1, 1)
                if not base:
                    split_to(S_MIX + 1)

            pre_norm(3, XN2)
            stream_lo("ffa")
            feed_forward(S_FFA, 0)
            post_norm(4, [f"fa{i}" for i in range(4)], 0.5, 1)
            dve.wait_ge(x_half, 2)
            dve.wait_ge(x_new, 4)
            pre_norm(5, XN2)
            stream_lo("mix")
            dve.wait_ge(mix_in, 16 * 3)
            b = take("dt")
            read_done(dve.tensor_tensor(DT, b[:, 0:2 * SSM_H].rearrange("p (t h) -> p t h", t=NT),
                                        SMALL[:, 0, :].unsqueeze(1).broadcast_to([P, NT, SSM_H]), ALU.add))
            after("dt")
            dve.scalar_tensor_tensor(DU, DT, -1.0, DT, ALU.mult, ALU.max).then_inc(dt_abs, 1)
            link(dve.tensor_scalar(DT, DT, 0.0, None, ALU.max))
            lam = LAM.rearrange("p (a b) n -> p a b n", a=2)
            link(dve.tensor_tensor(lam[:, :, 0, :], lam[:, :, 0, :], lam[:, :, 1, :], ALU.mult))
            dve.tensor_reduce(LS[:, 0:2], lam[:, :, 0, :], AX, ALU.add).then_inc(lam_sum, 1)
            dve.wait_ge(dt_ln, 1)
            link(dve.tensor_tensor(DT, DT, DU, ALU.add))
            ins = dve.scalar_tensor_tensor(AD, DT, -1.0, SMALL[:, 1, :].unsqueeze(1).broadcast_to([P, NT, SSM_H]),
                                           ALU.mult, ALU.mult)
            ins.then_inc(ad_ready, 1)
            dve.wait_ge(lam_exp, 1)
            link(dve.tensor_tensor(LS[:, 4:5], LS[:, 3:4], LS[:, 2:3], ALU.subtract))
            link(dve.tensor_scalar(LS[:, 5:6], LS[:, 4:5], -LAMBDA_INIT, None, ALU.add))
            for name, dst, scale in (("aq", AQ, float(AT_D) ** -0.5), ("ak", AK, 1.0)):
                for j in range(2):
                    b = take(f"{name}{j}")
                    read_done(dve.tensor_scalar(dst[:, 2 * j:2 * j + 2, :], b.rearrange("p (c t) -> p c t", c=2),
                                                scale, None, ALU.mult))
            dve.wait_ge(pool_const2, 9)
            for i in range(16):
                r, g = i // 4, i % 4
                h = 2 * r + g // 2
                b = take(f"at{i}")
                read_done(dve.scalar_tensor_tensor(PR[:, r, g, :], DB, 2.0 ** (-8.0 * (h + 1) / AT_H), b[:, 0:384],
                                                   ALU.mult, ALU.add))
            after("at15")
            pr = PR.rearrange("p r g n -> p (r g) n")
            dve.tensor_reduce(AMAX[:, :, 0], pr[:, :, 0:P], AX, ALU.max, negate=True)
            split_to(S_XB + 2)
            dve.tensor_reduce(AMAX[:, 0:8, 1], pr[:, 0:8, P:384], AX, ALU.max, negate=True)
            split_to(S_XB + 3)
            dve.tensor_reduce(AMAX[:, 8:16, 1], pr[:, 8:16, P:384], AX, ALU.max, negate=True).then_inc(att_max, 1)

            def normalise():
                dve.wait_ge(att_exp, 1)
                link(dve.reciprocal(ASUM, ASUM))
                second = ASUM.rearrange("p (h b) t -> p h b t", b=2)[:, :, 1, :]
                link(dve.tensor_scalar(second, second, LS[:, 5:6], None, ALU.mult))
                segs = (slice(0, P), slice(P, 384))
                split_to(S_XB + 10)
                for i in range(1, 16, 2):
                    for tt, seg in enumerate(segs):
                        p2 = PR[:, i // 4, i % 4, seg]
                        ins = dve.tensor_scalar(p2, p2, ASUM[:, i, tt:tt + 1], None, ALU.mult)
                link(ins)
                split_to(S_XB + 11)
                for i in range(0, 16, 2):
                    for tt, seg in enumerate(segs):
                        p1 = PR[:, i // 4, i % 4, seg]
                        ins = dve.scalar_tensor_tensor(p1, p1, ASUM[:, i, tt:tt + 1], PR[:, i // 4, i % 4 + 1, seg],
                                                       ALU.mult, ALU.add)
                ins.then_inc(att_a, 1)

            dve.wait_ge(pool_const2, 3)
            for i in range(1, 6, 2):
                if i == 5:
                    normalise()
                b = take(f"xb{i}")
                read_done(dve.tensor_copy(XRAW[:, 2 * i:2 * i + 2, CONVW - 1:], b.rearrange("p (c t) -> p c t", c=2)))
            after("xb4")
            after("xb5")
            for c in range(XC):
                ins = dve.tensor_scalar(XBC[:, c, :], XRAW[:, c, 0:T], col("convw", CONVW * c), col("convb", c),
                                        ALU.mult, ALU.add)
            link(ins)
            for w in range(1, CONVW):
                for c in range(XC):
                    ins = dve.scalar_tensor_tensor(XBC[:, c, :], XRAW[:, c, w:w + T], col("convw", CONVW * c + w),
                                                   XBC[:, c, :], ALU.mult, ALU.add)
                    if w == CONVW - 1 and c in (7, XC - 1):
                        ins.then_inc(conv_out, 1)
                if w < CONVW - 1:
                    link(ins)
            for j in t_mine(0, "xs", 4):
                turned_pair("xs", j)
                b = t_bank("xs", j).rearrange("p (k t n) -> p t k n", k=2, t=NT)
                dst = XS[:, :, T * j:T * j + T].rearrange("p t (k n) -> p t k n", k=2)
                dve.tensor_copy(dst, b).then_inc(t_read[0], 1)
            for j in t_mine(0, "bm", 1):
                turned_pair("bm", 0)
                dve.tensor_copy(BM, t_bank("bm", 0)[:, 0:2 * P].rearrange("p (g n) -> p g n", g=2))\
                   .then_inc(t_read[0], 1)
            b = take("cb")
            read_done(dve.tensor_tensor(CB, b.rearrange("p (a l) -> p a l", a=4),
                                        MLE.unsqueeze(1).broadcast_to([P, 4, P]), ALU.mult))
            after("cb")
            def weights(c):
                after(f"ss{4 * c + 3}")
                for g in range(2):
                    w = W[c][:, 8 * g:8 * g + 8, :]
                    dve.tensor_tensor(w, w, CB[:, 2 * c + g, :].unsqueeze(1).broadcast_to([P, 8, P]), ALU.mult)\
                       .then_inc(w_ready, 1)

            weights(0)
            for j in t_mine(0, "pt", 6):
                turned_pair("pt", j)
                dve.tensor_copy(AT[:, 4 * j:4 * j + 4, :], t_bank("pt", j).rearrange("p (a q) -> p a q", a=4))\
                   .then_inc(t_read[0], 1)
            weights(1)
            dve.wait_ge(xskip_ready, 2)
            for i in range(4):
                c, g = i // 2, i % 2
                b = take(f"yd{i}")
                y = XS[:, c, 512 * g:512 * g + 512]
                read_done(dve.tensor_tensor(y, y, b, ALU.add))
                if i == 1:
                    after("yd1")
                    dve.tensor_tensor(XS[:, 0, :], XS[:, 0, :], Z[:, 0, :], ALU.mult).then_inc(ssm_gated, 1)
            for g in range(2):
                b = take(f"yo{g}")
                e = ECUM[:, 1, 8 * g:8 * g + 8].unsqueeze(2).broadcast_to([P, 8, SSM_P])
                read_done(dve.tensor_tensor(YOFF[:, 512 * g:512 * g + 512].rearrange("p (h n) -> p h n", h=8),
                                            b.rearrange("p (h n) -> p h n", h=8), e, ALU.mult))
            after("yo1")
            link(dve.tensor_tensor(XS[:, 1, :], XS[:, 1, :], YOFF, ALU.add))
            dve.tensor_tensor(XS[:, 1, :], XS[:, 1, :], Z[:, 1, :], ALU.mult).then_inc(ssm_gated, 1)
            for tt in range(NT):
                b = take(f"ao{tt}")
                read_done(dve.tensor_copy(AOUT[:, tt, :], b))
            after("ao1")
            link(dve.tensor_tensor(ASQ, AOUT, AOUT, ALU.mult))
            link(dve.tensor_reduce(hst[:, 2 % 2, 0, 0:16], ASQ.rearrange("p t (h v) -> p (t h) v", h=AT_H), AX, ALU.add))
            rs = head_scale(2, 16, AT_V, 1.0 - LAMBDA_INIT)
            a16 = AOUT.rearrange("p t (h v) -> p (t h) v", h=AT_H)
            dve.tensor_tensor(a16, a16, rs.unsqueeze(2).broadcast_to([P, 16, AT_V]), ALU.mult).then_inc(att_y, 1)
            turned("att", 2, MIXA, lambda k: col("subln"))
            dve.wait_ge(ssm_sq, 1)
            rs = head_scale(3, 4, 512)
            y4 = XS.rearrange("p t (g n) -> p (t g) n", g=2)
            dve.tensor_tensor(y4, y4, rs.unsqueeze(2).broadcast_to([P, 4, 512]), ALU.mult).then_inc(ssm_y, 1)
            stream_lo("ssm")
            post_norm(6, [f"wm{i}" for i in range(4)], 1.0, 2)
            dve.wait_ge(x_half, 3)
            dve.wait_ge(x_new, 5)
            pre_norm(7, XN2)
            stream_lo("ffb")
            feed_forward(S_FFB, NF)
            post_norm(8, [f"fb{i}" for i in range(4)], 0.5, 3)


def kernel(**inputs):
    import numpy as np
    import concourse.bacc as bacc
    from concourse.bass_utils import run_bass_kernel_spmd as run

    a = {k: np.asarray(v) for k, v in inputs.items()}

    def items(parts):
        return parts.reshape(-1, 2, P, PART).transpose(0, 2, 1, 3).reshape(-1, P, ITEM)

    def tok(w):
        return items(w.reshape(4, 2, P, 512).transpose(0, 2, 1, 3).reshape(4, P, PART))

    def feat(w):
        return items(w.reshape(NK, P, 4, P).transpose(2, 1, 0, 3).reshape(4, P, PART))

    def wide(w):
        return items(w.reshape(4, P, D))

    def features(v, n):
        return v.reshape(n, P).T

    w_in = a["w_in"][0]
    at1 = {"q": 0, "k": 512, "v": 1024, "r": 1536, "su": 2064, "sv": 2576, "ga0": 3088, "ga1": 3600, "gb0": 4112,
           "gb1": 4624}
    p1 = [(feat if n == "q" else tok)(w_in[:, c:c + 512]) for n, c in at1.items()]
    p1 += [wide(a["w_branch_a"][0]), wide(a["w_branch_b"][0])]
    p1 += [tok(a["w_out"][0][:, 512 * j:512 * j + 512]) for j in range(2)]
    p1 += [feat(a["peer_wq"][0][:, 512 * j:512 * j + 512]) for j in range(4)]
    u = a["peer_u"][0].reshape(P, P, NK, P).transpose(1, 3, 2, 0).reshape(P, P, PART)
    v = a["peer_v"][0].reshape(P, P, D).transpose(1, 0, 2)
    between = np.stack([u[EARLY + 2:], v[EARLY:-2]], axis=1).reshape(-1, P, PART)
    experts = items(np.concatenate([u[:EARLY], v[:EARLY], u[EARLY:EARLY + 2], between, v[-2:]]))

    def ffn(n):
        gu = np.stack([a[f"ffn{n}_w_{w}_2"][0].reshape(NK, P, NF, P).transpose(2, 1, 0, 3).reshape(NF, P, PART)
                       for w in ("gate", "up")], axis=1)
        down = a[f"ffn{n}_w_down_2"][0].reshape(NF, 1, P, D)
        steps = np.concatenate([gu[1:], down[:-1]], axis=1).reshape(-1, P, PART)
        return items(np.concatenate([gu[0], steps, down[-1]]))

    w2 = a["w_in_2"][0]
    at2 = {"aq": 0, "ak": 512, "av": 1024, "xbc0": 2560, "xbc1": 3072, "xbc2": 3584, "z0": 1536, "z1": 2048}
    p2 = [(feat if n[0] in "xa" and n != "av" else tok)(w2[:, c:c + 512]) for n, c in at2.items()]
    p2 += [wide(a["w_out_2"][0][512 * j:512 * j + 512]) for j in range(3)]
    cols = np.concatenate([
        features(a["norm1_g"][0], 8), features(a["norm2_g"][0], 8), features(a["gla_norm_g"][0], 4),
        features(a["ffn1_pre_g_2"][0], 8), features(a["mix_pre_g_2"][0], 8), features(a["ffn2_pre_g_2"][0], 8),
        np.tile(a["attn_subln_g_2"][0], 2)[:, None], features(a["ssm_norm_g_2"][0], 8),
        a["conv_w_2"][0].reshape(CONVW, XC, P).transpose(2, 1, 0).reshape(P, -1),
        features(a["conv_b_2"][0], XC), a["sgu_b"][0].T], axis=1)
    arrays = {
        "x": a["x"], "panels1": np.concatenate(p1), "experts": experts, "ffa": ffn(1), "panels2": np.concatenate(p2),
        "ffb": ffn(2), "cols": cols,
        "w_low": w_in[:, 2048:2064].reshape(NK, P, LOWR).transpose(1, 0, 2),
        "w_gate_up": np.concatenate([a["w_gate_up"][0], a["b_gate"]]),
        "w_sgu": a["sgu_w"][0].transpose(2, 0, 1),
        "k12": np.stack([a["peer_k1"][0].T, a["peer_k2"][0].T], axis=1),
        "w_dt": w2[:, 4096:4112].reshape(NK, P, SSM_H).transpose(1, 0, 2),
        "row_ln": np.concatenate([a["sgu_ln_g"], a["sgu_ln_b"]]),
        "row_post": np.stack([a["final_g"], a["ffn1_post_g_2"][0], a["mix_post_g_2"][0], a["ffn2_post_g_2"][0]]),
        "row_small": np.concatenate([a["dt_bias_2"], a["a_log_2"], a["d_skip_2"]]),
        "row_lam": np.concatenate([a[f"lambda_{n}_2"] for n in ("q1", "k1", "q2", "k2")]),
    }
    arrays = {f"in_{n}": np.ascontiguousarray(v) for n, v in arrays.items()}
    nc = bacc.Bacc("TRN2", target_bir_lowering=False, num_devices=1)
    args = [nc.dram_tensor(n, v.shape, mybir.dt.from_np(v.dtype), kind="ExternalInput").ap()
            for n, v in arrays.items()]
    out = nc.dram_tensor("out", (1, T, D), mybir.dt.float32, kind="ExternalOutput").ap()
    program(nc, *args, out)
    r = run(nc, [arrays], core_ids=[0])
    return r.results[0]["out"]
```
